# Optimizing a Trainium2 kernel written in Bass

```python
import jax, jax.numpy as jnp
from jax import lax
import numpy as np

D_MODEL = 1024
BATCH = 1
SEQ = 256
DEPTH = 2

CHUNK = 64
Q_BLOCK = 128
N_MIXERS = 3
EPS = 1e-6

RET_HEADS = 4
RET_DK = D_MODEL
RET_DV = 2 * D_MODEL
RET_HK = RET_DK // RET_HEADS
RET_HV = RET_DV // RET_HEADS
RET_IN = 2 * RET_DK + 2 * RET_DV
ROPE_BASE = 10000.0

FOX_HEADS = 16
FOX_HD = 64
FOX_W = FOX_HEADS * FOX_HD
FOX_IN = 4 * FOX_W + FOX_HEADS
FOX_FORGET_BIAS = 2.0

GLA_HEADS = 4
GLA_DK = D_MODEL // 2
GLA_DV = D_MODEL
GLA_HK = GLA_DK // GLA_HEADS
GLA_HV = GLA_DV // GLA_HEADS
GLA_RANK = 16
GLA_TAU = 16.0
GLA_IN = 2 * GLA_DK + 2 * GLA_DV + GLA_RANK

MAX_POS_OFFSET = 100000


def _rms_norm(x, gain=None):
    xf = x.astype(jnp.float32)
    y = xf * lax.rsqrt(jnp.mean(xf * xf, axis=-1, keepdims=True) + EPS)
    if gain is not None:
        y = y * gain.astype(jnp.float32)
    return y.astype(x.dtype)

def _layer_norm(x):
    xf = x.astype(jnp.float32)
    mu = jnp.mean(xf, axis=-1, keepdims=True)
    var = jnp.mean(jnp.square(xf - mu), axis=-1, keepdims=True)
    return ((xf - mu) * lax.rsqrt(var + EPS)).astype(x.dtype)

def _rope(x, positions):
    half = x.shape[-1] // 2
    inv = ROPE_BASE ** (-jnp.arange(half, dtype=jnp.float32) / half)
    ang = positions.astype(jnp.float32)[..., None, None] * inv
    cos, sin = jnp.cos(ang), jnp.sin(ang)
    x1, x2 = x[..., :half], x[..., half:]
    return jnp.concatenate([x1 * cos - x2 * sin, x1 * sin + x2 * cos], axis=-1)

def _to_chunks(t):
    b, s, h, d = t.shape
    return t.reshape(b, s // CHUNK, CHUNK, h, d).transpose(0, 3, 1, 2, 4)

def _from_chunks(t):
    b, h, n, c, d = t.shape
    return t.transpose(0, 2, 3, 1, 4).reshape(b, n * c, h, d)

def _chunk_state_scan(q_in, k_in, v, state_decay):
    b, h, _, _, dk = q_in.shape
    dv = v.shape[-1]

    def step(state, inp):
        qi, ki, vi, di = inp
        out = jnp.einsum('bhcd,bhde->bhce', qi, state)
        state = di[..., None] * state + jnp.einsum('bhcd,bhce->bhde', ki, vi)
        return state, out

    xs = (jnp.moveaxis(q_in, 2, 0), jnp.moveaxis(k_in, 2, 0), jnp.moveaxis(v, 2, 0),
          jnp.moveaxis(state_decay, 2, 0))
    init = jnp.zeros((b, h, dk, dv), q_in.dtype)
    _, outs = lax.scan(step, init, xs)
    return jnp.moveaxis(outs, 0, 2)

def _retention(h, positions, w_in, w_out):
    b, s, _ = h.shape
    n = s // CHUNK
    q, k, v, g = jnp.split(h @ w_in, [RET_DK, 2 * RET_DK, 2 * RET_DK + RET_DV], axis=-1)
    q = _rope(q.astype(jnp.float32).reshape(b, s, RET_HEADS, RET_HK), positions) * (RET_HK ** -0.5)
    k = _rope(k.astype(jnp.float32).reshape(b, s, RET_HEADS, RET_HK), positions)
    qc, kc = _to_chunks(q), _to_chunks(k)
    vc = _to_chunks(v.astype(jnp.float32).reshape(b, s, RET_HEADS, RET_HV))
    log_gamma = jnp.log1p(-jnp.exp2(-5.0 - jnp.arange(RET_HEADS, dtype=jnp.float32)))
    pos = jnp.arange(CHUNK, dtype=jnp.float32)
    dist = jnp.abs(pos[:, None] - pos[None, :])
    intra_decay = jnp.exp(log_gamma[:, None, None] * dist)
    scores = jnp.einsum('bhncd,bhnmd->bhncm', qc, kc) * intra_decay[:, None]
    o = jnp.einsum('bhncm,bhnme->bhnce', scores, vc)
    q_in = qc * jnp.exp(log_gamma[:, None] * (pos + 1.0))[:, None, :, None]
    k_in = kc * jnp.exp(log_gamma[:, None] * (CHUNK - 1.0 - pos))[:, None, :, None]
    state_decay = jnp.broadcast_to(jnp.exp(log_gamma * CHUNK)[None, :, None, None], (b, RET_HEADS, n, RET_HK))
    o = o + _chunk_state_scan(q_in, k_in, vc, state_decay)
    o = _layer_norm(_from_chunks(o)).reshape(b, s, RET_DV)
    return (o.astype(h.dtype) * jax.nn.silu(g)) @ w_out

def _forgetting_attention(h, w_in, b_f, q_gain, k_gain, w_out):
    b, s, _ = h.shape
    q, k, v, g, f = jnp.split(h @ w_in, [FOX_W, 2 * FOX_W, 3 * FOX_W, 4 * FOX_W], axis=-1)
    q = _rms_norm(q.astype(jnp.float32).reshape(b, s, FOX_HEADS, FOX_HD), q_gain).transpose(0, 2, 1, 3) * (FOX_HD ** -0.5)
    k = _rms_norm(k.astype(jnp.float32).reshape(b, s, FOX_HEADS, FOX_HD), k_gain).transpose(0, 2, 1, 3)
    v = v.astype(jnp.float32).reshape(b, s, FOX_HEADS, FOX_HD).transpose(0, 2, 1, 3)
    log_f = jax.nn.log_sigmoid(f.astype(jnp.float32) + b_f.astype(jnp.float32))
    cum = jnp.cumsum(log_f, axis=1).transpose(0, 2, 1)
    outs = []
    for qs in range(0, s, Q_BLOCK):
        qe = qs + Q_BLOCK
        logits = (jnp.einsum('bhqd,bhkd->bhqk', q[:, :, qs:qe], k[:, :, :qe])
                  + cum[:, :, qs:qe, None] - cum[:, :, None, :qe])
        causal = jnp.arange(qs, qe)[:, None] >= jnp.arange(qe)[None, :]
        p = jax.nn.softmax(jnp.where(causal, logits, -jnp.inf), axis=-1)
        outs.append(jnp.einsum('bhqk,bhkd->bhqd', p, v[:, :, :qe]))
    o = jnp.concatenate(outs, axis=2).transpose(0, 2, 1, 3).reshape(b, s, FOX_W)
    return (o.astype(h.dtype) * jax.nn.silu(g)) @ w_out

def _gated_linear_attention(h, w_in, w_gate2, b_gate, w_out):
    b, s, _ = h.shape
    q, k, v, g, r = jnp.split(h @ w_in, [GLA_DK, 2 * GLA_DK, 2 * GLA_DK + GLA_DV, 2 * GLA_DK + 2 * GLA_DV], axis=-1)
    log_a = jax.nn.log_sigmoid((r @ w_gate2 + b_gate).astype(jnp.float32)) / GLA_TAU
    qc = _to_chunks(q.astype(jnp.float32).reshape(b, s, GLA_HEADS, GLA_HK)) * (GLA_HK ** -0.5)
    kc = _to_chunks(k.astype(jnp.float32).reshape(b, s, GLA_HEADS, GLA_HK))
    vc = _to_chunks(v.astype(jnp.float32).reshape(b, s, GLA_HEADS, GLA_HV))
    cb = jnp.cumsum(_to_chunks(log_a.reshape(b, s, GLA_HEADS, GLA_HK)), axis=3)
    cb_last = cb[:, :, :, -1:, :]
    eb, enb = jnp.exp(cb), jnp.exp(-cb)
    a_causal = jnp.einsum('bhncd,bhnmd->bhncm', qc * eb, kc * enb)
    a_anti = jnp.einsum('bhncd,bhnmd->bhncm', qc * enb, kc * eb)
    idx = jnp.arange(CHUNK)
    attn = jnp.where(idx[:, None] >= idx[None, :], a_causal, a_anti)
    o = jnp.einsum('bhncm,bhnme->bhnce', attn, vc)
    o = o + _chunk_state_scan(qc * eb, kc * jnp.exp(cb_last - cb), vc, jnp.exp(cb_last[:, :, :, 0, :]))
    o = _rms_norm(_from_chunks(o)).reshape(b, s, GLA_DV)
    return (o.astype(h.dtype) * jax.nn.silu(g)) @ w_out

def first_inputs(seed: int = 0) -> dict:
    key = jax.random.key(seed)
    ks = jax.random.split(key, 20)
    f32 = jnp.float32
    n_a = len(range(0, DEPTH, N_MIXERS))
    n_b = len(range(1, DEPTH, N_MIXERS))
    n_c = len(range(2, DEPTH, N_MIXERS))

    def w(k, shape, fan_in):
        return jax.random.normal(k, shape, f32) * (fan_in ** -0.5)

    x = jax.random.normal(ks[0], (BATCH, SEQ, D_MODEL), f32)
    c = jax.random.normal(ks[1], (BATCH, D_MODEL), f32)
    offs = jax.random.randint(ks[2], (BATCH, 1), 0, MAX_POS_OFFSET, dtype=jnp.int32)
    positions = (offs + jnp.arange(SEQ, dtype=jnp.int32)[None, :]).astype(jnp.int32)
    return {
        "x": x,
        "c": c,
        "positions": positions,
        "mod_w": w(ks[3], (DEPTH, D_MODEL, 3 * D_MODEL), D_MODEL),
        "mod_b": 0.01 * jax.random.normal(ks[4], (DEPTH, 3 * D_MODEL), f32),
        "norm_g": 1.0 + 0.01 * jax.random.normal(ks[5], (DEPTH, D_MODEL), f32),
        "ret_w_in": w(ks[6], (n_a, D_MODEL, RET_IN), D_MODEL),
        "ret_w_out": w(ks[7], (n_a, RET_DV, D_MODEL), RET_DV),
        "fox_w_in": w(ks[8], (n_b, D_MODEL, FOX_IN), D_MODEL),
        "fox_b_f": FOX_FORGET_BIAS + 0.1 * jax.random.normal(ks[9], (n_b, FOX_HEADS), f32),
        "fox_q_gain": 1.0 + 0.01 * jax.random.normal(ks[10], (n_b, FOX_HD), f32),
        "fox_k_gain": 1.0 + 0.01 * jax.random.normal(ks[11], (n_b, FOX_HD), f32),
        "fox_w_out": w(ks[12], (n_b, FOX_W, D_MODEL), FOX_W),
        "gla_w_in": w(ks[13], (n_c, D_MODEL, GLA_IN), D_MODEL),
        "gla_w_gate2": w(ks[14], (n_c, GLA_RANK, GLA_DK), GLA_RANK),
        "gla_b_gate": 0.01 * jax.random.normal(ks[15], (n_c, GLA_DK), f32),
        "gla_w_out": w(ks[16], (n_c, GLA_DV, D_MODEL), GLA_DV),
        "final_g": 1.0 + 0.01 * jax.random.normal(ks[17], (D_MODEL,), f32),
    }

def first_block(x, c, positions, mod_w, mod_b, norm_g, ret_w_in, ret_w_out, fox_w_in, fox_b_f,
              fox_q_gain, fox_k_gain, fox_w_out, gla_w_in, gla_w_gate2, gla_b_gate, gla_w_out, final_g):
    c_act = jax.nn.silu(c)
    for i in range(DEPTH):
        shift, scale, gate = jnp.split(c_act @ mod_w[i] + mod_b[i], 3, axis=-1)
        h = _rms_norm(x, norm_g[i]) * (1.0 + scale[:, None, :]) + shift[:, None, :]
        j = i // N_MIXERS
        kind = i % N_MIXERS
        if kind == 0:
            y = _retention(h, positions, ret_w_in[j], ret_w_out[j])
        elif kind == 1:
            y = _forgetting_attention(h, fox_w_in[j], fox_b_f[j], fox_q_gain[j], fox_k_gain[j], fox_w_out[j])
        else:
            y = _gated_linear_attention(h, gla_w_in[j], gla_w_gate2[j], gla_b_gate[j], gla_w_out[j])
        x = x + gate[:, None, :] * y
    return _rms_norm(x, final_g)


DEEPNORM_ALPHA = (2.0 * DEPTH) ** 0.25
DEEPNORM_BETA = (8.0 * DEPTH) ** -0.25
LN_EPS = 1e-5
NEG_INF = -1e30

CONV_KERNEL = 31
SHORT_KERNEL = 3
NSA_HEADS = 16
NSA_KV_HEADS = 4
NSA_GROUP = NSA_HEADS // NSA_KV_HEADS
HEAD_DIM = D_MODEL // NSA_HEADS
CMP_BLOCK = 32
CMP_STRIDE = 16
SLC_BLOCK = 64
SLC_TOP_N = 16
SLC_FORCED_LOCAL = 2
FORCE_BONUS = 1e4
WINDOW = 512
PHI_HIDDEN = 2 * HEAD_DIM
NSA_QBLK = 64
NSA_IN_COLS = NSA_HEADS * HEAD_DIM + 6 * NSA_KV_HEADS * HEAD_DIM + 3 * NSA_HEADS
D_FF = 2816
N_EXPERTS = 8
TOP_K = 2
D_FF_EXPERT = 3584


def _count(period, phase):
    return len(range(phase, DEPTH, period))

def _layer_norm_2(x, g, b):
    xf = x.astype(jnp.float32)
    mu = jnp.mean(xf, -1, keepdims=True)
    var = jnp.mean(jnp.square(xf - mu), -1, keepdims=True)
    y = (xf - mu) * lax.rsqrt(var + LN_EPS)
    return (y * g.astype(jnp.float32) + b.astype(jnp.float32)).astype(x.dtype)

def _causal_depthwise_conv(x, w):
    k = w.shape[0]
    return lax.conv_general_dilated(
        x, w[:, None, :], window_strides=(1,), padding=[(k - 1, 0)],
        dimension_numbers=("NWC", "WIO", "NWC"), feature_group_count=x.shape[-1])

def _masked_softmax(s, mask):
    s = jnp.where(mask, s.astype(jnp.float32), NEG_INF)
    m = jnp.max(s, -1, keepdims=True)
    e = jnp.exp(s - m) * mask
    return e / jnp.maximum(jnp.sum(e, -1, keepdims=True), 1e-30)

def conformer_conv(x, w_in, w_dw, b_dw, ln_g, ln_b, w_out):
    a, gate = jnp.split(x @ w_in, 2, axis=-1)
    u = a * jax.nn.sigmoid(gate)
    u = _causal_depthwise_conv(u, w_dw) + b_dw
    u = jax.nn.silu(_layer_norm_2(u, ln_g, ln_b))
    return u @ w_out

def short_gated_conv(x, w_in, w_conv, w_out):
    b_gate, c_gate, h = jnp.split(x @ w_in, 3, axis=-1)
    y = b_gate * _causal_depthwise_conv(c_gate * h, w_conv)
    return y @ w_out

def _compress(kv, pe, w1, w2):
    B, T, Hk, dh = kv.shape
    n_cmp = (T - CMP_BLOCK) // CMP_STRIDE + 1
    idx = jnp.arange(n_cmp)[:, None] * CMP_STRIDE + jnp.arange(CMP_BLOCK)[None, :]
    blocks = kv[:, idx] + pe[:, None, :]
    blocks = jnp.moveaxis(blocks, 3, 1).reshape(B, Hk, n_cmp, CMP_BLOCK * dh)
    return jax.nn.gelu(blocks @ w1) @ w2

def native_sparse_attention(x, w_in, pe_k, pe_v, wk1, wk2, wv1, wv2, w_out):
    B, T, _ = x.shape
    H, Hk, G, dh = NSA_HEADS, NSA_KV_HEADS, NSA_GROUP, HEAD_DIM
    qd, kd = H * dh, Hk * dh
    cuts = [qd, qd + kd, qd + 2 * kd, qd + 3 * kd, qd + 4 * kd, qd + 5 * kd, qd + 6 * kd]
    q, kc, vc, ks, vs, kw, vw, g = jnp.split(x @ w_in, cuts, axis=-1)
    q = q.reshape(B, T, Hk, G, dh).transpose(0, 2, 3, 1, 4) * (dh ** -0.5)
    kv_shape = (B, T, Hk, dh)
    kc, vc = kc.reshape(kv_shape), vc.reshape(kv_shape)
    ks = ks.reshape(kv_shape).transpose(0, 2, 1, 3)
    vs = vs.reshape(kv_shape).transpose(0, 2, 1, 3)
    kw = kw.reshape(kv_shape).transpose(0, 2, 1, 3)
    vw = vw.reshape(kv_shape).transpose(0, 2, 1, 3)
    t_pos = jnp.arange(T)

    k_cmp = _compress(kc, pe_k, wk1, wk2)
    v_cmp = _compress(vc, pe_v, wv1, wv2)
    n_cmp = k_cmp.shape[2]
    cmp_start = jnp.arange(n_cmp) * CMP_STRIDE
    mask_c = (cmp_start + CMP_BLOCK - 1)[None, :] <= t_pos[:, None]
    p_cmp = _masked_softmax(jnp.einsum("bhgtd,bhcd->bhgtc", q, k_cmp), mask_c)
    o_cmp = jnp.einsum("bhgtc,bhcd->bhgtd", p_cmp.astype(v_cmp.dtype), v_cmp)

    n_slc = T // SLC_BLOCK
    blk = jnp.arange(n_slc)
    slc_start = blk * SLC_BLOCK
    overlap = ((cmp_start[:, None] < (slc_start + SLC_BLOCK)[None, :]) &
               ((cmp_start + CMP_BLOCK)[:, None] > slc_start[None, :])).astype(jnp.float32)
    imp = jnp.einsum("bhgtc,cn->bhtn", p_cmp, overlap)
    valid = slc_start[None, :] <= t_pos[:, None]
    d_cur = (t_pos // SLC_BLOCK)[:, None] - blk[None, :]
    forced = (blk[None, :] == 0) | ((d_cur >= 0) & (d_cur < SLC_FORCED_LOCAL))
    score = jnp.where(forced, FORCE_BONUS, jnp.where(valid, imp, NEG_INF))
    top_n = min(SLC_TOP_N, n_slc)
    _, sel = lax.top_k(score, top_n)

    ks_blk = ks.reshape(B, Hk, n_slc, SLC_BLOCK, dh)
    vs_blk = vs.reshape(B, Hk, n_slc, SLC_BLOCK, dh)
    kw_pad = jnp.pad(kw, ((0, 0), (0, 0), (WINDOW, 0), (0, 0)))
    vw_pad = jnp.pad(vw, ((0, 0), (0, 0), (WINDOW, 0), (0, 0)))
    QB = NSA_QBLK
    nq = T // QB
    q_blocks = jnp.moveaxis(q.reshape(B, Hk, G, nq, QB, dh), 3, 0)
    sel_blocks = jnp.moveaxis(sel.reshape(B, Hk, nq, QB, top_n), 2, 0)
    bi = jnp.arange(B)[:, None, None, None]
    hi = jnp.arange(Hk)[None, :, None, None]

    def local_branches(args):
        qi, q_b, sel_b = args
        t_b = qi * QB + jnp.arange(QB)
        k_sel = ks_blk[bi, hi, sel_b]
        v_sel = vs_blk[bi, hi, sel_b].reshape(B, Hk, QB, top_n * SLC_BLOCK, dh)
        pos = sel_b[..., None] * SLC_BLOCK + jnp.arange(SLC_BLOCK)
        mask_s = (pos <= t_b[:, None, None]).reshape(B, Hk, 1, QB, top_n * SLC_BLOCK)
        s_sel = jnp.einsum("bhgqd,bhqnsd->bhgqns", q_b, k_sel).reshape(B, Hk, G, QB, top_n * SLC_BLOCK)
        p_sel = _masked_softmax(s_sel, mask_s)
        o_sel = jnp.einsum("bhgqk,bhqkd->bhgqd", p_sel.astype(v_sel.dtype), v_sel)
        k_win = lax.dynamic_slice_in_dim(kw_pad, qi * QB, WINDOW + QB, axis=2)
        v_win = lax.dynamic_slice_in_dim(vw_pad, qi * QB, WINDOW + QB, axis=2)
        kpos = qi * QB - WINDOW + jnp.arange(WINDOW + QB)
        diff = t_b[:, None] - kpos[None, :]
        mask_w = (diff >= 0) & (diff < WINDOW) & (kpos[None, :] >= 0)
        p_win = _masked_softmax(jnp.einsum("bhgqd,bhkd->bhgqk", q_b, k_win), mask_w)
        o_win = jnp.einsum("bhgqk,bhkd->bhgqd", p_win.astype(v_win.dtype), v_win)
        return o_sel, o_win

    o_sel, o_win = lax.map(local_branches, (jnp.arange(nq), q_blocks, sel_blocks))
    o_sel = jnp.moveaxis(o_sel, 0, 3).reshape(B, Hk, G, T, dh)
    o_win = jnp.moveaxis(o_win, 0, 3).reshape(B, Hk, G, T, dh)

    gates = jax.nn.sigmoid(g.reshape(B, T, Hk, G, 3).transpose(0, 2, 3, 1, 4))
    o = gates[..., 0:1] * o_cmp + gates[..., 1:2] * o_sel + gates[..., 2:3] * o_win
    o = o.transpose(0, 3, 1, 2, 4).reshape(B, T, H * dh)
    return o @ w_out

def swiglu(x, w_gate, w_up, w_down):
    return (jax.nn.silu(x @ w_gate) * (x @ w_up)) @ w_down

def moe_swiglu(x, w_router, w_gate, w_up, w_down):
    logits = (x @ w_router).astype(jnp.float32)
    top_val, top_idx = lax.top_k(logits, TOP_K)
    wts = jax.nn.softmax(top_val, axis=-1)
    gates = jnp.sum(jax.nn.one_hot(top_idx, N_EXPERTS, dtype=jnp.float32) * wts[..., None], axis=-2)
    out = jnp.zeros_like(x)
    for e in range(N_EXPERTS):
        h = jax.nn.silu(x @ w_gate[e]) * (x @ w_up[e])
        out = out + gates[..., e:e + 1].astype(x.dtype) * (h @ w_down[e])
    return out

def second_inputs(seed: int = 0) -> dict:
    key = jax.random.key(seed)
    ks = iter(jax.random.split(key, 40))
    f32 = jnp.float32
    D, dh = D_MODEL, HEAD_DIM
    nA, nB, nC = _count(N_MIXERS, 0), _count(N_MIXERS, 1), _count(N_MIXERS, 2)
    nDense, nMoE = _count(2, 0), _count(2, 1)

    def nrm(shape, scale):
        return jax.random.normal(next(ks), shape, f32) * scale

    def gain(shape):
        return 1.0 + nrm(shape, 0.02)

    beta = DEEPNORM_BETA
    return {
        "x": nrm((BATCH, SEQ, D), 1.0),
        "ln_mix_g": gain((DEPTH, D)),
        "ln_mix_b": nrm((DEPTH, D), 0.02),
        "ln_ffn_g": gain((DEPTH, D)),
        "ln_ffn_b": nrm((DEPTH, D), 0.02),
        "conf_w_in": nrm((nA, D, 2 * D), D ** -0.5),
        "conf_w_dw": nrm((nA, CONV_KERNEL, D), CONV_KERNEL ** -0.5),
        "conf_b_dw": nrm((nA, D), 0.02),
        "conf_ln_g": gain((nA, D)),
        "conf_ln_b": nrm((nA, D), 0.02),
        "conf_w_out": nrm((nA, D, D), beta * D ** -0.5),
        "sc_w_in": nrm((nB, D, 3 * D), D ** -0.5),
        "sc_w_conv": nrm((nB, SHORT_KERNEL, D), SHORT_KERNEL ** -0.5),
        "sc_w_out": nrm((nB, D, D), beta * D ** -0.5),
        "nsa_w_in": nrm((nC, D, NSA_IN_COLS), D ** -0.5),
        "nsa_pe_k": nrm((nC, CMP_BLOCK, dh), 0.1),
        "nsa_pe_v": nrm((nC, CMP_BLOCK, dh), 0.1),
        "nsa_wk1": nrm((nC, CMP_BLOCK * dh, PHI_HIDDEN), (CMP_BLOCK * dh) ** -0.5),
        "nsa_wk2": nrm((nC, PHI_HIDDEN, dh), PHI_HIDDEN ** -0.5),
        "nsa_wv1": nrm((nC, CMP_BLOCK * dh, PHI_HIDDEN), (CMP_BLOCK * dh) ** -0.5),
        "nsa_wv2": nrm((nC, PHI_HIDDEN, dh), PHI_HIDDEN ** -0.5),
        "nsa_w_out": nrm((nC, D, D), beta * D ** -0.5),
        "ffn_w_gate": nrm((nDense, D, D_FF), D ** -0.5),
        "ffn_w_up": nrm((nDense, D, D_FF), D ** -0.5),
        "ffn_w_down": nrm((nDense, D_FF, D), beta * D_FF ** -0.5),
        "moe_w_router": nrm((nMoE, D, N_EXPERTS), D ** -0.5),
        "moe_w_gate": nrm((nMoE, N_EXPERTS, D, D_FF_EXPERT), D ** -0.5),
        "moe_w_up": nrm((nMoE, N_EXPERTS, D, D_FF_EXPERT), D ** -0.5),
        "moe_w_down": nrm((nMoE, N_EXPERTS, D_FF_EXPERT, D), beta * D_FF_EXPERT ** -0.5),
    }

def second_block(x, ln_mix_g, ln_mix_b, ln_ffn_g, ln_ffn_b,
              conf_w_in, conf_w_dw, conf_b_dw, conf_ln_g, conf_ln_b, conf_w_out,
              sc_w_in, sc_w_conv, sc_w_out,
              nsa_w_in, nsa_pe_k, nsa_pe_v, nsa_wk1, nsa_wk2, nsa_wv1, nsa_wv2, nsa_w_out,
              ffn_w_gate, ffn_w_up, ffn_w_down,
              moe_w_router, moe_w_gate, moe_w_up, moe_w_down):
    for i in range(DEPTH):
        kind, j = i % N_MIXERS, i // N_MIXERS
        if kind == 0:
            mix = conformer_conv(x, conf_w_in[j], conf_w_dw[j], conf_b_dw[j],
                                 conf_ln_g[j], conf_ln_b[j], conf_w_out[j])
        elif kind == 1:
            mix = short_gated_conv(x, sc_w_in[j], sc_w_conv[j], sc_w_out[j])
        else:
            mix = native_sparse_attention(x, nsa_w_in[j], nsa_pe_k[j], nsa_pe_v[j],
                                          nsa_wk1[j], nsa_wk2[j], nsa_wv1[j], nsa_wv2[j],
                                          nsa_w_out[j])
        x = _layer_norm_2(DEEPNORM_ALPHA * x + mix, ln_mix_g[i], ln_mix_b[i])
        f = i // 2
        if i % 2 == 0:
            ffn = swiglu(x, ffn_w_gate[f], ffn_w_up[f], ffn_w_down[f])
        else:
            ffn = moe_swiglu(x, moe_w_router[f], moe_w_gate[f], moe_w_up[f], moe_w_down[f])
        x = _layer_norm_2(DEEPNORM_ALPHA * x + ffn, ln_ffn_g[i], ln_ffn_b[i])
    return x


def setup_inputs(seed=0):
    out = dict(first_inputs(seed))
    for name, value in second_inputs(seed + 1).items():
        if name != "x":
            out[name + "_2"] = value
    return out


def reference(
    x, c, positions, mod_w, mod_b, norm_g, ret_w_in, ret_w_out, fox_w_in, fox_b_f, fox_q_gain,
    fox_k_gain, fox_w_out, gla_w_in, gla_w_gate2, gla_b_gate, gla_w_out, final_g, ln_mix_g_2,
    ln_mix_b_2, ln_ffn_g_2, ln_ffn_b_2, conf_w_in_2, conf_w_dw_2, conf_b_dw_2, conf_ln_g_2,
    conf_ln_b_2, conf_w_out_2, sc_w_in_2, sc_w_conv_2, sc_w_out_2, nsa_w_in_2, nsa_pe_k_2,
    nsa_pe_v_2, nsa_wk1_2, nsa_wk2_2, nsa_wv1_2, nsa_wv2_2, nsa_w_out_2, ffn_w_gate_2,
    ffn_w_up_2, ffn_w_down_2, moe_w_router_2, moe_w_gate_2, moe_w_up_2, moe_w_down_2,
):
    x = first_block(
        x, c, positions, mod_w, mod_b, norm_g, ret_w_in, ret_w_out, fox_w_in, fox_b_f,
        fox_q_gain, fox_k_gain, fox_w_out, gla_w_in, gla_w_gate2, gla_b_gate, gla_w_out,
        final_g,
    )
    return second_block(
        x, ln_mix_g_2, ln_mix_b_2, ln_ffn_g_2, ln_ffn_b_2, conf_w_in_2, conf_w_dw_2,
        conf_b_dw_2, conf_ln_g_2, conf_ln_b_2, conf_w_out_2, sc_w_in_2, sc_w_conv_2, sc_w_out_2,
        nsa_w_in_2, nsa_pe_k_2, nsa_pe_v_2, nsa_wk1_2, nsa_wk2_2, nsa_wv1_2, nsa_wv2_2,
        nsa_w_out_2, ffn_w_gate_2, ffn_w_up_2, ffn_w_down_2, moe_w_router_2, moe_w_gate_2,
        moe_w_up_2, moe_w_down_2,
    )


_drawn_inputs = setup_inputs


def setup_inputs(seed=0):
    import zlib

    import numpy as np

    out = dict(_drawn_inputs(seed))
    spreads = {}
    factors = {'norm_g': 3.479,
     'fox_b_f': 3.172,
     'fox_q_gain': 8.0,
     'fox_k_gain': 8.0,
     'final_g': 48.484,
     'conf_b_dw_2': 36.952,
     'conf_ln_g_2': 93.876,
     'conf_ln_b_2': 109.505}
    for name, (base, spread) in spreads.items():
        noise = np.random.default_rng([zlib.crc32(name.encode()), seed]).standard_normal(out[name].shape)
        drawn = base * np.exp(spread * noise) if base else spread * noise
        out[name] = __import__('jax').numpy.asarray(drawn.astype(out[name].dtype))
    for name, factor in factors.items():
        out[name] = (out[name] * factor).astype(out[name].dtype)
    return out
```

```python
from contextlib import ExitStack

import numpy as np

import concourse.bass as bass
from concourse import mybir

F32 = mybir.dt.float32
I32 = mybir.dt.int32
ACT = mybir.ActivationFunctionType
ALU = mybir.AluOpType
AX = mybir.AxisListType

P = 128
D = 1024
KB = D // P
T = 256
NT = T // P
CHUNK = 64
RH, RHK, RHV = 4, 256, 512
RV = RH * RHV
FH, FD = 16, 64
DFF = 2816
FB = DFF // P
NE = 8
EF = 3584
EB = EF // P
TAPS = 31
STAPS = 3
RMS_EPS = 1e-6
LN_EPS = 1e-5
ALPHA = float((2.0 * 2) ** 0.25)
BIG = 1e30
WIDTHS = (128, 256)

RING = 7
COLS = 512
ROWS = 4
PAIRS = EF // COLS
DOWNS = EB // ROWS
PER_EXPERT = 2 * PAIRS + DOWNS
assert PER_EXPERT % RING == 0

V_C, V_NORM, V_CB, V_CG, V_CBETA, V_SC = 0, 1, 3, 4, 5, 6
V_DW = V_SC + STAPS
NVEC = V_DW + TAPS

C_IDENT, C_TRI, C_STRICT, C_ONES = 0, 128, 256, 384
C_MASK = 512
C_IOTA = C_MASK + 384
C_DESC = C_IOTA + 256
C_INV = C_DESC + 8
C_END = C_INV + 1


def shape_constants():
    i = np.arange(P)
    c = np.zeros((P, C_END), np.float32)
    c[:, C_IDENT:C_IDENT + P] = np.eye(P)
    c[:, C_TRI:C_TRI + P] = i[:, None] <= i[None, :]
    c[:, C_STRICT:C_STRICT + P] = i[:, None] < i[None, :]
    c[:, C_ONES:C_ONES + P] = 1.0
    causal = np.where(i[:, None] >= i[None, :], 0.0, -BIG)
    c[:, C_MASK:C_MASK + P] = causal
    c[:, C_MASK + 2 * P:C_MASK + 3 * P] = causal
    c[:, C_IOTA:C_IOTA + 256] = np.arange(256)[None, :]
    c[:, C_DESC:C_DESC + 8] = 8 - np.arange(8)[None, :]
    half = RHK // 2
    exponent = -np.arange(half, dtype=np.float32) / np.float32(half)
    c[:, C_INV] = (10000.0 ** exponent.astype(np.float64)).astype(np.float32)
    lg = np.log1p(-np.exp2(-5.0 - np.arange(RH)))
    m, t = i[:, None], i[None, :]
    seen = (m // CHUNK == t // CHUNK) | (m < t)
    d = np.zeros((P, RH, 2, P), np.float32)
    for h in range(RH):
        d[:, h, 0] = np.where(seen, np.exp(lg[h] * abs(t - m)), 0.0) * RHK ** -0.5
        d[:, h, 1] = np.exp(lg[h] * (P + t - m)) * RHK ** -0.5
    return c, d.reshape(P, RH * 2 * P)


def weight_plan():
    plan = [("ret_q", 0), ("ret_q", 1), ("ret_k", 0), ("ret_k", 1)]
    plan += [("ret_v", i) for i in range(4)] + [("ret_g", i) for i in range(4)]
    plan += [("ret_out", i) for i in range(4)]
    plan += [(n, i) for n in ("fox_q", "fox_k", "fox_v", "fox_g") for i in range(2)]
    plan += [("fox_out", i) for i in range(2)]
    plan += [(n, i) for i in range(2) for n in ("conf_a", "conf_g")]
    plan += [("conf_out", i) for i in range(2)]
    plan += [(n, i) for i in range(6) for n in ("ffn_gate", "ffn_up")]
    plan += [("ffn_down", i) for i in range(6)]
    plan += [(n, i) for i in range(2) for n in ("sc_c", "sc_h", "sc_b")]
    plan += [("sc_out", i) for i in range(2)]
    return plan


PLAN = weight_plan()
CHUNK_AT = {key: n for n, key in enumerate(PLAN)}
PRE = len(PLAN)
PRE_RING = RING - 1
SHIFT = (-PRE) % PRE_RING


def pre_slot(n):
    return (n + SHIFT) % PRE_RING


def pre_fill(n):
    return sum(pre_slot(m) == pre_slot(n) for m in range(n + 1))


PRE_FILLS = [sum(pre_slot(m) == s for m in range(PRE)) for s in range(RING)]


def bank_plan():
    g = [("vecs", 0, "D"), ("mod_cols", 0, "D")] + [("x0T", i, "A") for i in range(4)]
    g += [("mod_gate", i, "D") for i in range(2)]
    g += [("ret_q", i, "D") for i in range(RH)] + [("ret_k", i, "D") for i in range(RH)]
    g += [("ret_v", i, "A") for i in range(8)] + [("ret_g", i, "A") for i in range(8)]
    g += [("ret_s", 0, "D")]
    for h in range(RH):
        if h + 1 < RH:
            g += [("ret_s", h + 1, "D")]
        g += [("ret_o", 2 * h, "D"), ("ret_o", 2 * h + 1, "D")]
    g += [("ret_uT", i, "A") for i in range(8)]
    g += [("ret_y", i, "D") for i in range(4)]
    g += [("mod_cols", 1, "D")] + [("mod_gate", 2 + i, "D") for i in range(2)]
    g += [("x1T", i, "A") for i in range(4)]
    g += [("fox_f", 0, "D")]
    g += [("fox_q", i, "D") for i in range(4)] + [("fox_k", i, "D") for i in range(4)]
    g += [("fox_cum", 0, "D")]
    g += [("fox_v", i, "A") for i in range(4)] + [("fox_g", i, "A") for i in range(4)]
    g += [("fox_qT", i, "D") for i in range(4)] + [("fox_kT", i, "D") for i in range(4)]
    for i in range(FH + 2):
        if i < FH:
            g += [("fox_s", i, "D")]
        if 1 <= i <= FH:
            g += [("fox_pT", i - 1, "A")]
        if i >= 3 and i % 2 == 1:
            g += [("fox_o", (i - 3) // 2, "D")]
    g += [("fox_y", i, "D") for i in range(4)]
    g += [("x2T", i, "A") for i in range(4)]
    g += [("conf", i, "D") for i in range(KB)]
    g += [("conf_cT", i, "D") for i in range(4)] + [("conf_nT", i, "A") for i in range(4)]
    g += [("conf_y", i, "D") for i in range(4)]
    g += [("x3T", i, "A") for i in range(4)]
    g += [("ffn", i, "D") for i in range(FB)]
    g += [("ffn_y", i, "D") for i in range(4)]
    g += [("x4T", i, "A") for i in range(4)]
    for i in range(KB):
        g += [("sc_ch", i, "D"), ("sc_b", i, "D")]
    g += [("sc_y", i, "D") for i in range(4)]
    g += [("x5T", i, "A") for i in range(4)]
    g += [("route", 0, "D"), ("rank", 0, "D")]
    return g


COL_BANKS = {**{n: (n, 2) for n in ("ret_q", "ret_k", "ret_v", "ret_g", "fox_q", "fox_k", "fox_v", "fox_g")},
             "conf_a": ("conf", 4), "conf_g": ("conf", 4), "ffn_gate": ("ffn", 4), "ffn_up": ("ffn", 4),
             "sc_c": ("sc_b", 4), "sc_h": ("sc_b", 4), "sc_b": ("sc_b", 4)}
OUT_BANKS = {"ret_out": "ret_y", "fox_out": "fox_y", "conf_out": "conf_y", "ffn_down": "ffn_y", "sc_out": "sc_y"}
PRE_ROWS = sum(name in OUT_BANKS and (name, i + 1) in CHUNK_AT for name, i in PLAN)

BANKS = bank_plan()
BANK_AT = {(name, i): n for n, (name, i, _) in enumerate(BANKS)}
NBANK = 8


def emptied_by(n):
    who = BANKS[n][2]
    return who, sum(b[2] == who for b in BANKS[:n + 1])


ALL_EMPTIED = {who: sum(b[2] == who for b in BANKS) for who in "AD"}

ROOTS = (["rms0"] + [f"ret{h}" for h in range(RH)] + ["rms1"] + [f"fq{i}" for i in range(4)]
         + [f"fk{i}" for i in range(4)] + ["final", "conf", "mix0", "ffn0", "mix1", "out"])
ROOT_WIDTH = {**{f"fq{i}": 8 for i in range(4)}, **{f"fk{i}": 8 for i in range(4)}}


def build(nc, t, out):
    ctx = ExitStack()
    with ctx:
        def sb(name, shape, dt=F32):
            return ctx.enter_context(nc.sbuf_tensor(name, shape, dt))

        def sem(name):
            return ctx.enter_context(nc.semaphore(name))

        ring = sb("ring", [P, RING, ROWS * D])
        x = sb("x", [P, NT, D])
        xT = sb("xT", [P, KB, T])
        R = sb("R", [P, 15360])
        dec_p = sb("dec_p", [P, 2, 3 * P])
        cos = sb("cos", [P, T])
        sin = sb("sin", [P, T])
        const = sb("const", [P, C_END])
        vec = sb("vec", [P, KB, NVEC])
        c_act = sb("c_act", [P, KB])
        in_scale = sb("in_scale", [P, KB])
        in_shift = sb("in_shift", [P, KB])
        wf = sb("wf", [P, KB, FH])
        w_router = sb("w_router", [P, KB, NE])
        gains = sb("gains", [P, 2])
        qk_gain = sb("qk_gain", [P, 1])
        bf_row = sb("bf_row", [P, FH])
        logf = sb("logf", [P, NT, FH])
        logf_t = sb("logf_t", [P, 2, NT * FH])
        cum = sb("cum", [P, NT, FH])
        ncumT = sb("ncumT", [FH, T])
        mx = sb("mx", [P, 2, 2])
        rsum = sb("rsum", [P, 2, 2])
        rinv = sb("rinv", [P, 2, 2])
        sumsq = sb("sumsq", [P, NT])
        head_sq = sb("head_sq", [P, 2, 8])
        root_in = sb("root_in", [P, 2, 8])
        root_out = sb("root_out", [P, 2, 8])
        neg_half = sb("neg_half", [P, 8])
        stats = sb("stats", [P, NT, 2, 6])
        meanvar = sb("meanvar", [P, NT, 2])
        rt = sb("rt", [P, 14, NT, NE])
        slot_of = sb("slot_of", [P, NE, NT])
        gate_of = sb("gate_of", [P, NE, NT])
        counts = sb("counts", [1, NE], I32)

        psum = ctx.enter_context(nc.psum_tensor("psum", [P, NBANK, 512], F32))

        def region(at, *shape):
            n = int(np.prod(shape))
            v = R[:, at:at + n]
            if len(shape) == 2:
                return v.rearrange("p (a b) -> p a b", a=shape[0])
            if len(shape) == 3:
                return v.rearrange("p (a b c) -> p a b c", a=shape[0], b=shape[1])
            return v

        ident = const[:, C_IDENT:C_IDENT + P]
        tri = const[:, C_TRI:C_TRI + P]
        strict = const[:, C_STRICT:C_STRICT + P]
        ones = const[:, C_ONES:C_ONES + P]
        desc = const[:, C_DESC:C_DESC + NE]

        mod_w = ring[:, RING - 1, 0:3072].rearrange("p (b n) -> p b n", b=2)
        decay = ring[:, RING - 1, 3072:4096].rearrange("p (h n) -> p h n", h=RH)
        xn = region(0, NT, D)
        vec_rows = R[0:NVEC, 8192:8192 + D]
        rq, rk = region(0, KB, T), region(2048, KB, T)
        rv, rg = region(4096, NT, RV), region(8192, NT, RV)
        ruT = region(4096, RV // P, T)
        acc = region(12288, 3 * D)
        gate = sb("gate", [P, D])
        rot = R[:, 8192:9216].rearrange("p (a b c) -> p a b c", a=2, b=2)
        ang = region(4096, 6, T)
        pos_i = sb("pos_i", [P, T], I32)
        half_rows = region(0, 2, 512)
        fq_tok, fk_tok = region(2048, NT, D), region(4096, NT, D)
        fv, fgT = region(6144, NT, D), region(8192, KB, T)
        fqT, fkT = region(10240, KB, T), region(0, KB, T)
        fuT = region(2048, KB, T)
        fsq = region(12288, 2, 512)
        logits = region(12288, 2, 384)
        prob = region(13056, 2, 384)
        probT = region(13824, 4, 384)
        u_pad = region(0, KB, TAPS - 1 + T)
        conv = region(2304, KB, T)
        conf_n = region(4352, NT, D)
        conf_uT = region(6400, KB, T)
        half_gate = region(8448, 2, T)
        z = region(8960, NT, D)
        rows_gb = region(12288, 2, D)
        final_row = region(14336, D)
        out_g = gate[:, :]
        out_b = xT[:, 0:4, :].rearrange("p k n -> p (k n)")
        ffn_h = region(0, FB, T)
        ffn_s = region(5632, 2, T)
        ch = region(0, 2, STAPS - 1 + T)
        sc_c = region(600, 2, T)
        sc_t = region(1200, T)
        sc_uT = region(2048, KB, T)
        e_acc = region(0, NT, D)
        e_x = region(2048, KB, T)
        e_h = region(4096, EB, 256)
        e_y = region(11264, 2, D)
        e_sel = region(13312, NT, 256)
        e_selT = region(13824, 2, 256)
        e_s = region(14336, 2, 256)

        slot_filled = [sem(f"slot_filled{s}") for s in range(RING)]
        weights_used = sem("weights_used")
        mod_filled = [sem("mod_filled0"), sem("mod_filled1")]
        mod_used = sem("mod_used")
        acc_seeded = sem("acc_seeded")
        x_loaded = sem("x_loaded")
        vec_loaded = sem("vec_loaded")
        const_loaded = sem("const_loaded")
        small_loaded = sem("small_loaded")
        bf_loaded = sem("bf_loaded")
        pos_loaded = sem("pos_loaded")
        rows_loaded = sem("rows_loaded")
        final_loaded = sem("final_loaded")
        bank_filled = sem("bank_filled")
        emptied = {"A": sem("bank_emptied_by_scalar"), "D": sem("bank_emptied_by_vector")}
        c_ready = sem("c_ready")
        acc_clear = sem("acc_clear")
        sumsq_ready = sem("sumsq_ready")
        root_asked = sem("root_asked")
        root_ready = sem("root_ready")
        xn_ready = sem("xn_ready")
        ang_ready = sem("ang_ready")
        trig_ready = sem("trig_ready")
        ret_u_ready = sem("ret_u_ready")
        x_ready = sem("x_ready")
        fox_sq = sem("fox_sq")
        fox_sq_used = sem("fox_sq_used")
        logf_in = sem("logf_in")
        logf_mid = sem("logf_mid")
        logf_ready = sem("logf_ready")
        logits_ready = sem("logits_ready")
        probs_exp = sem("probs_exp")
        probs_ready = sem("probs_ready")
        half_ready = sem("half_ready")
        conv_ready = sem("conv_ready")
        silu_ready = sem("silu_ready")
        c_copied = sem("c_copied")
        lg_ready = sem("lg_ready")
        lg_exp = sem("lg_exp")
        mask_ready = sem("mask_ready")
        sel_ready = sem("sel_ready")
        wide_filled = sem("wide_filled")
        wide_emptied = sem("wide_emptied")
        gu_filled = sem("gu_filled")
        gu_emptied = sem("gu_emptied")
        e_silu = sem("e_silu")
        out_written = sem("out_written")
        vector_step = sem("vector_step")
        scalar_step = sem("scalar_step")
        gpsimd_step = sem("gpsimd_step")

        def cols(w, at, n=COLS):
            return w.rearrange("(k p) n -> p k n", p=P)[:, :, at:at + n]

        def rows(w, at, n=ROWS):
            return w.rearrange("(r p) n -> p r n", p=P)[:, at:at + n, :]

        w_ret, w_fox = t["ret_w_in"][0], t["fox_w_in"][0]
        w_conf, w_sc = t["conf_w_in_2"][0], t["sc_w_in_2"][0]
        COL_SOURCES = {
            "ret_q": (w_ret, 0), "ret_k": (w_ret, D), "ret_v": (w_ret, 2 * D), "ret_g": (w_ret, 2 * D + RV),
            "fox_q": (w_fox, 0), "fox_k": (w_fox, D), "fox_v": (w_fox, 2 * D), "fox_g": (w_fox, 3 * D),
            "conf_a": (w_conf, 0), "conf_g": (w_conf, D),
            "ffn_gate": (t["ffn_w_gate_2"][0], 0), "ffn_up": (t["ffn_w_up_2"][0], 0),
            "sc_b": (w_sc, 0), "sc_c": (w_sc, D), "sc_h": (w_sc, 2 * D)}
        ROW_SOURCES = {"ret_out": t["ret_w_out"][0], "fox_out": t["fox_w_out"][0],
                       "conf_out": t["conf_w_out_2"][0], "ffn_down": t["ffn_w_down_2"][0],
                       "sc_out": t["sc_w_out_2"][0]}

        def slot_cols(s):
            return ring[:, s].rearrange("p (k n) -> p k n", k=KB)

        def slot_rows(s):
            return ring[:, s].rearrange("p (r n) -> p r n", r=ROWS)

        def pre_load(n):
            name, i = PLAN[n]
            s = pre_slot(n)
            if name in COL_SOURCES:
                w, at = COL_SOURCES[name]
                at += COLS * i
                width = min(COLS, DFF - COLS * i) if name.startswith("ffn") else COLS
                return slot_cols(s)[:, :, 0:width], cols(w, at, width)
            w = ROW_SOURCES[name]
            blocks = min(ROWS, w.shape[0] // P - ROWS * i)
            return slot_rows(s)[:, 0:blocks, :], rows(w, ROWS * i, blocks)

        def released(n):
            name, i = PLAN[n]
            if name in ROW_SOURCES:
                if (name, i + 1) not in CHUNK_AT:
                    return bank_filled, BANK_AT[OUT_BANKS[name], 3] + 1
                return weights_used, sum(PLAN[m][0] in ROW_SOURCES and (PLAN[m][0], PLAN[m][1] + 1) in CHUNK_AT
                                         for m in range(n + 1))
            bank, per = COL_BANKS[name]
            i = min(per * (i + 1), FB) if bank == "ffn" else per * (i + 1)
            return bank_filled, BANK_AT[bank, i - 1] + 1

        def by_width(eng, e, body):
            count = eng.value_load(counts[0:1, bass.ds(e, 1)], min_val=0, max_val=T)

            def pick(widths):
                if len(widths) == 1:
                    body(e, widths[0])
                    return
                with eng.If(count <= widths[0]):
                    body(e, widths[0])
                with eng.Else():
                    pick(widths[1:])

            pick(WIDTHS)

        block = ctx.enter_context(nc.Block())

        @block.sync
        def _(sp):
            def load_mod(n):
                i, k, half = n // 16, (n % 16) // 2, n % 2
                if n >= 2:
                    sp.wait_ge(mod_used, n - 1)
                sp.dma_start(mod_w[:, n % 2, :], t["mod_w"][i, k * P:(k + 1) * P, half * 1536:(half + 1) * 1536]
                             ).then_inc(mod_filled[n % 2], 16)

            for n in range(16):
                load_mod(n)
            for n in range(PRE):
                if n >= PRE_RING:
                    sp.wait_ge(*released(n - PRE_RING))
                dst, src = pre_load(n)
                sp.dma_start(dst, src).then_inc(slot_filled[pre_slot(n)], 16)
                if 4 <= n < 12:
                    for m in range(2):
                        load_mod(16 + 2 * (n - 4) + m)

            def wait_used(e, j):
                r = j - 2 * PAIRS
                if r < 0:
                    sp.wait_ge(gu_filled, e * EB + 4 * (j // 2 + 1))
                elif r < DOWNS - 1:
                    sp.wait_ge(weights_used, e * (DOWNS - 1) + PRE_ROWS + r + 1)
                else:
                    sp.wait_ge(wide_filled, e * 4 + 3)

            def load_expert(e, j):
                s = j % RING
                if j < 2 * PAIRS:
                    w = t["moe_w_gate_2"] if j % 2 == 0 else t["moe_w_up_2"]
                    src = w[0].rearrange("e (k p) n -> e p k n", p=P)[
                        bass.ds(e, 1), :, :, (j // 2) * COLS:(j // 2 + 1) * COLS]
                    dst = slot_cols(s)
                else:
                    r = (j - 2 * PAIRS) * ROWS
                    src = t["moe_w_down_2"][0].rearrange("e (r p) n -> e p r n", p=P)[bass.ds(e, 1), :, r:r + ROWS, :]
                    dst = slot_rows(s)
                sp.dma_start(dst, src.rearrange("o p k n -> (o p) k n")).then_inc(slot_filled[s], 16)

            for j in range(PER_EXPERT):
                if j < PRE_RING:
                    sp.wait_ge(*released(PRE - PRE_RING + j))
                elif j == RING - 1:
                    sp.wait_ge(mod_used, 32)
                    sp.wait_ge(emptied["D"], emptied_by(BANK_AT["ret_s", RH - 1])[1])
                else:
                    wait_used(0, j - RING)
                load_expert(0, j)
            with sp.Fori(1, NE) as e:
                for j in range(PER_EXPERT):
                    if j < RING:
                        wait_used(e - 1, j + PER_EXPERT - RING)
                    else:
                        wait_used(e, j - RING)
                    load_expert(e, j)

            sp.wait_ge(x_ready, 5)
            sp.dma_start(out[0].rearrange("(t p) d -> p t d", p=P), x[:, :, :]).then_inc(out_written, 16)
            sp.wait_ge(out_written, 16)

        @block.tensor
        def _(pe):
            mm = nc.tensor.matmul

            def take_bank(name, i):
                n = BANK_AT[name, i]
                if n >= NBANK:
                    who, count = emptied_by(n - NBANK)
                    pe.wait_ge(emptied[who], count)
                return psum[:, n % NBANK, :]

            def weights(name, i):
                n = CHUNK_AT[name, i]
                s = pre_slot(n)
                pe.wait_ge(slot_filled[s], 16 * pre_fill(n))
                return slot_cols(s) if name in COL_SOURCES else slot_rows(s)

            def transpose_in(name, src, n=4):
                for g in range(n):
                    b = take_bank(name, g)
                    for j in range(2):
                        for tt in range(NT):
                            last = nc.tensor.transpose(b[:, j * T + tt * P:j * T + (tt + 1) * P],
                                                       src[:, tt, (2 * g + j) * P:(2 * g + j + 1) * P], ident)
                    last.then_inc(bank_filled, 1)

            def feature_block(dst, w, blk, src=xT):
                for k in range(KB):
                    last = mm(dst, w[:, k, blk * P:(blk + 1) * P], src[:, k, :], start=(k == 0), stop=(k == KB - 1))
                return last

            def token_chunk(name, i, bank_name=None):
                w = weights(name, i)
                for tt in range(NT):
                    b = take_bank(bank_name or name, NT * i + tt)
                    for k in range(KB):
                        last = mm(b, xT[:, k, tt * P:(tt + 1) * P], w[:, k, :], start=(k == 0), stop=(k == KB - 1))
                    last.then_inc(bank_filled, 1)
                return last

            def out_product(name, bank_name, src, blocks):
                banks = [take_bank(bank_name, i) for i in range(4)]
                for k in range(blocks):
                    if k % ROWS == 0:
                        w = weights(name, k // ROWS)
                    for tt in range(NT):
                        for half in range(2):
                            last = mm(banks[2 * tt + half], src[:, k, tt * P:(tt + 1) * P],
                                      w[:, k % ROWS, half * 512:(half + 1) * 512],
                                      start=(k == 0), stop=(k == blocks - 1))
                            if k == blocks - 1:
                                last.then_inc(bank_filled, 1)
                    if k % ROWS == ROWS - 1 and k < blocks - 1:
                        last.then_inc(weights_used, 1)

            pe.wait_ge(const_loaded, 16)
            pe.wait_ge(vec_loaded, 7 * 16)
            b = take_bank("vecs", 0)
            for k in range(KB):
                last = nc.tensor.transpose(b[:, k * NVEC:(k + 1) * NVEC], vec_rows[:, k * P:(k + 1) * P],
                                           ident[0:NVEC, 0:NVEC])
            last.then_inc(bank_filled, 1)

            def modulation_columns(i):
                pe.wait_ge(mod_used, 16 * (i + 1))
                b = take_bank("mod_cols", i)
                for m in range(2 * KB):
                    last = mm(b[:, m:m + 1], acc[:, m * P:(m + 1) * P], ones[:, 0:1], start=True, stop=True)
                last.then_inc(bank_filled, 1)

            def modulation_gate(i):
                for half in range(2):
                    b = take_bank("mod_gate", 2 * i + half)
                    mm(b, ones, acc[:, 2 * D + half * 512:2 * D + (half + 1) * 512], start=True, stop=True
                       ).then_inc(bank_filled, 1)

            modulation_columns(0)
            pe.wait_ge(xn_ready, 1)
            transpose_in("x0T", xn)
            modulation_gate(0)
            pe.wait_ge(emptied["A"], emptied_by(BANK_AT["x0T", 3])[1])
            for name in ("ret_q", "ret_k"):
                for c in range(2):
                    w = weights(name, c)
                    for j in range(2):
                        b = take_bank(name, 2 * c + j)
                        feature_block(b[:, 0:T], w, 2 * j)
                        last = feature_block(b[:, T:2 * T], w, 2 * j + 1)
                        last.then_inc(bank_filled, 1)
            for name in ("ret_v", "ret_g"):
                for c in range(4):
                    token_chunk(name, c)

            def ret_scores(h):
                b = take_bank("ret_s", h)
                pe.wait_ge(emptied["D"], emptied_by(BANK_AT["ret_k", RH - 1])[1])
                for d in range(2):
                    mm(b[:, 0:T], rk[:, 2 * h + d, 0:P], rq[:, 2 * h + d, :], start=(d == 0), stop=(d == 1))
                for d in range(2):
                    last = mm(b[:, T:T + P], rk[:, 2 * h + d, P:T], rq[:, 2 * h + d, P:T], start=(d == 0), stop=(d == 1))
                last.then_inc(bank_filled, 1)

            ret_scores(0)
            pe.wait_ge(emptied["A"], emptied_by(BANK_AT["ret_v", 7])[1])
            for h in range(RH):
                if h + 1 < RH:
                    ret_scores(h + 1)
                pe.wait_ge(emptied["D"], emptied_by(BANK_AT["ret_s", h])[1])
                p, cols_h = dec_p[:, h % 2, :], slice(h * RHV, (h + 1) * RHV)
                b = take_bank("ret_o", 2 * h)
                mm(b, p[:, 0:P], rv[:, 0, cols_h], start=True, stop=True).then_inc(bank_filled, 1)
                b = take_bank("ret_o", 2 * h + 1)
                mm(b, p[:, P:2 * P], rv[:, 0, cols_h], start=True, stop=False)
                mm(b, p[:, 2 * P:3 * P], rv[:, 1, cols_h], start=False, stop=True).then_inc(bank_filled, 1)
            pe.wait_ge(ret_u_ready, 2 * RH)
            transpose_in("ret_uT", rg, 8)
            pe.wait_ge(emptied["A"], emptied_by(BANK_AT["ret_uT", 7])[1])
            out_product("ret_out", "ret_y", ruT, RV // P)

            modulation_columns(1)
            modulation_gate(1)
            pe.wait_ge(xn_ready, 2)
            transpose_in("x1T", xn)
            pe.wait_ge(emptied["A"], emptied_by(BANK_AT["x1T", 3])[1])
            b = take_bank("fox_f", 0)
            pe.wait_ge(small_loaded, 7 * 16)
            for tt in range(NT):
                for k in range(KB):
                    last = mm(b[:, tt * FH:(tt + 1) * FH], xT[:, k, tt * P:(tt + 1) * P], wf[:, k, :],
                              start=(k == 0), stop=(k == KB - 1))
            last.then_inc(bank_filled, 1)
            for name in ("fox_q", "fox_k"):
                for c in range(2):
                    token_chunk(name, c)
            pe.wait_ge(logf_ready, 1)
            b = take_bank("fox_cum", 0)
            mm(b[:, 0:FH], tri, logf[:, 0, :], start=True, stop=True)
            mm(b[:, FH:2 * FH], ones, logf[:, 0, :], start=True, stop=False)
            mm(b[:, FH:2 * FH], tri, logf[:, 1, :], start=False, stop=True)
            mm(b[0:FH, P:2 * P], logf[:, 0, :], tri, start=True, stop=True)
            mm(b[0:FH, 2 * P:3 * P], logf[:, 0, :], ones, start=True, stop=False)
            mm(b[0:FH, 2 * P:3 * P], logf[:, 1, :], tri, start=False, stop=True).then_inc(bank_filled, 1)
            for c in range(2):
                token_chunk("fox_v", c)
            for c in range(2):
                w = weights("fox_g", c)
                for j in range(2):
                    b = take_bank("fox_g", 2 * c + j)
                    feature_block(b[:, 0:T], w, 2 * j)
                    last = feature_block(b[:, T:2 * T], w, 2 * j + 1)
                    last.then_inc(bank_filled, 1)
            pe.wait_ge(emptied["D"], emptied_by(BANK_AT["fox_q", 3])[1])
            transpose_in("fox_qT", fq_tok)
            pe.wait_ge(emptied["D"], emptied_by(BANK_AT["fox_k", 3])[1])
            transpose_in("fox_kT", fk_tok)

            def fox_scores(h):
                b = take_bank("fox_s", h)
                part, blk = FD * (h % 2), h // 2
                pick = ident[0:FH, h:h + 1].to_broadcast([FH, P])
                for tt, lo, n in ((0, 0, P), (1, P, T)):
                    mm(b[:, lo:lo + n], fqT[part:part + FD, blk, tt * P:(tt + 1) * P], fkT[part:part + FD, blk, 0:n],
                       start=True, stop=False)
                    last = mm(b[:, lo:lo + n], pick, ncumT[:, 0:n], start=False, stop=True)
                last.then_inc(bank_filled, 1)

            def fox_turn(h):
                b = take_bank("fox_pT", h)
                pe.wait_ge(probs_ready, h + 1)
                for j in range(3):
                    last = nc.tensor.transpose(b[:, j * P:(j + 1) * P], prob[:, h % 2, j * P:(j + 1) * P], ident)
                last.then_inc(bank_filled, 1)

            def fox_read(pair):
                b = take_bank("fox_o", pair)
                pe.wait_ge(emptied["A"], emptied_by(BANK_AT["fox_pT", 2 * pair + 1])[1])
                for j in range(2):
                    h = 2 * pair + j
                    p, o, f = probT[:, h % 4, :], b[FD * j:FD * (j + 1), :], slice(h * FD, (h + 1) * FD)
                    mm(o[:, 0:T], fv[:, 0, f], p[:, 0:T], start=True, stop=False)
                    last = mm(o[:, P:T], fv[:, 1, f], p[:, T:3 * P], start=False, stop=True)
                last.then_inc(bank_filled, 1)

            pe.wait_ge(emptied["D"], emptied_by(BANK_AT["fox_kT", 3])[1])
            for i in range(FH + 2):
                if i < FH:
                    fox_scores(i)
                if 1 <= i <= FH:
                    fox_turn(i - 1)
                if i >= 3 and i % 2 == 1:
                    fox_read((i - 3) // 2)
            pe.wait_ge(emptied["D"], emptied_by(BANK_AT["fox_o", KB - 1])[1])
            out_product("fox_out", "fox_y", fuT, KB)

            pe.wait_ge(x_ready, 1)
            transpose_in("x2T", x)
            pe.wait_ge(emptied["A"], emptied_by(BANK_AT["x2T", 3])[1])
            for c in range(2):
                wa, wg = weights("conf_a", c), weights("conf_g", c)
                for blk in range(4):
                    b = take_bank("conf", 4 * c + blk)
                    feature_block(b[:, 0:T], wa, blk)
                    last = feature_block(b[:, T:2 * T], wg, blk)
                    last.then_inc(bank_filled, 1)
            for g in range(4):
                tt, half = g // 2, g % 2
                b = take_bank("conf_cT", g)
                pe.wait_ge(conv_ready, 4 * half + 4)
                for j in range(4):
                    last = nc.tensor.transpose(b[:, j * P:(j + 1) * P], conv[:, 4 * half + j, tt * P:(tt + 1) * P], ident)
                last.then_inc(bank_filled, 1)
            pe.wait_ge(emptied["D"], emptied_by(BANK_AT["conf_cT", 3])[1])
            transpose_in("conf_nT", conf_n)
            pe.wait_ge(emptied["A"], emptied_by(BANK_AT["conf_nT", 3])[1])
            out_product("conf_out", "conf_y", conf_uT, KB)

            pe.wait_ge(x_ready, 2)
            transpose_in("x3T", x)
            pe.wait_ge(emptied["A"], emptied_by(BANK_AT["x3T", 3])[1])
            for c in range(6):
                wg, wu = weights("ffn_gate", c), weights("ffn_up", c)
                for blk in range(min(4, FB - 4 * c)):
                    b = take_bank("ffn", 4 * c + blk)
                    feature_block(b[:, 0:T], wg, blk)
                    last = feature_block(b[:, T:2 * T], wu, blk)
                    last.then_inc(bank_filled, 1)
            pe.wait_ge(emptied["D"], emptied_by(BANK_AT["ffn", FB - 1])[1])
            out_product("ffn_down", "ffn_y", ffn_h, FB)

            pe.wait_ge(x_ready, 3)
            transpose_in("x4T", x)
            pe.wait_ge(emptied["A"], emptied_by(BANK_AT["x4T", 3])[1])
            for c in range(2):
                wc, wh, wb = weights("sc_c", c), weights("sc_h", c), weights("sc_b", c)
                for blk in range(4):
                    b = take_bank("sc_ch", 4 * c + blk)
                    feature_block(b[:, 0:T], wc, blk)
                    feature_block(b[:, T:2 * T], wh, blk).then_inc(bank_filled, 1)
                    b = take_bank("sc_b", 4 * c + blk)
                    last = feature_block(b[:, 0:T], wb, blk)
                    last.then_inc(bank_filled, 1)
            pe.wait_ge(emptied["D"], emptied_by(BANK_AT["sc_b", KB - 1])[1])
            out_product("sc_out", "sc_y", sc_uT, KB)

            pe.wait_ge(x_ready, 4)
            transpose_in("x5T", x)
            pe.wait_ge(emptied["A"], emptied_by(BANK_AT["x5T", 3])[1])
            b = take_bank("route", 0)
            for tt in range(NT):
                for k in range(KB):
                    last = mm(b[:, tt * NE:(tt + 1) * NE], xT[:, k, tt * P:(tt + 1) * P], w_router[:, k, :],
                              start=(k == 0), stop=(k == KB - 1))
            last.then_inc(bank_filled, 1)
            chosen = rt[:, 9]
            pe.wait_ge(mask_ready, 1)
            b = take_bank("rank", 0)
            mm(b[:, 0:NE], strict, chosen[:, 0, :], start=True, stop=True)
            mm(b[:, NE:2 * NE], ones, chosen[:, 0, :], start=True, stop=False)
            mm(b[:, NE:2 * NE], strict, chosen[:, 1, :], start=False, stop=True)
            mm(b[:, 2 * NE:3 * NE], ones, chosen[:, 0, :], start=True, stop=False)
            mm(b[:, 2 * NE:3 * NE], ones, chosen[:, 1, :], start=False, stop=True).then_inc(bank_filled, 1)

            pe.wait_ge(emptied["A"], ALL_EMPTIED["A"])
            pe.wait_ge(emptied["D"], ALL_EMPTIED["D"])

            def expert(e, width):
                rows_n, tiles = min(width, P), -(-width // P)

                def chunk(j):
                    s = j % RING
                    pe.wait_ge(slot_filled[s], e * (16 * PER_EXPERT // RING) + 16 * (PRE_FILLS[s] + j // RING + 1))
                    return slot_cols(s) if j < 2 * PAIRS else slot_rows(s)

                pe.wait_ge(sel_ready, e + 1)
                pe.wait_ge(wide_emptied, e * 4 + 1)
                for k in range(KB):
                    dst = psum[:, k // 2, (k % 2) * 256:(k % 2) * 256 + width]
                    for tt in range(NT):
                        last = mm(dst, x[:, tt, k * P:(k + 1) * P], e_sel[:, tt, 0:width],
                                  start=(tt == 0), stop=(tt == NT - 1))
                last.then_inc(wide_filled, 1)
                pe.wait_ge(wide_emptied, e * 4 + 2)
                for c in range(PAIRS):
                    wg, wu = chunk(2 * c), chunk(2 * c + 1)
                    for blk in range(4):
                        n = 4 * c + blk
                        b = psum[:, 4 + n % 4, :]
                        pe.wait_ge(gu_emptied, e * EB + n + 1)
                        for k in range(KB):
                            mm(b[:, 0:width], wg[:, k, blk * P:(blk + 1) * P], e_x[:, k, 0:width],
                               start=(k == 0), stop=(k == KB - 1))
                        for k in range(KB):
                            last = mm(b[:, 256:256 + width], wu[:, k, blk * P:(blk + 1) * P], e_x[:, k, 0:width],
                                      start=(k == 0), stop=(k == KB - 1))
                        last.then_inc(gu_filled, 1)
                for j in range(tiles):
                    for tt in range(NT):
                        last = nc.tensor.transpose(psum[0:rows_n, 0, j * 256 + tt * P:j * 256 + (tt + 1) * P],
                                                   e_sel[:, tt, j * P:j * P + rows_n], ident)
                last.then_inc(wide_filled, 1)
                pe.wait_ge(wide_emptied, e * 4 + 3)
                for k in range(EB):
                    if k % ROWS == 0:
                        w = chunk(2 * PAIRS + k // ROWS)
                    if k == 0 or k >= EB - 4:
                        pe.wait_ge(gu_emptied, e * EB + 4 + max(k + 1, EB - 4))
                    for j in range(tiles):
                        for half in range(2):
                            last = mm(psum[0:rows_n, 2 * j + half, :], e_h[:, k, j * P:j * P + rows_n],
                                      w[:, k % ROWS, half * 512:(half + 1) * 512], start=(k == 0), stop=(k == EB - 1))
                    if k % ROWS == ROWS - 1 and k < EB - 1:
                        last.then_inc(weights_used, 1)
                last.then_inc(wide_filled, 1)
                pe.wait_ge(wide_emptied, e * 4 + 4)
                for tt in range(NT):
                    for half in range(2):
                        for j in range(tiles):
                            last = mm(psum[:, 2 * tt + half, :], e_selT[0:rows_n, j, tt * P:(tt + 1) * P],
                                      e_y[0:rows_n, j, half * 512:(half + 1) * 512],
                                      start=(j == 0), stop=(j == tiles - 1))
                last.then_inc(wide_filled, 1)

            with pe.Fori(0, NE) as e:
                by_width(pe, e, expert)

        @block.scalar
        def _(act):
            act.dma_start(const[:, :], t["const"]).then_inc(const_loaded, 16)
            for lo, src in ((V_C, t["c"]), (V_NORM, t["norm_g"]), (V_CB, t["conf_b_dw_2"]),
                            (V_CG, t["conf_ln_g_2"]), (V_CBETA, t["conf_ln_b_2"]),
                            (V_SC, t["sc_w_conv_2"][0]), (V_DW, t["conf_w_dw_2"][0])):
                act.dma_start(vec_rows[lo:lo + src.shape[0], :], src).then_inc(vec_loaded, 16)
            act.dma_start(x[:, :, :], t["x"][0].rearrange("(t p) d -> p t d", p=P)).then_inc(x_loaded, 16)
            act.dma_start(pos_i[:, :], t["positions"][0:1, :].to_broadcast([P, T])).then_inc(pos_loaded, 16)
            act.dma_start(decay, t["decay"].rearrange("p (h n) -> p h n", h=RH)).then_inc(small_loaded, 16)
            act.dma_start(wf[:, :, :], cols(w_fox, 4 * D, FH)).then_inc(small_loaded, 16)
            act.dma_start(w_router[:, :, :], cols(t["moe_w_router_2"][0], 0, NE)).then_inc(small_loaded, 16)
            for j in range(2):
                act.dma_start(gains[j * FD:(j + 1) * FD, 0:1], t["fox_q_gain"].rearrange("a d -> d a")
                              ).then_inc(small_loaded, 16)
                act.dma_start(gains[j * FD:(j + 1) * FD, 1:2], t["fox_k_gain"].rearrange("a d -> d a")
                              ).then_inc(small_loaded, 16)

            steps = [0]

            def step(ins):
                steps[0] += 1
                ins.then_inc(scalar_step, 1)
                act.wait_ge(scalar_step, steps[0])

            def bank(name, i):
                n = BANK_AT[name, i]
                act.wait_ge(bank_filled, n + 1)
                return psum[:, n % NBANK, :]

            def pairs(b):
                return b.rearrange("p (j n) -> p j n", j=2)

            def square_rows():
                for tt in range(NT):
                    last = nc.scalar.activation(xn[:, tt, :], x[:, tt, :], ACT.Square, scale=float(D) ** -0.5,
                                                accum_out=sumsq[:, tt:tt + 1])
                last.then_inc(sumsq_ready, 1)

            act.wait_ge(x_loaded, 16)
            square_rows()
            act.wait_ge(emptied["D"], emptied_by(BANK_AT["vecs", 0])[1])
            nc.scalar.activation(c_act[:, :], vec[:, :, V_C], ACT.Silu).then_inc(c_ready, 1)
            act.wait_ge(ang_ready, 1)
            nc.scalar.activation(cos[:, :], ang[:, 4, :], ACT.Sin)
            nc.scalar.activation(sin[:, :], ang[:, 3, :], ACT.Sin).then_inc(trig_ready, 1)

            def layer_input(name):
                for g in range(4):
                    b = pairs(bank(name, g))
                    for j in range(2):
                        k = 2 * g + j
                        last = nc.scalar.activation(xT[:, k, :], b[:, j, :], ACT.Identity,
                                                    scale=in_scale[:, k:k + 1], bias=in_shift[:, k:k + 1])
                    last.then_inc(emptied["A"], 1)

            def copy_in(name, dst, n=4):
                for g in range(n):
                    nc.scalar.copy(dst[:, 2 * g:2 * g + 2, :], pairs(bank(name, g))).then_inc(emptied["A"], 1)

            act.wait_ge(emptied["D"], emptied_by(BANK_AT["mod_cols", 0])[1])
            layer_input("x0T")
            for i in range(8):
                tt, c = i % 2, i // 2
                if i == 0:
                    act.wait_ge(trig_ready, 1)
                nc.scalar.copy(rv[:, tt, c * 512:(c + 1) * 512], bank("ret_v", i)).then_inc(emptied["A"], 1)
            for i in range(8):
                tt, c = i % 2, i // 2
                nc.scalar.activation(rg[:, tt, c * 512:(c + 1) * 512], bank("ret_g", i), ACT.Silu
                                     ).then_inc(emptied["A"], 1)
            copy_in("ret_uT", ruT, 8)

            act.wait_ge(emptied["D"], emptied_by(BANK_AT["ret_y", 3])[1])
            square_rows()
            act.wait_ge(emptied["D"], emptied_by(BANK_AT["mod_cols", 1])[1])
            layer_input("x1T")
            for s, name in enumerate(("fox_q", "fox_k")):
                for i in range(4):
                    n = 4 * s + i
                    b = bank(name, i)
                    if n >= 2:
                        act.wait_ge(fox_sq_used, n - 1)
                    if n == 0:
                        act.wait_ge(emptied["D"], emptied_by(BANK_AT["mod_gate", 3])[1])
                    nc.scalar.activation(fsq[:, n % 2, :], b, ACT.Square).then_inc(fox_sq, 1)
                if s == 0:
                    act.wait_ge(logf_in, 1)
                    step(nc.scalar.activation(logf_t[:, 1, :], logf_t[:, 1, :], ACT.Exp))
                    nc.scalar.activation(logf_t[:, 1, :], logf_t[:, 1, :], ACT.Ln, bias=1.0).then_inc(logf_mid, 1)
            for i in range(4):
                tt, c = i % 2, i // 2
                nc.scalar.copy(fv[:, tt, c * 512:(c + 1) * 512], bank("fox_v", i)).then_inc(emptied["A"], 1)
            for g in range(4):
                nc.scalar.activation(fgT[:, 2 * g:2 * g + 2, :], pairs(bank("fox_g", g)), ACT.Silu
                                     ).then_inc(emptied["A"], 1)
            for i in range(FH + 1):
                if i < FH:
                    act.wait_ge(logits_ready, i + 1)
                    if i >= 2:
                        act.wait_ge(bank_filled, BANK_AT["fox_pT", i - 2] + 1)
                    nc.scalar.activation(prob[:, i % 2, 0:P], logits[:, i % 2, 0:P], ACT.Exp,
                                         bias=mx[:, i % 2, 0:1], accum_out=rsum[:, i % 2, 0:1])
                    nc.scalar.activation(prob[:, i % 2, P:3 * P], logits[:, i % 2, P:3 * P], ACT.Exp,
                                         bias=mx[:, i % 2, 1:2], accum_out=rsum[:, i % 2, 1:2]).then_inc(probs_exp, 1)
                if i >= 1:
                    h = i - 1
                    if h >= 4:
                        act.wait_ge(bank_filled, BANK_AT["fox_o", (h - 4) // 2] + 1)
                    nc.scalar.copy(probT[:, h % 4, :], bank("fox_pT", h)[:, 0:3 * P]).then_inc(emptied["A"], 1)
            act.wait_ge(emptied["D"], emptied_by(BANK_AT["fox_y", 3])[1])
            square_rows()

            def load_rows(g, b, n):
                act.wait_ge(x_ready, n)
                act.dma_start(rows_gb[:, 0, :], g.to_broadcast([P, D])).then_inc(rows_loaded, 16)
                act.dma_start(rows_gb[:, 1, :], b.to_broadcast([P, D])).then_inc(rows_loaded, 16)

            act.dma_start(final_row, t["final_g"].to_broadcast([P, D])).then_inc(final_loaded, 16)

            load_rows(t["ln_mix_g_2"][0:1, :], t["ln_mix_b_2"][0:1, :], 1)
            copy_in("x2T", xT)
            for i in range(KB):
                b = bank("conf", i)
                if i >= 2:
                    act.wait_ge(emptied["D"], emptied_by(BANK_AT["conf", i - 2])[1])
                nc.scalar.activation(half_gate[:, i % 2, :], b[:, T:2 * T], ACT.Tanh, scale=0.5).then_inc(half_ready, 1)
            for g in range(4):
                b = pairs(bank("conf_nT", g))
                for j in range(2):
                    k = 2 * g + j
                    last = nc.scalar.activation(conf_uT[:, k, :], b[:, j, :], ACT.Silu,
                                                scale=vec[:, k, V_CG:V_CG + 1], bias=vec[:, k, V_CBETA:V_CBETA + 1])
                last.then_inc(emptied["A"], 1)

            load_rows(t["ln_ffn_g_2"][0:1, :], t["ln_ffn_b_2"][0:1, :], 2)
            copy_in("x3T", xT)
            for i in range(FB):
                b = bank("ffn", i)
                if i >= 2:
                    act.wait_ge(emptied["D"], emptied_by(BANK_AT["ffn", i - 2])[1])
                nc.scalar.activation(ffn_s[:, i % 2, :], b[:, 0:T], ACT.Silu).then_inc(silu_ready, 1)

            load_rows(t["ln_mix_g_2"][1:2, :], t["ln_mix_b_2"][1:2, :], 3)
            copy_in("x4T", xT)
            for i in range(KB):
                b = bank("sc_ch", i)
                if i >= 2:
                    act.wait_ge(emptied["D"], emptied_by(BANK_AT["sc_ch", i - 2])[1])
                nc.scalar.copy(sc_c[:, i % 2, :], b[:, 0:T]).then_inc(c_copied, 1)

            act.wait_ge(x_ready, 4)
            copy_in("x5T", xT)
            act.wait_ge(lg_ready, 1)
            nc.scalar.activation(rt[:, 11, :, 0], rt[:, 10, :, 0], ACT.Exp).then_inc(lg_exp, 1)
            act.wait_ge(emptied["D"], ALL_EMPTIED["D"])

            def expert(e, width):
                for n in range(EB):
                    act.wait_ge(gu_filled, e * EB + n + 1)
                    act.wait_ge(gu_emptied, e * EB + n + 3)
                    nc.scalar.activation(e_s[:, n % 2, 0:width], psum[:, 4 + n % 4, 0:width], ACT.Silu
                                         ).then_inc(e_silu, 1)

            act.dma_start(out_g, t["ln_ffn_g_2"][1:2, :].to_broadcast([P, D])).then_inc(rows_loaded, 16)
            act.dma_start(out_b, t["ln_ffn_b_2"][1:2, :].to_broadcast([P, D])).then_inc(rows_loaded, 16)
            with act.Fori(0, NE) as e:
                by_width(act, e, expert)

        @block.gpsimd
        def _(pool):
            pool.dma_start(bf_row[:, :], t["fox_b_f"].to_broadcast([P, FH])).then_inc(bf_loaded, 16)
            nc.gpsimd.memset(neg_half[:, :], -0.5).then_inc(gpsimd_step, 1)
            pool.wait_ge(gpsimd_step, 1)
            for n, name in enumerate(ROOTS):
                if name in ("rms0", "ret0"):
                    i = int(name == "ret0")
                    pool.wait_ge(acc_clear, i + 1)
                    pool.dma_start(acc[0:1, :], t["mod_b"][i:i + 1, :]).then_inc(acc_seeded, 16)
                w = ROOT_WIDTH.get(name, NT)
                pool.wait_ge(root_asked, n + 1)
                nc.gpsimd.tensor_tensor(root_out[:, n % 2, 0:w], root_in[:, n % 2, 0:w], neg_half[:, 0:w], ALU.pow
                                        ).then_inc(root_ready, 1)

        @block.vector
        def _(dve):
            v = nc.vector
            steps = [0]
            base = [0]

            def step(ins):
                steps[0] += 1
                ins.then_inc(vector_step, 1)
                dve.wait_ge(vector_step, base[0] + steps[0])

            def bank(name, i):
                n = BANK_AT[name, i]
                dve.wait_ge(bank_filled, n + 1)
                return psum[:, n % NBANK, :]

            def pairs(b):
                return b.rearrange("p (j n) -> p j n", j=2)

            def ask_root(name, src, scale, eps):
                n = ROOTS.index(name)
                w = ROOT_WIDTH.get(name, NT)
                v.tensor_scalar(root_in[:, n % 2, 0:w], src, scale, eps, ALU.mult, ALU.add).then_inc(root_asked, 1)

            def root(name):
                n = ROOTS.index(name)
                dve.wait_ge(root_ready, n + 1)
                return root_out[:, n % 2, :]

            def angles():
                dve.wait_ge(pos_loaded, 16)
                dve.wait_ge(const_loaded, 16)
                step(v.tensor_copy(ang[:, 0, :], pos_i[:, :]))
                step(v.tensor_scalar(ang[:, 1, :], ang[:, 0, :], const[:, C_INV:C_INV + 1], None, ALU.mult))
                magic = 12582912.0
                step(v.tensor_scalar(ang[:, 2, :], ang[:, 1, :], float(1 / (2 * np.pi)), magic, ALU.mult, ALU.add))
                step(v.tensor_scalar(ang[:, 2, :], ang[:, 2, :], magic, None, ALU.subtract))
                c1 = 6.28125
                c2 = float(np.round((2 * np.pi - c1) * 2 ** 19) / 2 ** 19)
                c3 = float(2 * np.pi - c1 - c2)
                for c in (c1, c2, c3):
                    step(v.scalar_tensor_tensor(ang[:, 1, :], ang[:, 2, :], -c, ang[:, 1, :], ALU.mult, ALU.add))
                top = 3.1415925
                step(v.tensor_scalar(ang[:, 4, :], ang[:, 1, :], float(np.pi / 2), None, ALU.add))
                step(v.tensor_scalar(ang[:, 5, :], ang[:, 4, :], float(np.pi), float(-2 * np.pi), ALU.is_gt, ALU.mult))
                step(v.tensor_tensor(ang[:, 5, :], ang[:, 5, :], ang[:, 4, :], ALU.add))
                step(v.tensor_scalar(ang[:, 4, :], ang[:, 5, :], top, -top, ALU.min, ALU.max))
                v.tensor_scalar(ang[:, 3, :], ang[:, 1, :], top, -top, ALU.min, ALU.max).then_inc(ang_ready, 1)

            v.tensor_copy(vec[:, :, :].rearrange("p k n -> p (k n)"), bank("vecs", 0)[:, 0:KB * NVEC]
                          ).then_inc(emptied["D"], 1)

            def clear_acc(i):
                v.memset(acc, 0.0).then_inc(acc_clear, 1)

            def modulation(i, n):
                if n % 16 == 0:
                    dve.wait_ge(acc_seeded, 16 * (i + 1))
                    if i == 0:
                        dve.wait_ge(c_ready, 1)
                half = n % 2
                dve.wait_ge(mod_filled[n % 2], 16 * (n // 2 + 1))
                a = acc[:, half * 1536:(half + 1) * 1536]
                k = (n % 16) // 2
                if n % 16 >= 2:
                    dve.wait_ge(mod_used, n - 1)
                v.scalar_tensor_tensor(a, mod_w[:, n % 2, :], c_act[:, k:k + 1], a, ALU.mult, ALU.add
                                       ).then_inc(mod_used, 1)

            def normalise(name, n):
                dve.wait_ge(sumsq_ready, n)
                ask_root(name, sumsq[:, :], 1.0, RMS_EPS)
                r = root(name)
                for tt in range(NT):
                    last = v.tensor_scalar(xn[:, tt, :], x[:, tt, :], r[:, tt:tt + 1], None, ALU.mult)
                last.then_inc(xn_ready, 1)

            def input_affine(i):
                b = bank("mod_cols", i)
                v.scalar_tensor_tensor(in_scale[:, :], b[:, KB:2 * KB], 1.0, vec[:, :, V_NORM + i], ALU.add, ALU.mult)
                v.tensor_copy(in_shift[:, :], b[:, 0:KB]).then_inc(emptied["D"], 1)

            def gate_row(i):
                for half in range(2):
                    v.tensor_copy(gate[:, half * 512:(half + 1) * 512], bank("mod_gate", 2 * i + half)
                                  ).then_inc(emptied["D"], 1)

            def gated_residual(name, tmp):
                for i in range(4):
                    xi = x[:, i // 2, (i % 2) * 512:(i % 2 + 1) * 512]
                    step(v.tensor_tensor(tmp[:, i % 2, :], bank(name, i), gate[:, (i % 2) * 512:(i % 2 + 1) * 512],
                                         ALU.mult))
                    v.tensor_tensor(xi, xi, tmp[:, i % 2, :], ALU.add).then_inc(emptied["D"], 1)

            clear_acc(0)
            dve.wait_ge(acc_clear, 1)
            normalise("rms0", 1)
            angles()
            for n in range(16):
                modulation(0, n)
            input_affine(0)
            gate_row(0)

            dve.wait_ge(trig_ready, 1)
            dve.wait_ge(emptied["D"], emptied_by(BANK_AT["mod_gate", 1])[1])
            clear_acc(1)
            for name, dst in (("ret_q", rq), ("ret_k", rk)):
                for h in range(RH):
                    b = pairs(bank(name, h))
                    c2 = cos[:, :].unsqueeze(1).to_broadcast([P, 2, T])
                    s2 = sin[:, :].unsqueeze(1).to_broadcast([P, 2, T])
                    v.tensor_tensor(rot[:, 0], b, c2, ALU.mult)
                    step(v.tensor_tensor(rot[:, 1], b, s2, ALU.mult))
                    v.tensor_tensor(dst[:, 2 * h, :], rot[:, 0, 0, :], rot[:, 1, 1, :], ALU.subtract)
                    v.tensor_tensor(dst[:, 2 * h + 1, :], rot[:, 1, 0, :], rot[:, 0, 1, :], ALU.add
                                    ).then_inc(emptied["D"], 1)
                    dve.wait_ge(emptied["D"], emptied_by(BANK_AT[name, h])[1])
            for n in range(16, 32):
                modulation(1, n)

            def ret_decay(h):
                if h == 0:
                    dve.wait_ge(small_loaded, 7 * 16)
                b = bank("ret_s", h)
                if h >= 2:
                    dve.wait_ge(bank_filled, BANK_AT["ret_o", 2 * (h - 2) + 1] + 1)
                v.tensor_tensor(dec_p[:, h % 2, 0:T], b[:, 0:T], decay[:, h, :], ALU.mult)
                v.tensor_tensor(dec_p[:, h % 2, T:3 * P], b[:, T:3 * P], decay[:, h, 0:P], ALU.mult
                                ).then_inc(emptied["D"], 1)

            ret_decay(0)
            dve.wait_ge(emptied["A"], emptied_by(BANK_AT["ret_g", 7])[1])
            for h in range(RH):
                if h + 1 < RH:
                    ret_decay(h + 1)
                b = [bank("ret_o", 2 * h + tt) for tt in range(NT)]
                for tt in range(NT):
                    last = v.bn_stats(stats[:, tt, 0, :], b[tt])
                step(last)
                for tt in range(NT):
                    last = v.bn_aggr(meanvar[:, tt, :], stats[:, tt, 0, :])
                step(last)
                ask_root(f"ret{h}", meanvar[:, :, 1], 1.0, RMS_EPS)
                r = root(f"ret{h}")
                for tt in range(NT):
                    v.tensor_scalar(half_rows[:, tt, :], b[tt], meanvar[:, tt, 0:1], r[:, tt:tt + 1],
                                    ALU.subtract, ALU.mult).then_inc(emptied["D"], 1)
                dve.wait_ge(emptied["D"], emptied_by(BANK_AT["ret_o", 2 * h + 1])[1])
                for tt in range(NT):
                    g = rg[:, tt, h * RHV:(h + 1) * RHV]
                    v.tensor_tensor(g, g, half_rows[:, tt, :], ALU.mult).then_inc(ret_u_ready, 1)
                dve.wait_ge(ret_u_ready, 2 * (h + 1))
            gated_residual("ret_y", half_rows)

            input_affine(1)
            gate_row(1)
            normalise("rms1", 2)
            dve.wait_ge(small_loaded, 7 * 16)
            dve.wait_ge(bf_loaded, 16)
            f = logf_t[:, 0, :]
            bfb = bf_row[:, :].unsqueeze(1).to_broadcast([P, NT, FH])
            v.tensor_tensor(f.rearrange("p (t h) -> p t h", t=NT),
                            bank("fox_f", 0)[:, 0:NT * FH].rearrange("p (t h) -> p t h", t=NT), bfb, ALU.add
                            ).then_inc(emptied["D"], 1)
            dve.wait_ge(emptied["D"], emptied_by(BANK_AT["fox_f", 0])[1])
            v.scalar_tensor_tensor(logf_t[:, 1, :], f, -1.0, f, ALU.mult, ALU.min).then_inc(logf_in, 1)
            step(v.tensor_tensor(qk_gain[:, :], gains[:, 0:1], gains[:, 1:2], ALU.mult))
            step(v.tensor_scalar(qk_gain[:, :], qk_gain[:, :], float(FD) ** -0.5, None, ALU.mult))

            def unit_heads(name, key, dst, s):
                for i in range(4):
                    n = 4 * s + i
                    b = bank(name, i)
                    tt, c = i % 2, i // 2
                    dve.wait_ge(fox_sq, n + 1)
                    v.tensor_reduce(head_sq[:, n % 2, :], fsq[:, n % 2, :].rearrange("p (h d) -> p h d", d=FD),
                                    AX.X, ALU.add).then_inc(fox_sq_used, 1)
                    dve.wait_ge(fox_sq_used, n + 1)
                    ask_root(f"{key}{i}", head_sq[:, n % 2, :], 1.0 / FD, RMS_EPS)
                    r = root(f"{key}{i}")[:, 0:8].unsqueeze(2).to_broadcast([P, 8, FD])
                    v.tensor_tensor(dst[:, tt, c * 512:(c + 1) * 512].rearrange("p (h d) -> p h d", d=FD),
                                    b.rearrange("p (h d) -> p h d", d=FD), r, ALU.mult).then_inc(emptied["D"], 1)
                    dve.wait_ge(emptied["D"], emptied_by(BANK_AT[name, i])[1])

            unit_heads("fox_q", "fq", fq_tok, 0)
            dve.wait_ge(logf_mid, 1)
            v.scalar_tensor_tensor(logf[:, :, :].rearrange("p t h -> p (t h)"), f, 0.0, logf_t[:, 1, :],
                                   ALU.min, ALU.subtract).then_inc(logf_ready, 1)
            unit_heads("fox_k", "fk", fk_tok, 1)
            b = bank("fox_cum", 0)
            v.tensor_copy(cum[:, :, :].rearrange("p t h -> p (t h)"), b[:, 0:NT * FH])
            v.tensor_scalar(ncumT[:, :], b[0:FH, P:3 * P], -1.0, None, ALU.mult).then_inc(emptied["D"], 1)
            for g in range(4):
                v.tensor_scalar(fqT[:, 2 * g:2 * g + 2, :], pairs(bank("fox_qT", g)), qk_gain[:, 0:1], None, ALU.mult
                                ).then_inc(emptied["D"], 1)
            for g in range(4):
                v.tensor_copy(fkT[:, 2 * g:2 * g + 2, :], pairs(bank("fox_kT", g))).then_inc(emptied["D"], 1)

            for i in range(FH + 2):
                if i < FH:
                    b = bank("fox_s", i)
                    if i == 0:
                        dve.wait_ge(emptied["D"], emptied_by(BANK_AT["fox_kT", 3])[1])
                    if i >= 2:
                        dve.wait_ge(probs_exp, i - 1)
                    j = i % 2
                    v.scalar_tensor_tensor(logits[:, j, 0:P], b[:, 0:P], cum[:, 0, i:i + 1],
                                           const[:, C_MASK:C_MASK + P], ALU.add, ALU.add)
                    v.scalar_tensor_tensor(logits[:, j, P:3 * P], b[:, P:3 * P], cum[:, 1, i:i + 1],
                                           const[:, C_MASK + P:C_MASK + 3 * P], ALU.add, ALU.add
                                           ).then_inc(emptied["D"], 1)
                    dve.wait_ge(emptied["D"], emptied_by(BANK_AT["fox_s", i])[1])
                    v.tensor_reduce(mx[:, j, 0:1], logits[:, j, 0:P], AX.X, ALU.max, negate=True)
                    v.tensor_reduce(mx[:, j, 1:2], logits[:, j, P:3 * P], AX.X, ALU.max, negate=True
                                    ).then_inc(logits_ready, 1)
                if 1 <= i <= FH:
                    h, j = i - 1, (i - 1) % 2
                    dve.wait_ge(probs_exp, h + 1)
                    step(v.reciprocal(rinv[:, j, :], rsum[:, j, :]))
                    v.tensor_scalar(prob[:, j, 0:P], prob[:, j, 0:P], rinv[:, j, 0:1], None, ALU.mult)
                    v.tensor_scalar(prob[:, j, P:3 * P], prob[:, j, P:3 * P], rinv[:, j, 1:2], None, ALU.mult
                                    ).then_inc(probs_ready, 1)
                if i >= 3 and i % 2 == 1:
                    g = (i - 3) // 2
                    v.tensor_tensor(fuT[:, g, :], bank("fox_o", g)[:, 0:T], fgT[:, g, :], ALU.mult
                                    ).then_inc(emptied["D"], 1)
            gated_residual("fox_y", half_rows)

            dve.wait_ge(sumsq_ready, 3)
            ask_root("final", sumsq[:, :], 1.0, RMS_EPS)
            r = root("final")
            dve.wait_ge(final_loaded, 16)
            for tt in range(NT):
                last = v.scalar_tensor_tensor(x[:, tt, :], x[:, tt, :], r[:, tt:tt + 1], final_row, ALU.mult, ALU.mult)
            last.then_inc(x_ready, 1)

            step(v.memset(u_pad[:, :, 0:TAPS - 1], 0.0))
            step(v.tensor_scalar(vec[:, :, V_DW:V_DW + TAPS], vec[:, :, V_DW:V_DW + TAPS], 0.5, None, ALU.mult))
            for i in range(KB):
                b = bank("conf", i)
                dve.wait_ge(half_ready, i + 1)
                v.scalar_tensor_tensor(u_pad[:, i, TAPS - 1:], half_gate[:, i % 2, :], 1.0, b[:, 0:T],
                                       ALU.add, ALU.mult).then_inc(emptied["D"], 1)
                dve.wait_ge(emptied["D"], emptied_by(BANK_AT["conf", i])[1])
                step(v.tensor_scalar(conv[:, i, :], u_pad[:, i, 0:T], vec[:, i, V_DW:V_DW + 1],
                                     vec[:, i, V_CB:V_CB + 1], ALU.mult, ALU.add))
                for k in range(1, TAPS):
                    ins = v.scalar_tensor_tensor(conv[:, i, :], u_pad[:, i, k:k + T], vec[:, i, V_DW + k:V_DW + k + 1],
                                                 conv[:, i, :], ALU.mult, ALU.add)
                    if k < TAPS - 1:
                        step(ins)
                    else:
                        ins.then_inc(conv_ready, 1)
            for tt in range(NT):
                for half in range(2):
                    last = v.bn_stats(stats[:, tt, half, :], bank("conf_cT", 2 * tt + half))
            step(last)
            for tt in range(NT):
                last = v.bn_aggr(meanvar[:, tt, :], stats[:, tt, :, :].rearrange("p a b -> p (a b)"))
            step(last)
            ask_root("conf", meanvar[:, :, 1], 1.0, LN_EPS)
            r = root("conf")
            for tt in range(NT):
                for half in range(2):
                    v.tensor_scalar(conf_n[:, tt, half * 512:(half + 1) * 512], bank("conf_cT", 2 * tt + half),
                                    meanvar[:, tt, 0:1], r[:, tt:tt + 1], ALU.subtract, ALU.mult
                                    ).then_inc(emptied["D"], 1)

            def layer_norm(name, n, y, done, g_row=rows_gb[:, 0, :], b_row=rows_gb[:, 1, :]):
                for tt in range(NT):
                    for half in range(2):
                        hs = slice(half * 512, (half + 1) * 512)
                        src, tell = y(tt, half)
                        ins = v.scalar_tensor_tensor(z[:, tt, hs], x[:, tt, hs], ALPHA, src, ALU.mult, ALU.add)
                        if tell is None:
                            step(ins)
                        else:
                            ins.then_inc(tell[0], 1)
                            dve.wait_ge(tell[0], tell[1])
                        last = v.bn_stats(stats[:, tt, half, :], z[:, tt, hs])
                step(last)
                for tt in range(NT):
                    last = v.bn_aggr(meanvar[:, tt, :], stats[:, tt, :, :].rearrange("p a b -> p (a b)"))
                step(last)
                ask_root(name, meanvar[:, :, 1], 1.0, LN_EPS)
                r = root(name)
                for tt in range(NT):
                    step(v.tensor_scalar(z[:, tt, :], z[:, tt, :], meanvar[:, tt, 0:1], r[:, tt:tt + 1],
                                         ALU.subtract, ALU.mult))
                dve.wait_ge(rows_loaded, 32 * n)
                for tt in range(NT):
                    step(v.tensor_tensor(z[:, tt, :], z[:, tt, :], g_row, ALU.mult))
                for tt in range(NT):
                    last = v.tensor_tensor(x[:, tt, :], z[:, tt, :], b_row, ALU.add)
                last.then_inc(done, 1)

            def from_banks(name):
                def y(tt, half):
                    i = 2 * tt + half
                    return bank(name, i), (emptied["D"], emptied_by(BANK_AT[name, i])[1])
                return y

            layer_norm("mix0", 1, from_banks("conf_y"), x_ready)

            for i in range(FB):
                b = bank("ffn", i)
                dve.wait_ge(silu_ready, i + 1)
                v.tensor_tensor(ffn_h[:, i, :], ffn_s[:, i % 2, :], b[:, T:2 * T], ALU.mult).then_inc(emptied["D"], 1)
            layer_norm("ffn0", 2, from_banks("ffn_y"), x_ready)

            step(v.memset(ch[:, :, 0:STAPS - 1], 0.0))
            for i in range(KB):
                j = i % 2
                b = bank("sc_ch", i)
                dve.wait_ge(c_copied, i + 1)
                v.tensor_tensor(ch[:, j, STAPS - 1:], sc_c[:, j, :], b[:, T:2 * T], ALU.mult).then_inc(emptied["D"], 1)
                dve.wait_ge(emptied["D"], emptied_by(BANK_AT["sc_ch", i])[1])
                step(v.tensor_scalar(sc_t, ch[:, j, 0:T], vec[:, i, V_SC:V_SC + 1], None, ALU.mult))
                for k in range(1, STAPS):
                    step(v.scalar_tensor_tensor(sc_t, ch[:, j, k:k + T], vec[:, i, V_SC + k:V_SC + k + 1], sc_t,
                                                ALU.mult, ALU.add))
                v.tensor_tensor(sc_uT[:, i, :], sc_t, bank("sc_b", i)[:, 0:T], ALU.mult).then_inc(emptied["D"], 1)
                dve.wait_ge(emptied["D"], emptied_by(BANK_AT["sc_b", i])[1])
            layer_norm("mix1", 3, from_banks("sc_y"), x_ready)

            LG, M, E, C, OH1, LG2, OH2, G1, G2, CH, DIF, EX = range(12)
            row8 = desc.unsqueeze(1).to_broadcast([P, NT, NE])

            def one(i):
                return rt[:, i, :, 0:1]

            def wide(i):
                return rt[:, i, :, 0:1].to_broadcast([P, NT, NE])

            step(v.memset(rt[:, :, :, :], 0.0))
            v.tensor_copy(rt[:, LG].rearrange("p t e -> p (t e)"), bank("route", 0)[:, 0:NT * NE]
                          ).then_inc(emptied["D"], 1)
            dve.wait_ge(emptied["D"], emptied_by(BANK_AT["route", 0])[1])
            for src, top, hot in ((LG, M, OH1), (LG2, E, OH2)):
                if src == LG2:
                    step(v.scalar_tensor_tensor(rt[:, LG2], rt[:, OH1], -3e38, rt[:, LG], ALU.mult, ALU.add))
                step(v.tensor_reduce(rt[:, top, :, 0], rt[:, src], AX.X, ALU.max))
                step(v.tensor_tensor(rt[:, C], rt[:, src], wide(top), ALU.is_equal))
                step(v.tensor_tensor(rt[:, C], rt[:, C], row8, ALU.mult))
                step(v.tensor_reduce(rt[:, 12, :, 0], rt[:, C], AX.X, ALU.max))
                step(v.tensor_tensor(rt[:, hot], row8, wide(12), ALU.is_equal))
            v.tensor_tensor(rt[:, CH], rt[:, OH1], rt[:, OH2], ALU.add).then_inc(mask_ready, 1)
            v.tensor_tensor(rt[:, DIF, :, 0], rt[:, E, :, 0], rt[:, M, :, 0], ALU.subtract).then_inc(lg_ready, 1)
            dve.wait_ge(lg_exp, 1)
            step(v.tensor_scalar(rt[:, 13, :, 0], rt[:, EX, :, 0], 1.0, None, ALU.add))
            step(v.reciprocal(rt[:, G1, :, 0], rt[:, 13, :, 0]))
            step(v.tensor_tensor(rt[:, G2, :, 0], rt[:, G1, :, 0], rt[:, EX, :, 0], ALU.mult))
            step(v.tensor_tensor(rt[:, C], rt[:, OH1], wide(G1), ALU.mult))
            step(v.tensor_tensor(rt[:, LG2], rt[:, OH2], wide(G2), ALU.mult))
            step(v.tensor_tensor(gate_of[:, :, :].rearrange("p e t -> p t e"), rt[:, C], rt[:, LG2], ALU.add))
            b = bank("rank", 0)
            step(v.scalar_tensor_tensor(rt[:, C], b[:, 0:NT * NE].rearrange("p (t e) -> p t e", t=NT), 1.0,
                                        rt[:, CH], ALU.add, ALU.mult))
            v.tensor_scalar(slot_of[:, :, :].rearrange("p e t -> p t e"), rt[:, C], -1.0, None, ALU.add
                            ).then_inc(wide_emptied, 1)
            for q in range(4):
                v.memset(e_acc[:, q // 2, (q % 2) * 512:(q % 2 + 1) * 512], 0.0).then_inc(gu_emptied, 1)
            v.tensor_copy(counts[0:1, :], b[0:1, 2 * NE:3 * NE]).then_inc(emptied["D"], 1)
            dve.wait_ge(emptied["D"], ALL_EMPTIED["D"])

            def expert(e, width):
                rows_n, tiles = min(width, P), -(-width // P)
                for tt in range(NT):
                    last = v.tensor_scalar(e_sel[:, tt, 0:width], const[:, C_IOTA:C_IOTA + width],
                                           slot_of[:, bass.ds(e, 1), tt], None, ALU.is_equal)
                last.then_inc(sel_ready, 1)
                dve.wait_ge(wide_filled, e * 4 + 1)
                v.tensor_copy(e_x[:, :, 0:width],
                              psum[:, 0:4, :].rearrange("p b (j n) -> p (b j) n", j=2)[:, :, 0:width]
                              ).then_inc(wide_emptied, 1)
                for n in range(EB):
                    dve.wait_ge(e_silu, e * EB + n + 1)
                    v.tensor_tensor(e_h[:, n, 0:width], e_s[:, n % 2, 0:width], psum[:, 4 + n % 4, 256:256 + width],
                                    ALU.mult).then_inc(gu_emptied, 1)
                dve.wait_ge(wide_filled, e * 4 + 2)
                v.tensor_copy(e_selT[0:rows_n, 0:tiles, :],
                              psum[0:rows_n, 0, 0:tiles * 256].rearrange("p (j n) -> p j n", j=tiles)
                              ).then_inc(wide_emptied, 1)
                dve.wait_ge(wide_filled, e * 4 + 3)
                v.tensor_copy(e_y[0:rows_n, 0:tiles, :].rearrange("p j n -> p (j n)"),
                              psum[0:rows_n, 0:2 * tiles, :].rearrange("p b n -> p (b n)")).then_inc(wide_emptied, 1)
                dve.wait_ge(wide_emptied, e * 4 + 4)
                dve.wait_ge(wide_filled, e * 4 + 4)
                for tt in range(NT):
                    last = v.scalar_tensor_tensor(e_acc[:, tt, :], psum[:, 2 * tt:2 * tt + 2, :].rearrange("p b n -> p (b n)"),
                                                  gate_of[:, bass.ds(e, 1), tt], e_acc[:, tt, :], ALU.mult, ALU.add)
                last.then_inc(wide_emptied, 1)

            with dve.Fori(0, NE) as e:
                by_width(dve, e, expert)
            dve.wait_ge(wide_emptied, 4 * NE + 1)

            layer_norm("out", 4, lambda tt, half: (e_acc[:, tt, half * 512:(half + 1) * 512], None), x_ready, out_g, out_b)
    return nc


_INS = ['x', 'c', 'positions', 'mod_w', 'mod_b', 'norm_g', 'ret_w_in', 'ret_w_out', 'fox_w_in', 'fox_b_f',
        'fox_q_gain', 'fox_k_gain', 'fox_w_out', 'final_g', 'ln_mix_g_2', 'ln_mix_b_2', 'ln_ffn_g_2',
        'ln_ffn_b_2', 'conf_w_in_2', 'conf_w_dw_2', 'conf_b_dw_2', 'conf_ln_g_2', 'conf_ln_b_2', 'conf_w_out_2',
        'sc_w_in_2', 'sc_w_conv_2', 'sc_w_out_2', 'ffn_w_gate_2', 'ffn_w_up_2', 'ffn_w_down_2',
        'moe_w_router_2', 'moe_w_gate_2', 'moe_w_up_2', 'moe_w_down_2']


def kernel(**inputs):
    import concourse.bacc as bacc
    from concourse.bass_utils import run_bass_kernel_spmd

    nc = bacc.Bacc("TRN2", target_bir_lowering=False, num_devices=1)
    arrays, views = {}, {}
    const, decay = shape_constants()
    given = {name: np.ascontiguousarray(inputs[name]) for name in _INS}
    given["final_g"] = given["final_g"].reshape(1, D)
    given["const"], given["decay"] = const, decay
    for name, a in given.items():
        arrays[f"in_{name}"] = a
        views[name] = nc.dram_tensor(f"in_{name}", a.shape, mybir.dt.from_np(a.dtype), kind="ExternalInput").ap()
    out = nc.dram_tensor("out", (1, T, D), F32, kind="ExternalOutput").ap()
    build(nc, views, out)
    r = run_bass_kernel_spmd(nc, [arrays], core_ids=[0])
    return r.results[0]["out"]
```

```python
from contextlib import ExitStack

import numpy as np

import concourse.bass as bass
from concourse import mybir

F32 = mybir.dt.float32
I32 = mybir.dt.int32
ACT = mybir.ActivationFunctionType
ALU = mybir.AluOpType
AX = mybir.AxisListType

P = 128
D = 1024
KB = D // P
T = 256
NT = T // P
CHUNK = 64
RH, RHK, RHV = 4, 256, 512
RV = RH * RHV
FH, FD = 16, 64
DFF = 2816
FB = DFF // P
NE = 8
EF = 3584
EB = EF // P
TAPS = 31
GATHER_AFTER = 7
CONV_BY_VECTOR = 5
DIAGS = 22
STAPS = 3
RMS_EPS = 1e-6
LN_EPS = 1e-5
ALPHA = float((2.0 * 2) ** 0.25)
BIG = 1e30

RING = 3
UNITS = 4
MOD_BUFS = 5
COLS = 512
ROWS = 4
PAIRS = EF // COLS
DOWNS = EB // ROWS
PER_EXPERT = 2 * PAIRS + DOWNS
assert PER_EXPERT % RING == 0 and 2 * PER_EXPERT % UNITS != 1

V_C, V_NORM, V_CB, V_CG, V_CBETA, V_SC = 0, 1, 3, 4, 5, 6
V_DW = V_SC + STAPS
NVEC = V_DW + TAPS
REGION = 15360

C_IDENT, C_TRI, C_ONES = 0, 128, 256
C_MASK = 384
C_IOTA = C_MASK + 256
C_DESC = C_IOTA + P
C_INV = C_DESC + 8
C_END = C_INV + 1


def shape_constants():
    i = np.arange(P)
    c = np.zeros((P, C_END), np.float32)
    c[:, C_IDENT:C_IDENT + P] = np.eye(P)
    c[:, C_TRI:C_TRI + P] = i[:, None] <= i[None, :]
    c[:, C_ONES:C_ONES + P] = 1.0
    c[:, C_MASK + P:C_MASK + 2 * P] = np.where(i[:, None] >= i[None, :], 0.0, -BIG)
    c[:, C_IOTA:C_IOTA + P] = i[None, :]
    c[:, C_DESC:C_DESC + 8] = 8 - np.arange(8)[None, :]
    half = RHK // 2
    exponent = -np.arange(half, dtype=np.float32) / np.float32(half)
    c[:, C_INV] = (10000.0 ** exponent.astype(np.float64)).astype(np.float32)
    lg = np.log1p(-np.exp2(-5.0 - np.arange(RH)))
    m, t = i[:, None], i[None, :]
    seen = (m // CHUNK == t // CHUNK) | (m < t)
    d = np.zeros((P, RH, 2, P), np.float32)
    for h in range(RH):
        d[:, h, 0] = np.where(seen, np.exp(lg[h] * abs(t - m)), 0.0) * RHK ** -0.5
        d[:, h, 1] = np.exp(lg[h] * (P + t - m)) * RHK ** -0.5
    return c, d.reshape(P, RH * 2 * P)


def weight_plan():
    plan = [("ret_q", 0), ("ret_q", 1), ("ret_k", 0), ("ret_k", 1)]
    plan += [("ret_v", i) for i in range(4)] + [("ret_g", i) for i in range(4)]
    plan += [("ret_out", i) for i in range(4)]
    plan += [(n, i) for n in ("fox_q", "fox_k", "fox_v", "fox_g") for i in range(2)]
    plan += [("fox_out", i) for i in range(2)]
    plan += [(n, i) for i in range(2) for n in ("conf_g", "conf_a")]
    plan += [("conf_out", i) for i in range(2)]
    plan += [(n, i) for i in range(6) for n in ("ffn_gate", "ffn_up")]
    plan += [("ffn_down", i) for i in range(6)]
    plan += [(n, i) for i in range(2) for n in ("sc_c", "sc_h", "sc_b")]
    plan += [("sc_out", i) for i in range(2)]
    return plan


PLAN = weight_plan()
CHUNK_AT = {key: n for n, key in enumerate(PLAN)}
PRE = len(PLAN)
SWEEP = NE * PER_EXPERT
assert PRE % 2 == 0 and SWEEP % 2 == 0 and SWEEP % RING == 0


def bank_plan():
    g = [("vecs", 0, "D"), ("mod_cols", 0, "D")] + [("x0T", i, "S") for i in range(4)]
    g += [("mod_gate", i, "D") for i in range(2)]
    g += [("ret_q", i, "D") for i in range(RH)] + [("ret_k", i, "D") for i in range(RH)]
    g += [("ret_v", i, "A") for i in range(8)] + [("ret_g", i, "A") for i in range(6)]
    g += [("mod_cols", 1, "D")] + [("ret_g", i, "A") for i in range(6, 8)]
    g += [("ret_s", 0, "D")]
    for h in range(RH):
        if h + 1 < RH:
            g += [("ret_s", h + 1, "D")]
        g += [("ret_o", 2 * h, "D"), ("ret_o", 2 * h + 1, "D")]
    g += [("ret_uT", i, "S") for i in range(8)]
    g += [("ret_y", i, "D") for i in range(4)]
    g += [("mod_gate", 2 + i, "D") for i in range(2)]
    g += [("x1T", i, "S") for i in range(4)]
    g += [("fox_f", 0, "D")]
    g += [("fox_q", i, "D") for i in range(4)] + [("fox_k", i, "D") for i in range(4)]
    g += [("fox_v", i, "A") for i in range(4)] + [("fox_g", i, "A") for i in range(4)]
    g += [("fox_cum", 0, "D")]
    g += [("fox_qT", i, "D") for i in range(4)] + [("fox_kT", i, "D") for i in range(4)]
    for i in range(FH + 3):
        if i < FH:
            g += [("fox_s", i, "D")]
        if 2 <= i < FH + 2:
            g += [("fox_pT", i - 2, "A")]
        if i >= 4 and i % 2 == 0:
            g += [("fox_o", (i - 4) // 2, "D")]
    g += [("fox_y", i, "D") for i in range(4)]
    g += [("x2T", i, "S") for i in range(4)]
    for c in range(2):
        g += [("conf_g", 2 * c + i, "A") for i in range(2)] + [("conf_a", 2 * c + i, "D") for i in range(2)]
    g += [("conf_taps", i, "A") for i in range(CONV_BY_VECTOR, KB)]
    g += [("conf_cT", i, "D") for i in range(4)] + [("conf_nT", i, "A") for i in range(4)]
    g += [("conf_y", i, "D") for i in range(4)]
    g += [("x3T", i, "S") for i in range(4)]
    for c in range(6):
        n = min(2, FB // 2 - 2 * c)
        g += [("ffn_gate", 2 * c + i, "A") for i in range(n)] + [("ffn_up", 2 * c + i, "D") for i in range(n)]
    g += [("ffn_y", i, "D") for i in range(4)]
    g += [("x4T", i, "S") for i in range(4)]
    for c in range(2):
        g += [("sc_c", 2 * c + i, "A") for i in range(2)] + [("sc_h", 2 * c + i, "D") for i in range(2)]
        g += [("sc_b", 2 * c + i, "D") for i in range(2)]
    g += [("sc_y", i, "D") for i in range(4)]
    g += [("x5T", i, "A") for i in range(4)]
    g += [("route", 0, "D"), ("rank", 0, "D")]
    return g


OUT_BANKS = {"ret_out": "ret_y", "fox_out": "fox_y", "conf_out": "conf_y", "ffn_down": "ffn_y", "sc_out": "sc_y"}
TOKEN_MAJOR = ("ret_v", "ret_g", "fox_q", "fox_k", "fox_v")

BANKS = bank_plan()
BANK_AT = {(name, i): n for n, (name, i, _) in enumerate(BANKS)}
NBANK = 8


EMPTIER = {"A": "A", "D": "D", "S": "D"}


def emptied_by(n):
    who = EMPTIER[BANKS[n][2]]
    return who, sum(EMPTIER[b[2]] == who for b in BANKS[:n + 1])


def high_count(n):
    return sum(b[2] == "S" for b in BANKS[:n + 1])


ALL_EMPTIED = {who: sum(EMPTIER[b[2]] == who for b in BANKS) for who in "AD"}


def mod_steps(n):
    return range(2 * n, 2 * n + 2) if n < KB else range(0)


def unit_counted(u):
    name, i = PLAN[u // 2]
    if name in OUT_BANKS:
        return (name, i + 1) in CHUNK_AT or (u % 2 == 0 and (name, i) != ("ffn_down", FB // ROWS))
    return name in TOKEN_MAJOR and u % 2 == 0


EXPERT_UNITS_COUNTED = 2 * PAIRS + 2 * DOWNS - 1
PRE_UNITS_COUNTED = sum(unit_counted(u) for u in range(2 * PRE))


def unit_bank(u):
    name, i = PLAN[u // 2]
    if name in OUT_BANKS:
        return BANK_AT[OUT_BANKS[name], 3]
    return BANK_AT[name, min(2 * i + 1, FB // 2 - 1) if name.startswith("ffn") else 2 * i + 1]


ROOTS = (["rms0"] + [f"ret{h}" for h in range(RH)] + ["rms1"] + [f"fq{i}" for i in range(4)]
         + [f"fk{i}" for i in range(4)] + ["final", "conf", "mix0", "ffn0", "mix1", "out"])
ROOT_WIDTH = {**{f"fq{i}": 8 for i in range(4)}, **{f"fk{i}": 8 for i in range(4)}}


def build(nc, t, out):
    ctx = ExitStack()
    with ctx:
        def sb(name, shape, dt=F32):
            return ctx.enter_context(nc.sbuf_tensor(name, shape, dt))

        def sem(name):
            return ctx.enter_context(nc.semaphore(name))

        ring = sb("ring", [P, RING, ROWS * D])
        F32R = mybir.dt.float32r
        units_at = nc.sbuf_base
        units = sb("units", [P, UNITS, 2, ROWS * D // 2], F32R)
        mod_first = nc.alloc_sbuf_tensor_at("mod_first", [P, MOD_BUFS, 3 * D], F32, offset=units_at)
        x = sb("x", [P, NT, D])
        xr_at = nc.sbuf_base
        xr = sb("xr", [P, 2, KB, T], F32R)
        X = nc.alloc_sbuf_tensor_at("X", [P, D], F32, offset=xr_at)
        region_at = nc.sbuf_base
        R = nc.alloc_sbuf_tensor_at("R", [P, REGION], F32, offset=region_at)
        H = nc.alloc_sbuf_tensor_at("H", [P, 2 * FB * T], F32R, offset=region_at)
        fence = sb("fence", [P, REGION])
        const = sb("const", [P, C_END])
        vec = sb("vec", [P, KB, NVEC])
        c_act = sb("c_act", [P, KB])
        in_scale = sb("in_scale", [P, KB])
        in_shift = sb("in_shift", [P, KB])
        wf_r = sb("wf_r", [P, KB, 2 * FH], F32R)
        w_router = sb("w_router", [P, KB, NE])
        gains = sb("gains", [P, 2])
        qk_gain = sb("qk_gain", [P, 1])
        bf_row = sb("bf_row", [P, FH])
        logf = sb("logf", [P, NT, FH])
        logf_t = sb("logf_t", [P, 2, NT * FH])
        cum = sb("cum", [P, NT, FH])
        mx = sb("mx", [P, 2, 2])
        rsum = sb("rsum", [P, 2, 2])
        rinv = sb("rinv", [P, 2, 2])
        sumsq = sb("sumsq", [P, NT])
        head_sq = sb("head_sq", [P, 2, 8])
        root_in = sb("root_in", [P, 2, 8])
        root_out = sb("root_out", [P, 2, 8])
        neg_half = sb("neg_half", [P, 8])
        stats = sb("stats", [P, NT, 2, 6])
        meanvar = sb("meanvar", [P, NT, 2])
        slot_of = sb("slot_of", [P, NE + 1, NT])
        gate_of = sb("gate_of", [P, NE, NT])
        gate = sb("gate", [P, D])
        over = sb("over", [1, 1], I32)
        big = sb("big", [1, 2])

        psum = ctx.enter_context(nc.psum_tensor("psum", [P, NBANK, 512], F32))

        def region(at, *shape):
            n = int(np.prod(shape))
            v = R[:, at:at + n]
            if len(shape) == 2:
                return v.rearrange("p (a b) -> p a b", a=shape[0])
            if len(shape) == 3:
                return v.rearrange("p (a b c) -> p a b c", a=shape[0], b=shape[1])
            return v

        ident = const[:, C_IDENT:C_IDENT + P]
        tri = const[:, C_TRI:C_TRI + P]
        ones = const[:, C_ONES:C_ONES + P]
        desc = const[:, C_DESC:C_DESC + NE]

        def split_region(at, *shape):
            n = int(np.prod(shape))
            return [H[:, at + i * n:at + (i + 1) * n].rearrange("p (a b) -> p a b", a=shape[0]) for i in range(2)]

        xn = region(0, NT, D)
        rq, rk = region(0, KB, T), region(2048, KB, T)
        rv, rg = region(4096, NT, RV), region(8192, NT, RV)
        ang = region(4096, 6, T)
        cos, sin = region(5632, T), region(5888, T)
        pos_i = region(6144, T).bitcast(I32)
        vec_rows = R[0:NVEC, 6400:6400 + D]
        affine_t = region(6400, 4, T)
        mod_w = region(8192, 2, 1536)
        rot = R[:, 11264:12288].rearrange("p (a b c) -> p a b c", a=2, b=2)
        acc = region(12288, 3 * D)
        decay = region(12288, RH, T)
        dec_p = region(13312, 2, 3 * P)
        half_rows = X[:, :].rearrange("p (a b) -> p a b", a=2)
        ruT = split_region(0, RV // P, T)
        y_tmp = region(8192, 2, 512)
        wf = region(7424, KB, FH)
        ncumT = X[0:FH, 0:T]
        xn1 = region(8192, NT, D)
        fq_tok, fk_tok = region(0, NT, D), region(2048, NT, D)
        fv, fgT = region(4096, NT, D), region(6144, KB, T)
        fqT, fkT = region(8192, KB, T), region(10240, KB, T)
        fuT = split_region(0, KB, T)
        fsq = region(12288, 2, 512)
        logits = region(12288, 2, 384)
        prob = region(13056, 2, 384)
        probT = region(13824, 4, 384)
        u_pad = region(0, KB, TAPS - 1 + T)
        conv = region(2288, KB, T)
        conf_n = region(4336, NT, D)
        conf_uT = split_region(0, KB, T)
        half_gate = region(6400, 2, 4, T)
        conf_t = region(6400, 2, 2 * T)
        diags = region(8448, DIAGS, P)
        rows_gb = region(11264, 2, D)
        final_row = region(14336, D)
        ffn_h = split_region(0, FB, T)
        ffn_s = region(11264, 2, 4, T)
        ffn_t = region(13312, 2, 2 * T)
        sc_c = region(4096, 2, 4, T)
        ch = region(6144, KB, STAPS - 1 + T)
        sc_t = region(10240, 4, T)
        sc_uT = split_region(0, KB, T)
        x5T = region(4096, KB, T)
        rt = R[:, 10496:10496 + 14 * NT * NE].rearrange("p (i t e) -> p i t e", i=14, t=NT)
        e_x = [[xr[:, i].rearrange("p k t -> p (k t)")[:, q * D:(q + 1) * D].rearrange("p (k t) -> p k t", k=KB)
                for i in range(2)] for q in range(2)]
        e_h = split_region(0, EB, P)
        e_acc = region(7168, NT, D)
        e_y = region(9216, D)
        e_sel = [region(10240 + q * NT * P, NT, P) for q in range(2)]
        e_selT = region(10752, NT * P)
        e_ht = region(11264, 2, 512)
        e_s = region(12288, 2, 512)
        out_g = gate[:, :]
        out_b = region(13312, D)

        slot_filled = [sem(f"slot_filled{s}") for s in range(RING)]
        weights_used = sem("weights_used")
        first_filled = [sem(f"mod_first_filled{b}") for b in range(MOD_BUFS)]
        first_used = sem("mod_first_used")
        mod_filled = [sem("mod_filled0"), sem("mod_filled1")]
        mod_used = sem("mod_used")
        acc_seeded = sem("acc_seeded")
        x_loaded = sem("x_loaded")
        vec_loaded = sem("vec_loaded")
        const_loaded = sem("const_loaded")
        small_loaded = sem("small_loaded")
        bf_loaded = sem("bf_loaded")
        pos_loaded = sem("pos_loaded")
        rows_loaded = sem("rows_loaded")
        final_loaded = sem("final_loaded")
        decay_loaded = sem("decay_loaded")
        bank_filled = sem("bank_filled")
        unit_high = sem("unit_high")
        unit_ready = sem("unit_ready")
        bank_high = sem("bank_high")
        wf_ready = sem("wf_ready")
        conf_high = sem("conf_high")
        conf_low = sem("conf_low")
        ffn_low = sem("ffn_low")
        sc_low = sem("sc_low")
        over_done = sem("over_done")
        emptied = {"A": sem("bank_emptied_by_scalar"), "D": sem("bank_emptied_by_vector")}
        c_ready = sem("c_ready")
        acc_clear = sem("acc_clear")
        sumsq_ready = sem("sumsq_ready")
        root_asked = sem("root_asked")
        root_ready = sem("root_ready")
        xn_ready = sem("xn_ready")
        ang_ready = sem("ang_ready")
        trig_ready = sem("trig_ready")
        ret_u_ready = sem("ret_u_ready")
        x_ready = sem("x_ready")
        fox_sq = sem("fox_sq")
        fox_sq_used = sem("fox_sq_used")
        logf_in = sem("logf_in")
        logf_mid = sem("logf_mid")
        logf_ready = sem("logf_ready")
        logits_ready = sem("logits_ready")
        probs_exp = sem("probs_exp")
        probs_ready = sem("probs_ready")
        half_ready = sem("half_ready")
        conv_ready = sem("conv_ready")
        taps_halved = sem("taps_halved")
        diag_ready = sem("diag_ready")
        diag_used = sem("diag_used")
        lg_ready = sem("lg_ready")
        lg_exp = sem("lg_exp")
        mask_ready = sem("mask_ready")
        sel_ready = sem("sel_ready")
        gather_filled = sem("gather_filled")
        gather_high = sem("gather_high")
        gather_emptied = sem("gather_emptied")
        down_filled = sem("down_filled")
        down_emptied = sem("down_emptied")
        scatter_filled = sem("scatter_filled")
        scatter_emptied = sem("scatter_emptied")
        gu_filled = sem("gu_filled")
        gate_emptied = sem("gate_emptied")
        up_emptied = sem("up_emptied")
        turn_filled = sem("turn_filled")
        turn_high = sem("turn_high")
        turn_emptied = sem("turn_emptied")
        out_written = sem("out_written")
        vector_step = sem("vector_step")
        scalar_step = sem("scalar_step")
        gpsimd_step = sem("gpsimd_step")

        def cols(w, at, n=COLS):
            return w.rearrange("(k p) n -> p k n", p=P)[:, :, at:at + n]

        def rows(w, at, n=ROWS):
            return w.rearrange("(r p) n -> p r n", p=P)[:, at:at + n, :]

        w_ret, w_fox = t["ret_w_in"][0], t["fox_w_in"][0]
        w_conf, w_sc = t["conf_w_in_2"][0], t["sc_w_in_2"][0]
        COL_SOURCES = {
            "ret_q": (w_ret, 0), "ret_k": (w_ret, D), "ret_v": (w_ret, 2 * D), "ret_g": (w_ret, 2 * D + RV),
            "fox_q": (w_fox, 0), "fox_k": (w_fox, D), "fox_v": (w_fox, 2 * D), "fox_g": (w_fox, 3 * D),
            "conf_a": (w_conf, 0), "conf_g": (w_conf, D),
            "ffn_gate": (t["ffn_w_gate_2"][0], 0), "ffn_up": (t["ffn_w_up_2"][0], 0),
            "sc_b": (w_sc, 0), "sc_c": (w_sc, D), "sc_h": (w_sc, 2 * D)}
        ROW_SOURCES = {"ret_out": t["ret_w_out"][0], "fox_out": t["fox_w_out"][0],
                       "conf_out": t["conf_w_out_2"][0], "ffn_down": t["ffn_w_down_2"][0],
                       "sc_out": t["sc_w_out_2"][0]}

        def as_cols(flat, n):
            return flat.rearrange("p (k n) -> p k n", k=n)

        def as_rows(flat, n):
            return flat.rearrange("p (r n) -> p r n", r=n)

        def chunk_width(n):
            name, i = PLAN[n]
            return min(COLS, DFF - COLS * i) if name.startswith("ffn_") and name in COL_SOURCES else COLS

        def chunk_blocks(n):
            name, i = PLAN[n]
            return min(ROWS, ROW_SOURCES[name].shape[0] // P - ROWS * i)

        def pre_load(n):
            name, i = PLAN[n]
            s = n % RING
            if name in COL_SOURCES:
                w, at = COL_SOURCES[name]
                width = chunk_width(n)
                return as_cols(ring[:, s], KB)[:, :, 0:width], cols(w, at + COLS * i, width)
            blocks = chunk_blocks(n)
            return as_rows(ring[:, s], ROWS)[:, 0:blocks, :], rows(ROW_SOURCES[name], ROWS * i, blocks)

        def unit_parts(n, half):
            size = ROWS * D // 2
            src = ring[:, n % RING, half * size:(half + 1) * size]
            dst = [units[:, (2 * n + half) % UNITS, i, :] for i in range(2)]
            return src, dst

        def released(u):
            if unit_counted(u):
                return weights_used, sum(unit_counted(v) for v in range(u + 1))
            return bank_filled, unit_bank(u) + 1

        def used_units(n):
            if n >= PRE:
                return [(0, None), (1, None)]
            name, i = PLAN[n]
            if name in COL_SOURCES:
                w = chunk_width(n)
                narrow = None if w == COLS else (lambda a: as_cols(a, 4)[:, :, 0:w])
                return [(0, narrow), (1, narrow)]
            blocks = chunk_blocks(n)
            return [(h, None) for h in range(2)] if blocks > 2 else [(0, None)]

        def expert_unit_parts(q, j, half, part):
            size = ROWS * D // 2
            return (units[:, (2 * (PRE + q * PER_EXPERT + j) + half) % UNITS, part, :],
                    ring[:, (PRE + j) % RING, half * size:(half + 1) * size])

        def expert_unit_released(e, j, half):
            if j < 2 * PAIRS:
                if half == 0:
                    return weights_used, e * EXPERT_UNITS_COUNTED + PRE_UNITS_COUNTED + j + 1
                return gu_filled, e * (2 * PAIRS) + j + 1
            r = 2 * (j - 2 * PAIRS) + half
            if r < 2 * DOWNS - 1:
                return weights_used, e * EXPERT_UNITS_COUNTED + PRE_UNITS_COUNTED + 2 * PAIRS + r + 1
            return down_filled, e + 1

        def sweeps(eng, body, before=None):
            def sweep(number):
                with eng.Fori(number * NE, (number + 1) * NE - 2, 2) as pair:
                    for q in range(2):
                        body(pair + q, q, True, number)
                for q in range(2):
                    body((number + 1) * NE - 2 + q, q, q == 0, number)

            sweep(0)
            again = eng.value_load(over[0:1, 0:1], min_val=0, max_val=1)
            with eng.If(again > 0):
                if before is not None:
                    before()
                sweep(1)

        block = ctx.enter_context(nc.Block())

        @block.sync
        def _(sp):
            def load_mod(n):
                k, half = n // 2, n % 2
                if n >= 2:
                    sp.wait_ge(mod_used, n - 1)
                sp.dma_start(mod_w[:, n % 2, :], t["mod_w"][1, k * P:(k + 1) * P, half * 1536:(half + 1) * 1536]
                             ).then_inc(mod_filled[n % 2], 16)

            for lo, src in ((V_C, t["c"]), (V_NORM, t["norm_g"]), (V_CB, t["conf_b_dw_2"]),
                            (V_CG, t["conf_ln_g_2"]), (V_CBETA, t["conf_ln_b_2"]),
                            (V_SC, t["sc_w_conv_2"][0]), (V_DW, t["conf_w_dw_2"][0])):
                sp.dma_start(vec_rows[lo:lo + src.shape[0], :], src).then_inc(vec_loaded, 16)
            sp.dma_start(const[:, :], t["const"]).then_inc(const_loaded, 16)
            for k in range(KB):
                if k >= MOD_BUFS:
                    sp.wait_ge(first_used, k - MOD_BUFS + 1)
                sp.dma_start(mod_first[:, k % MOD_BUFS, :], t["mod_w"][0, k * P:(k + 1) * P, :]
                             ).then_inc(first_filled[k % MOD_BUFS], 16)
            for n in range(PRE):
                if n >= RING:
                    sp.wait_ge(unit_ready, 2 * (n - RING) + 2)
                dst, src = pre_load(n)
                sp.dma_start(dst, src).then_inc(slot_filled[n % RING], 16)
                if n >= 2:
                    for m in mod_steps(n - 2):
                        load_mod(m)

            def expert(e, q, more, number):
                for j in range(PER_EXPERT):
                    sp.wait_ge(unit_ready, e * (2 * PER_EXPERT) + 2 * (PRE + j - RING) + 2)
                    if j < 2 * PAIRS:
                        w = t["moe_w_gate_2"] if j % 2 == 0 else t["moe_w_up_2"]
                        src = w[0].rearrange("e (k p) n -> e p k n", p=P)[
                            bass.ds(e - number * NE, 1), :, :, (j // 2) * COLS:(j // 2 + 1) * COLS]
                        dst = as_cols(ring[:, (PRE + j) % RING], KB)
                    else:
                        r = (j - 2 * PAIRS) * ROWS
                        src = t["moe_w_down_2"][0].rearrange("e (r p) n -> e p r n", p=P)[
                            bass.ds(e - number * NE, 1), :, r:r + ROWS, :]
                        dst = as_rows(ring[:, (PRE + j) % RING], ROWS)
                    sp.dma_start(dst, src.rearrange("o p k n -> (o p) k n")).then_inc(slot_filled[(PRE + j) % RING], 16)

            sweeps(sp, expert)

            sp.wait_ge(x_ready, 5)
            sp.dma_start(out[0].rearrange("(t p) d -> p t d", p=P), x[:, :, :]).then_inc(out_written, 16)
            sp.wait_ge(out_written, 16)

        @block.tensor
        def _(pe):
            mm = nc.tensor.matmul

            def take_bank(name, i):
                n = BANK_AT[name, i]
                if n >= NBANK:
                    who, count = emptied_by(n - NBANK)
                    pe.wait_ge(emptied[who], count)
                return psum[:, n % NBANK, :]

            def wait_emptied(name, i):
                who, count = emptied_by(BANK_AT[name, i])
                pe.wait_ge(emptied[who], count)

            def unit(n, half, view):
                pe.wait_ge(unit_ready, 2 * n + half + 1)
                return [view(units[:, (2 * n + half) % UNITS, i, :]) for i in range(2)]

            def product(dst, left, right, first, last):
                mm(dst, left[0], right[0], start=first, stop=False)
                mm(dst, left[0], right[1], start=False, stop=False)
                return mm(dst, left[1], right[0], start=False, stop=last)

            def transpose_in(name, src, n=4):
                for g in range(n):
                    b = take_bank(name, g)
                    for j in range(2):
                        for tt in range(NT):
                            last = nc.tensor.transpose(b[:, j * T + tt * P:j * T + (tt + 1) * P],
                                                       src[:, tt, (2 * g + j) * P:(2 * g + j + 1) * P], ident)
                    last.then_inc(bank_filled, 1)

            def both(a, *index):
                return [a[:, i][index] for i in range(2)]

            def token_chunk(name, i):
                n = CHUNK_AT[name, i]
                banks = [take_bank(name, NT * i + tt) for tt in range(NT)]
                for half in range(2):
                    w = unit(n, half, lambda a: as_cols(a, 4))
                    for tt in range(NT):
                        for k in range(4):
                            kk = 4 * half + k
                            left = [xr[:, h, kk, tt * P:(tt + 1) * P] for h in range(2)]
                            last = product(banks[tt], left, [a[:, k, :] for a in w], kk == 0, kk == KB - 1)
                        if half == 1:
                            last.then_inc(bank_filled, 1)
                    if half == 0:
                        last.then_inc(weights_used, 1)

            def feature_chunk(name, i):
                n = CHUNK_AT[name, i]
                w = [unit(n, half, lambda a: as_cols(a, 4)) for half in range(2)]
                for g in range(chunk_width(n) // (2 * P)):
                    b = take_bank(name, 2 * i + g)
                    for j in range(2):
                        c = slice((2 * g + j) * P, (2 * g + j + 1) * P)
                        for k in range(KB):
                            last = product(b[:, j * T:(j + 1) * T], [a[:, k % 4, c] for a in w[k // 4]],
                                           [xr[:, h, k, :] for h in range(2)], k == 0, k == KB - 1)
                    last.then_inc(bank_filled, 1)

            def out_product(name, src, blocks):
                banks = [take_bank(OUT_BANKS[name], i) for i in range(4)]
                for k in range(blocks):
                    n, half = CHUNK_AT[name, k // ROWS], k % ROWS // 2
                    if k % 2 == 0:
                        w = unit(n, half, lambda a: as_rows(a, 2))
                    for tt in range(NT):
                        for c in range(2):
                            last = product(banks[2 * tt + c], [a[:, k, tt * P:(tt + 1) * P] for a in src],
                                           [a[:, k % 2, c * 512:(c + 1) * 512] for a in w], k == 0, k == blocks - 1)
                            if k == blocks - 1:
                                last.then_inc(bank_filled, 1)
                    if k % 2 == 1 and k < blocks - 1:
                        last.then_inc(weights_used, 1)

            pe.wait_ge(const_loaded, 16)
            pe.wait_ge(vec_loaded, 7 * 16)
            b = take_bank("vecs", 0)
            for k in range(KB):
                last = nc.tensor.transpose(b[:, k * NVEC:(k + 1) * NVEC], vec_rows[:, k * P:(k + 1) * P],
                                           ident[0:NVEC, 0:NVEC])
            last.then_inc(bank_filled, 1)

            def modulation_columns(i):
                if i == 0:
                    pe.wait_ge(first_used, KB)
                else:
                    pe.wait_ge(mod_used, 2 * KB)
                b = take_bank("mod_cols", i)
                for m in range(2 * KB):
                    last = mm(b[:, m:m + 1], acc[:, m * P:(m + 1) * P], ones[:, 0:1], start=True, stop=True)
                last.then_inc(bank_filled, 1)

            def modulation_gate(i):
                for half in range(2):
                    b = take_bank("mod_gate", 2 * i + half)
                    mm(b, ones, acc[:, 2 * D + half * 512:2 * D + (half + 1) * 512], start=True, stop=True
                       ).then_inc(bank_filled, 1)

            modulation_columns(0)
            pe.wait_ge(xn_ready, 1)
            transpose_in("x0T", xn)
            modulation_gate(0)
            wait_emptied("x0T", 3)
            for name in ("ret_q", "ret_k"):
                for c in range(2):
                    feature_chunk(name, c)
            for c in range(4):
                token_chunk("ret_v", c)
            for c in range(4):
                if c == 3:
                    modulation_columns(1)
                token_chunk("ret_g", c)

            def ret_scores(h):
                b = take_bank("ret_s", h)
                for d in range(2):
                    mm(b[:, 0:T], rk[:, 2 * h + d, 0:P], rq[:, 2 * h + d, :], start=(d == 0), stop=(d == 1))
                for d in range(2):
                    last = mm(b[:, T:T + P], rk[:, 2 * h + d, P:T], rq[:, 2 * h + d, P:T], start=(d == 0), stop=(d == 1))
                last.then_inc(bank_filled, 1)

            wait_emptied("ret_k", RH - 1)
            ret_scores(0)
            wait_emptied("ret_v", 7)
            for h in range(RH):
                if h + 1 < RH:
                    ret_scores(h + 1)
                wait_emptied("ret_s", h)
                p, cols_h = dec_p[:, h % 2, :], slice(h * RHV, (h + 1) * RHV)
                b = take_bank("ret_o", 2 * h)
                mm(b, p[:, 0:P], rv[:, 0, cols_h], start=True, stop=True).then_inc(bank_filled, 1)
                b = take_bank("ret_o", 2 * h + 1)
                mm(b, p[:, P:2 * P], rv[:, 0, cols_h], start=True, stop=False)
                mm(b, p[:, 2 * P:3 * P], rv[:, 1, cols_h], start=False, stop=True).then_inc(bank_filled, 1)
            for h in range(RH):
                pe.wait_ge(ret_u_ready, 2 * (h + 1))
                for g in range(2 * h, 2 * h + 2):
                    b = take_bank("ret_uT", g)
                    for j in range(2):
                        for tt in range(NT):
                            last = nc.tensor.transpose(b[:, j * T + tt * P:j * T + (tt + 1) * P],
                                                       rg[:, tt, (2 * g + j) * P:(2 * g + j + 1) * P], ident)
                    last.then_inc(bank_filled, 1)
            wait_emptied("ret_uT", 7)
            out_product("ret_out", ruT, RV // P)

            modulation_gate(1)
            pe.wait_ge(xn_ready, 2)
            transpose_in("x1T", xn1)
            wait_emptied("x1T", 3)
            b = take_bank("fox_f", 0)
            pe.wait_ge(wf_ready, 2)
            for tt in range(NT):
                for k in range(KB):
                    f = b[:, 2 * tt * FH:2 * (tt + 1) * FH]
                    mm(f, xr[:, 0, k, tt * P:(tt + 1) * P], wf_r[:, k, :], start=(k == 0), stop=False)
                    last = mm(f[:, 0:FH], xr[:, 1, k, tt * P:(tt + 1) * P], wf_r[:, k, 0:FH], start=False, stop=(k == KB - 1))
            last.then_inc(bank_filled, 1)
            for name in ("fox_q", "fox_k"):
                for c in range(2):
                    token_chunk(name, c)
            for c in range(2):
                token_chunk("fox_v", c)
            for c in range(2):
                feature_chunk("fox_g", c)
            pe.wait_ge(logf_ready, 1)
            b = take_bank("fox_cum", 0)
            mm(b[:, 0:FH], tri, logf[:, 0, :], start=True, stop=True)
            mm(b[:, FH:2 * FH], ones, logf[:, 0, :], start=True, stop=False)
            mm(b[:, FH:2 * FH], tri, logf[:, 1, :], start=False, stop=True)
            mm(b[0:FH, P:2 * P], logf[:, 0, :], tri, start=True, stop=True)
            mm(b[0:FH, 2 * P:3 * P], logf[:, 0, :], ones, start=True, stop=False)
            mm(b[0:FH, 2 * P:3 * P], logf[:, 1, :], tri, start=False, stop=True).then_inc(bank_filled, 1)
            wait_emptied("fox_q", 3)
            transpose_in("fox_qT", fq_tok)
            wait_emptied("fox_k", 3)
            transpose_in("fox_kT", fk_tok)

            def fox_scores(h):
                b = take_bank("fox_s", h)
                part, blk = FD * (h % 2), h // 2
                pick = ident[0:FH, h:h + 1].to_broadcast([FH, P])
                for tt, lo, n in ((0, 0, P), (1, P, T)):
                    mm(b[:, lo:lo + n], fqT[part:part + FD, blk, tt * P:(tt + 1) * P], fkT[part:part + FD, blk, 0:n],
                       start=True, stop=False)
                    last = mm(b[:, lo:lo + n], pick, ncumT[:, 0:n], start=False, stop=True)
                last.then_inc(bank_filled, 1)

            def fox_turn(h):
                b = take_bank("fox_pT", h)
                pe.wait_ge(probs_ready, h + 1)
                for j in range(3):
                    last = nc.tensor.transpose(b[:, j * P:(j + 1) * P], prob[:, h % 2, j * P:(j + 1) * P], ident)
                last.then_inc(bank_filled, 1)

            def fox_read(pair):
                b = take_bank("fox_o", pair)
                wait_emptied("fox_pT", 2 * pair + 1)
                for j in range(2):
                    h = 2 * pair + j
                    p, o, f = probT[:, h % 4, :], b[FD * j:FD * (j + 1), :], slice(h * FD, (h + 1) * FD)
                    mm(o[:, 0:T], fv[:, 0, f], p[:, 0:T], start=True, stop=False)
                    last = mm(o[:, P:T], fv[:, 1, f], p[:, T:3 * P], start=False, stop=True)
                last.then_inc(bank_filled, 1)

            wait_emptied("fox_kT", 3)
            for i in range(FH + 3):
                if i < FH:
                    fox_scores(i)
                if 2 <= i < FH + 2:
                    fox_turn(i - 2)
                if i >= 4 and i % 2 == 0:
                    fox_read((i - 4) // 2)
            wait_emptied("fox_o", KB - 1)
            out_product("fox_out", fuT, KB)

            pe.wait_ge(x_ready, 1)
            transpose_in("x2T", x)
            wait_emptied("x2T", 3)
            for c in range(2):
                feature_chunk("conf_g", c)
                feature_chunk("conf_a", c)
            wait_emptied("conf_a", 3)
            for k8 in range(CONV_BY_VECTOR, KB):
                b = take_bank("conf_taps", k8)
                for k in range(TAPS):
                    n = (k8 - CONV_BY_VECTOR) * TAPS + k
                    pe.wait_ge(diag_ready, n + 1)
                    last = mm(b[:, 0:T], diags[:, n % DIAGS, :], u_pad[:, k8, k:k + T], start=(k == 0), stop=(k == TAPS - 1))
                    if k < TAPS - 1:
                        last.then_inc(diag_used, 1)
                last.then_inc(bank_filled, 1)
            for g in range(4):
                tt, half = g // 2, g % 2
                b = take_bank("conf_cT", g)
                pe.wait_ge(conv_ready, 4 if half == 0 else CONV_BY_VECTOR)
                if half == 1:
                    wait_emptied("conf_taps", KB - 1)
                for j in range(4):
                    last = nc.tensor.transpose(b[:, j * P:(j + 1) * P], conv[:, 4 * half + j, tt * P:(tt + 1) * P], ident)
                last.then_inc(bank_filled, 1)
            wait_emptied("conf_cT", 3)
            transpose_in("conf_nT", conf_n)
            pe.wait_ge(conf_low, 4)
            out_product("conf_out", conf_uT, KB)

            pe.wait_ge(x_ready, 2)
            transpose_in("x3T", x)
            wait_emptied("x3T", 3)
            for c in range(6):
                feature_chunk("ffn_gate", c)
                feature_chunk("ffn_up", c)
            pe.wait_ge(ffn_low, FB // 2)
            out_product("ffn_down", ffn_h, FB)

            pe.wait_ge(x_ready, 3)
            transpose_in("x4T", x)
            wait_emptied("x4T", 3)
            for c in range(2):
                for name in ("sc_c", "sc_h", "sc_b"):
                    feature_chunk(name, c)
            pe.wait_ge(sc_low, 4)
            out_product("sc_out", sc_uT, KB)

            pe.wait_ge(x_ready, 4)
            transpose_in("x5T", x)
            wait_emptied("x5T", 3)
            b = take_bank("route", 0)
            for tt in range(NT):
                for k in range(KB):
                    last = mm(b[:, tt * NE:(tt + 1) * NE], x5T[:, k, tt * P:(tt + 1) * P], w_router[:, k, :],
                              start=(k == 0), stop=(k == KB - 1))
            last.then_inc(bank_filled, 1)
            chosen = rt[:, 9]
            pe.wait_ge(mask_ready, 1)
            b = take_bank("rank", 0)
            mm(b[:, 0:NE], tri, chosen[:, 0, :], start=True, stop=True)
            mm(b[:, NE:2 * NE], ones, chosen[:, 0, :], start=True, stop=False)
            mm(b[:, NE:2 * NE], tri, chosen[:, 1, :], start=False, stop=True)
            mm(b[:, 2 * NE:3 * NE], ones, chosen[:, 0, :], start=True, stop=False)
            mm(b[:, 2 * NE:3 * NE], ones, chosen[:, 1, :], start=False, stop=True).then_inc(bank_filled, 1)

            pe.wait_ge(emptied["A"], ALL_EMPTIED["A"])
            pe.wait_ge(emptied["D"], ALL_EMPTIED["D"])

            def expert_unit(e, q, j, half, view):
                pe.wait_ge(unit_ready, e * (2 * PER_EXPERT) + 2 * (PRE + j) + half + 1)
                s = (2 * (PRE + q * PER_EXPERT + j) + half) % UNITS
                return [view(units[:, s, i, :]) for i in range(2)]

            def gather(e, q):
                pe.wait_ge(sel_ready, e + 1)
                for k in range(KB):
                    for tt in range(NT):
                        last = mm(psum[:, k // 4, (k % 4) * P:(k % 4 + 1) * P], x[:, tt, k * P:(k + 1) * P],
                                  e_sel[q][:, tt, :], start=(tt == 0), stop=(tt == NT - 1))
                last.then_inc(gather_filled, 1)

            def wide_product(e, q, j):
                b = psum[:, 4 + (q * 2 * PAIRS + j) % 4, :]
                if j == 0:
                    pe.wait_ge(gather_emptied, e + 1)
                pe.wait_ge(gate_emptied if j % 2 == 0 else up_emptied, e * PAIRS + j // 2 + 1)
                for half in range(2):
                    w = expert_unit(e, q, j, half, lambda a: as_cols(a, 4))
                    for k in range(4):
                        kk = 4 * half + k
                        last = product(b, [a[:, kk, :] for a in e_x[q]], [a[:, k, :] for a in w], kk == 0, kk == KB - 1)
                    last.then_inc(weights_used if half == 0 else gu_filled, 1)

            def expert(e, q, more, number):
                def turn_bank(i):
                    pe.wait_ge(turn_emptied, e * 8 + i + 1)
                    return psum[:, 2 + i % 2, :]

                def turn_hidden(c):
                    pe.wait_ge(up_emptied, e * PAIRS + c + 3)
                    b = turn_bank(c if c < PAIRS - 1 else PAIRS)
                    for j in range(4):
                        last = nc.tensor.transpose(b[:, j * P:(j + 1) * P],
                                                   e_ht[:, (q * PAIRS + c) % 2, j * P:(j + 1) * P], ident)
                    last.then_inc(turn_filled, 1)

                for j in range(1, 2 * PAIRS):
                    wide_product(e, q, j)
                    if j == 3:
                        pe.wait_ge(scatter_emptied, e + 1)
                    if j % 2 == 1 and j > 1:
                        turn_hidden(j // 2 - 1)
                    if j == GATHER_AFTER and more:
                        gather(e + 1, 1 - q)
                if more:
                    pe.wait_ge(gather_emptied, e + 2)
                for k in range(EB):
                    if k == 2 * ROWS:
                        b = turn_bank(PAIRS - 1)
                        for tt in range(NT):
                            last = nc.tensor.transpose(b[:, tt * P:(tt + 1) * P], e_sel[q][:, tt, :], ident)
                        last.then_inc(turn_filled, 1)
                        turn_hidden(PAIRS - 1)
                    if k % 2 == 0:
                        w = expert_unit(e, q, 2 * PAIRS + k // ROWS, k % ROWS // 2, lambda a: as_rows(a, 2))
                    if k % 4 == 0:
                        c = k // 4
                        pe.wait_ge(turn_emptied, e * 8 + 2 + (c if c < PAIRS - 1 else PAIRS) + 1)
                    for c in range(2):
                        last = product(psum[:, c, :], [a[:, k, :] for a in e_h],
                                       [a[:, k % 2, c * 512:(c + 1) * 512] for a in w], k == 0, k == EB - 1)
                    if k % 2 == 1 and k < EB - 1:
                        last.then_inc(weights_used, 1)
                last.then_inc(down_filled, 1)
                if more:
                    wide_product(e + 1, 1 - q, 0)
                pe.wait_ge(down_emptied, e + 1)
                for tt in range(NT):
                    for c in range(2):
                        last = mm(psum[:, 2 * tt + c, :], e_selT[:, tt * P:(tt + 1) * P], e_y[:, c * 512:(c + 1) * 512],
                                  start=True, stop=True)
                last.then_inc(scatter_filled, 1)

            def start_second():
                gather(NE, 0)
                wide_product(NE, 0, 0)

            gather(0, 0)
            wide_product(0, 0, 0)
            sweeps(pe, expert, start_second)

        @block.scalar
        def _(act):
            act.dma_start(x[:, :, :], t["x"][0].rearrange("(t p) d -> p t d", p=P)).then_inc(x_loaded, 16)
            act.dma_start(pos_i, t["positions"][0:1, :].to_broadcast([P, T])).then_inc(pos_loaded, 16)
            act.dma_start(wf[:, :, :], cols(w_fox, 4 * D, FH)).then_inc(small_loaded, 16)
            act.dma_start(w_router[:, :, :], cols(t["moe_w_router_2"][0], 0, NE)).then_inc(small_loaded, 16)
            for j in range(2):
                act.dma_start(gains[j * FD:(j + 1) * FD, 0:1], t["fox_q_gain"].rearrange("a d -> d a")
                              ).then_inc(small_loaded, 16)
                act.dma_start(gains[j * FD:(j + 1) * FD, 1:2], t["fox_k_gain"].rearrange("a d -> d a")
                              ).then_inc(small_loaded, 16)

            def bank(name, i):
                n = BANK_AT[name, i]
                act.wait_ge(bank_filled, n + 1)
                return psum[:, n % NBANK, :]

            def pairs(b):
                return b.rearrange("p (j n) -> p j n", j=2)

            def wait_emptied(name, i):
                who, count = emptied_by(BANK_AT[name, i])
                act.wait_ge(emptied[who], count)

            split = [0]

            def highs_until(n):
                for m in range(split[0], n + 1):
                    act.wait_ge(slot_filled[m % RING], 16 * (m // RING + 1))
                    parts = used_units(m)
                    for half, narrow in parts:
                        if 2 * m + half >= UNITS:
                            act.wait_ge(*released(2 * m + half - UNITS))
                        src, dst = unit_parts(m, half)
                        if narrow:
                            src, dst = narrow(src), [narrow(d) for d in dst]
                        nc.scalar.copy(dst[0], src).then_inc(unit_high, 3 - len(parts))
                split[0] = max(split[0], n + 1)

            def square_rows(junk):
                for tt in range(NT):
                    last = nc.scalar.activation(junk[:, tt, :], x[:, tt, :], ACT.Square, scale=float(D) ** -0.5,
                                                accum_out=sumsq[:, tt:tt + 1])
                last.then_inc(sumsq_ready, 1)

            def high_affine(name):
                for g in range(4):
                    b = pairs(bank(name, g))
                    for j in range(2):
                        k = 2 * g + j
                        last = nc.scalar.activation(xr[:, 0, k, :], b[:, j, :], ACT.Identity,
                                                    scale=in_scale[:, k:k + 1], bias=in_shift[:, k:k + 1])
                    last.then_inc(bank_high, 1)

            def high_in(name, dst, n=4):
                for g in range(n):
                    nc.scalar.copy(dst[:, 2 * g:2 * g + 2, :], pairs(bank(name, g))).then_inc(bank_high, 1)

            act.wait_ge(x_loaded, 16)
            square_rows(xn)
            wait_emptied("vecs", 0)
            nc.scalar.activation(c_act[:, :], vec[:, :, V_C], ACT.Silu).then_inc(c_ready, 1)
            act.wait_ge(small_loaded, 6 * 16)
            nc.scalar.copy(wf_r[:, :, 0:FH], wf[:, :, :]).then_inc(wf_ready, 1)
            act.wait_ge(ang_ready, 1)
            nc.scalar.activation(cos, ang[:, 4, :], ACT.Sin)
            nc.scalar.activation(sin, ang[:, 3, :], ACT.Sin).then_inc(trig_ready, 1)
            act.wait_ge(first_used, KB)
            highs_until(1)

            wait_emptied("mod_cols", 0)
            high_affine("x0T")
            for name in ("ret_q", "ret_k"):
                for c in range(2):
                    highs_until(CHUNK_AT[name, c] + 2)
            wait_emptied("ret_k", RH - 1)
            for c in range(4):
                for tt in range(NT):
                    nc.scalar.copy(rv[:, tt, c * 512:(c + 1) * 512], bank("ret_v", 2 * c + tt)
                                   ).then_inc(emptied["A"], 1)
                highs_until(CHUNK_AT["ret_v", c] + 2)
            act.wait_ge(mod_used, 2 * KB)
            for c in range(4):
                for tt in range(NT):
                    nc.scalar.activation(rg[:, tt, c * 512:(c + 1) * 512], bank("ret_g", 2 * c + tt), ACT.Silu
                                         ).then_inc(emptied["A"], 1)
                if c == 3:
                    act.dma_start(decay, t["decay"].rearrange("p (h n) -> p h n", h=RH)).then_inc(decay_loaded, 16)
                highs_until(CHUNK_AT["ret_g", c] + 2)
            high_in("ret_uT", ruT[0], 8)
            highs_until(CHUNK_AT["ret_out", 3] + 1)

            wait_emptied("ret_y", 3)
            square_rows(xn1)
            high_affine("x1T")
            highs_until(CHUNK_AT["ret_out", 3] + 2)
            for s, name in enumerate(("fox_q", "fox_k")):
                for c in range(2):
                    for tt in range(NT):
                        i = 2 * c + tt
                        n = 4 * s + i
                        b = bank(name, i)
                        if n >= 2:
                            act.wait_ge(fox_sq_used, n - 1)
                        nc.scalar.activation(fsq[:, n % 2, :], b, ACT.Square).then_inc(fox_sq, 1)
                    highs_until(CHUNK_AT[name, c] + 2)
                if s == 0:
                    act.wait_ge(logf_in, 1)
                    nc.scalar.activation(logf_t[:, 1, :], logf_t[:, 1, :], ACT.Exp).then_inc(scalar_step, 1)
                    act.wait_ge(scalar_step, 1)
                    nc.scalar.activation(logf_t[:, 1, :], logf_t[:, 1, :], ACT.Ln, bias=1.0).then_inc(logf_mid, 1)
            for c in range(2):
                for tt in range(NT):
                    nc.scalar.copy(fv[:, tt, c * 512:(c + 1) * 512], bank("fox_v", 2 * c + tt)
                                   ).then_inc(emptied["A"], 1)
                highs_until(CHUNK_AT["fox_v", c] + 2)
            for c in range(2):
                for g in range(2 * c, 2 * c + 2):
                    nc.scalar.activation(fgT[:, 2 * g:2 * g + 2, :], pairs(bank("fox_g", g)), ACT.Silu
                                         ).then_inc(emptied["A"], 1)
                highs_until(CHUNK_AT["fox_g", c] + 2)
            for i in range(FH + 2):
                if i < FH:
                    act.wait_ge(logits_ready, i + 1)
                    if i >= 2:
                        act.wait_ge(bank_filled, BANK_AT["fox_pT", i - 2] + 1)
                    nc.scalar.activation(prob[:, i % 2, 0:P], logits[:, i % 2, 0:P], ACT.Exp,
                                         bias=mx[:, i % 2, 0:1], accum_out=rsum[:, i % 2, 0:1])
                    nc.scalar.activation(prob[:, i % 2, P:3 * P], logits[:, i % 2, P:3 * P], ACT.Exp,
                                         bias=mx[:, i % 2, 1:2], accum_out=rsum[:, i % 2, 1:2]).then_inc(probs_exp, 1)
                if i >= 2:
                    h = i - 2
                    if h >= 4:
                        act.wait_ge(bank_filled, BANK_AT["fox_o", (h - 4) // 2] + 1)
                    nc.scalar.copy(probT[:, h % 4, :], bank("fox_pT", h)[:, 0:3 * P]).then_inc(emptied["A"], 1)
            highs_until(CHUNK_AT["fox_out", 1] + 1)
            wait_emptied("fox_y", 3)
            act.dma_start(final_row, t["final_g"].to_broadcast([P, D])).then_inc(final_loaded, 16)
            square_rows(xn1)

            def load_rows(g, b):
                act.dma_start(rows_gb[:, 0, :], g.to_broadcast([P, D])).then_inc(rows_loaded, 16)
                act.dma_start(rows_gb[:, 1, :], b.to_broadcast([P, D])).then_inc(rows_loaded, 16)

            act.wait_ge(x_ready, 1)
            load_rows(t["ln_mix_g_2"][0:1, :], t["ln_mix_b_2"][0:1, :])
            DIAG_COUNT = (KB - CONV_BY_VECTOR) * TAPS

            def diagonal(n):
                at = V_DW + n % TAPS
                nc.scalar.activation(diags[:, n % DIAGS, :], ident, ACT.Identity,
                                     scale=vec[:, CONV_BY_VECTOR + n // TAPS, at:at + 1]).then_inc(diag_ready, 1)

            def take_taps(k8):
                nc.scalar.activation(conv[:, k8, :], bank("conf_taps", k8)[:, 0:T], ACT.Identity,
                                     bias=vec[:, k8, V_CB:V_CB + 1]).then_inc(emptied["A"], 1)

            high_in("x2T", xr[:, 0])
            highs_until(CHUNK_AT["fox_out", 1] + 2)
            for c in range(2):
                for i in range(2):
                    nc.scalar.activation(half_gate[:, c, 2 * i:2 * i + 2, :], pairs(bank("conf_g", 2 * c + i)), ACT.Tanh,
                                         scale=0.5).then_inc(emptied["A"], 1)
                highs_until(CHUNK_AT["conf_g", c] + 2)
                highs_until(CHUNK_AT["conf_a", c] + 2)
                if c == 0:
                    act.wait_ge(taps_halved, 1)
                    for n in range(DIAGS):
                        diagonal(n)
            for n in range(DIAGS, DIAG_COUNT):
                before = n - DIAGS
                if before % TAPS == TAPS - 1:
                    act.wait_ge(bank_filled, BANK_AT["conf_taps", CONV_BY_VECTOR + before // TAPS] + 1)
                else:
                    act.wait_ge(diag_used, before + 1 - before // TAPS)
                diagonal(n)
                if n >= DIAGS + TAPS and (n - DIAGS) % TAPS == 0:
                    take_taps(CONV_BY_VECTOR + (n - DIAGS) // TAPS - 1)
            for k8 in range(CONV_BY_VECTOR + (DIAG_COUNT - 1 - DIAGS) // TAPS, KB):
                take_taps(k8)
            for g in range(4):
                b = pairs(bank("conf_nT", g))
                if g >= 2:
                    act.wait_ge(conf_low, g - 1)
                tmp = pairs(conf_t[:, g % 2, :])
                for j in range(2):
                    k = 2 * g + j
                    last = nc.scalar.activation(tmp[:, j, :], b[:, j, :], ACT.Silu,
                                                scale=vec[:, k, V_CG:V_CG + 1], bias=vec[:, k, V_CBETA:V_CBETA + 1])
                last.then_inc(emptied["A"], 1)
                wait_emptied("conf_nT", g)
                nc.scalar.copy(conf_uT[0][:, 2 * g:2 * g + 2, :], tmp).then_inc(conf_high, 1)
            highs_until(CHUNK_AT["conf_out", 1] + 1)

            act.wait_ge(x_ready, 2)
            high_in("x3T", xr[:, 0])
            highs_until(CHUNK_AT["conf_out", 1] + 2)
            for c in range(6):
                for i in range(2 * c, min(2 * c + 2, FB // 2)):
                    if c >= 2:
                        wait_emptied("ffn_up", i - 4)
                    nc.scalar.activation(ffn_s[:, c % 2, 2 * (i % 2):2 * (i % 2) + 2, :], pairs(bank("ffn_gate", i)),
                                         ACT.Silu).then_inc(emptied["A"], 1)
                highs_until(CHUNK_AT["ffn_gate", c] + 2)
                highs_until(CHUNK_AT["ffn_up", c] + 2)
            wait_emptied("ffn_up", FB // 2 - 1)
            load_rows(t["ln_ffn_g_2"][0:1, :], t["ln_ffn_b_2"][0:1, :])
            highs_until(CHUNK_AT["ffn_down", 5] + 1)

            act.wait_ge(x_ready, 3)
            load_rows(t["ln_mix_g_2"][1:2, :], t["ln_mix_b_2"][1:2, :])
            high_in("x4T", xr[:, 0])
            highs_until(CHUNK_AT["ffn_down", 5] + 2)
            for c in range(2):
                for i in range(2):
                    nc.scalar.copy(sc_c[:, c, 2 * i:2 * i + 2, :], pairs(bank("sc_c", 2 * c + i))
                                   ).then_inc(emptied["A"], 1)
                for name in ("sc_c", "sc_h", "sc_b"):
                    highs_until(CHUNK_AT[name, c] + 2)
            highs_until(CHUNK_AT["sc_out", 1] + 1)

            act.wait_ge(x_ready, 4)
            for g in range(4):
                nc.scalar.copy(x5T[:, 2 * g:2 * g + 2, :], pairs(bank("x5T", g))).then_inc(emptied["A"], 1)
            highs_until(CHUNK_AT["sc_out", 1] + 2)
            act.wait_ge(lg_ready, 1)
            nc.scalar.activation(rt[:, 11, :, 0], rt[:, 10, :, 0], ACT.Exp).then_inc(lg_exp, 1)
            act.wait_ge(emptied["D"], ALL_EMPTIED["D"])
            act.dma_start(out_g, t["ln_ffn_g_2"][1:2, :].to_broadcast([P, D])).then_inc(rows_loaded, 16)
            act.dma_start(out_b, t["ln_ffn_b_2"][1:2, :].to_broadcast([P, D])).then_inc(rows_loaded, 16)

            def high(e, q, j):
                s = (PRE + j) % RING
                act.wait_ge(slot_filled[s], e * (16 * PER_EXPERT // RING) + 16 * ((PRE + j) // RING + 1))
                for half in range(2):
                    before = (e, j - 2) if j >= 2 else (e - 1, j - 2 + PER_EXPERT)
                    act.wait_ge(*expert_unit_released(*before, half))
                    nc.scalar.copy(*expert_unit_parts(q, j, half, 0)).then_inc(unit_high, 1)

            def gathered(e, q):
                act.wait_ge(gather_filled, e + 1)
                nc.scalar.copy(e_x[q][0].rearrange("p k t -> p (k t)"), psum[:, 0:2, :].rearrange("p b n -> p (b n)")
                               ).then_inc(gather_high, 1)

            def expert(e, q, more, number):
                def turned(c):
                    i = c if c < PAIRS - 1 else PAIRS
                    act.wait_ge(turn_filled, e * 8 + i + 1)
                    nc.scalar.copy(e_h[0][:, 4 * c:4 * c + 4, :], psum[:, 2 + i % 2, :].rearrange("p (j n) -> p j n", j=4)
                                   ).then_inc(turn_high, 1)

                for c in range(PAIRS):
                    if more and 2 * c - 1 == GATHER_AFTER:
                        gathered(e + 1, 1 - q)
                    high(e, q, 2 * c + 2)
                    act.wait_ge(gu_filled, e * (2 * PAIRS) + 2 * c + 1)
                    act.wait_ge(up_emptied, e * PAIRS + c + 1)
                    nc.scalar.activation(e_s[:, (q * PAIRS + c) % 2, :], psum[:, 4 + (q * 2 * PAIRS + 2 * c) % 4, :],
                                         ACT.Silu).then_inc(gate_emptied, 1)
                    high(e, q, 2 * c + 3)
                    if c >= 1:
                        turned(c - 1)
                for j in range(2 * PAIRS + 2, PER_EXPERT):
                    high(e, q, j)
                    if j == 2 * PAIRS + 3:
                        turned(PAIRS - 1)
                if more:
                    high(e + 1, 1 - q, 0)
                    high(e + 1, 1 - q, 1)

            def start_second():
                act.wait_ge(over_done, 1)
                high(NE, 0, 0)
                high(NE, 0, 1)
                gathered(NE, 0)

            gathered(0, 0)
            sweeps(act, expert, start_second)

        @block.gpsimd
        def _(pool):
            pool.dma_start(bf_row[:, :], t["fox_b_f"].to_broadcast([P, FH])).then_inc(bf_loaded, 16)
            nc.gpsimd.memset(neg_half[:, :], -0.5).then_inc(gpsimd_step, 1)
            pool.wait_ge(gpsimd_step, 1)
            for n, name in enumerate(ROOTS):
                if name in ("rms0", "ret0"):
                    i = int(name == "ret0")
                    if i == 0:
                        pool.wait_ge(acc_clear, i + 1)
                        pool.dma_start(acc[0:1, :], t["mod_b"][i:i + 1, :]).then_inc(acc_seeded, 16)
                w = ROOT_WIDTH.get(name, NT)
                pool.wait_ge(root_asked, n + 1)
                nc.gpsimd.tensor_tensor(root_out[:, n % 2, 0:w], root_in[:, n % 2, 0:w], neg_half[:, 0:w], ALU.pow
                                        ).then_inc(root_ready, 1)
                if name == "rms0":
                    pool.wait_ge(acc_clear, 2)
                    pool.dma_start(acc[0:1, :], t["mod_b"][1:2, :]).then_inc(acc_seeded, 16)

        @block.vector
        def _(dve):
            v = nc.vector
            steps = [0]

            def step(ins):
                steps[0] += 1
                ins.then_inc(vector_step, 1)
                dve.wait_ge(vector_step, steps[0])

            def bank(name, i):
                n = BANK_AT[name, i]
                dve.wait_ge(bank_filled, n + 1)
                return psum[:, n % NBANK, :]

            def pairs(b):
                return b.rearrange("p (j n) -> p j n", j=2)

            def wait_emptied(name, i):
                who, count = emptied_by(BANK_AT[name, i])
                dve.wait_ge(emptied[who], count)

            def low(dst, src, high):
                return v.tensor_tensor(dst, src, high.bitcast(F32), ALU.subtract)

            split = [0]

            def lows_until(n):
                for m in range(split[0], n + 1):
                    parts = used_units(m)
                    for half, narrow in parts:
                        dve.wait_ge(unit_high, 2 * m + half + 3 - len(parts))
                        src, dst = unit_parts(m, half)
                        if narrow:
                            src, dst = narrow(src), [narrow(d) for d in dst]
                        low(dst[1], src, dst[0]).then_inc(unit_ready, 3 - len(parts))
                split[0] = max(split[0], n + 1)

            def low_in(name, dst, n=4):
                for g in range(n):
                    dve.wait_ge(bank_high, high_count(BANK_AT[name, g]))
                    low(dst[1][:, 2 * g:2 * g + 2, :], pairs(bank(name, g)), dst[0][:, 2 * g:2 * g + 2, :]
                        ).then_inc(emptied["D"], 1)

            xr_parts = [xr[:, 0], xr[:, 1]]

            def ask_root(name, src, scale, eps):
                n = ROOTS.index(name)
                w = ROOT_WIDTH.get(name, NT)
                v.tensor_scalar(root_in[:, n % 2, 0:w], src, scale, eps, ALU.mult, ALU.add).then_inc(root_asked, 1)

            def root(name):
                n = ROOTS.index(name)
                dve.wait_ge(root_ready, n + 1)
                return root_out[:, n % 2, :]

            def angles():
                dve.wait_ge(pos_loaded, 16)
                dve.wait_ge(const_loaded, 16)
                step(v.tensor_copy(ang[:, 0, :], pos_i))
                step(v.tensor_scalar(ang[:, 1, :], ang[:, 0, :], const[:, C_INV:C_INV + 1], None, ALU.mult))
                magic = 12582912.0
                step(v.tensor_scalar(ang[:, 2, :], ang[:, 1, :], float(1 / (2 * np.pi)), magic, ALU.mult, ALU.add))
                step(v.tensor_scalar(ang[:, 2, :], ang[:, 2, :], magic, None, ALU.subtract))
                c1 = 6.28125
                c2 = float(np.round((2 * np.pi - c1) * 2 ** 19) / 2 ** 19)
                c3 = float(2 * np.pi - c1 - c2)
                for c in (c1, c2, c3):
                    step(v.scalar_tensor_tensor(ang[:, 1, :], ang[:, 2, :], -c, ang[:, 1, :], ALU.mult, ALU.add))
                top = 3.1415925
                step(v.tensor_scalar(ang[:, 4, :], ang[:, 1, :], float(np.pi / 2), None, ALU.add))
                step(v.tensor_scalar(ang[:, 5, :], ang[:, 4, :], float(np.pi), float(-2 * np.pi), ALU.is_gt, ALU.mult))
                step(v.tensor_tensor(ang[:, 5, :], ang[:, 5, :], ang[:, 4, :], ALU.add))
                step(v.tensor_scalar(ang[:, 4, :], ang[:, 5, :], top, -top, ALU.min, ALU.max))
                v.tensor_scalar(ang[:, 3, :], ang[:, 1, :], top, -top, ALU.min, ALU.max).then_inc(ang_ready, 1)

            v.tensor_copy(vec[:, :, :].rearrange("p k n -> p (k n)"), bank("vecs", 0)[:, 0:KB * NVEC]
                          ).then_inc(emptied["D"], 1)

            def clear_acc():
                v.memset(acc, 0.0).then_inc(acc_clear, 1)

            def modulation_first(k):
                if k == 0:
                    dve.wait_ge(acc_seeded, 16)
                    dve.wait_ge(c_ready, 1)
                else:
                    dve.wait_ge(first_used, k)
                dve.wait_ge(first_filled[k % MOD_BUFS], 16 * (k // MOD_BUFS + 1))
                v.scalar_tensor_tensor(acc, mod_first[:, k % MOD_BUFS, :], c_act[:, k:k + 1], acc, ALU.mult, ALU.add
                                       ).then_inc(first_used, 1)

            def modulation(n):
                k, half = n // 2, n % 2
                if n == 0:
                    dve.wait_ge(acc_seeded, 32)
                dve.wait_ge(mod_filled[half], 16 * (n // 2 + 1))
                a = acc[:, half * 1536:(half + 1) * 1536]
                if n >= 2:
                    dve.wait_ge(mod_used, n - 1)
                v.scalar_tensor_tensor(a, mod_w[:, half, :], c_act[:, k:k + 1], a, ALU.mult, ALU.add
                                       ).then_inc(mod_used, 1)

            def normalise(name, n, dst):
                dve.wait_ge(sumsq_ready, n)
                ask_root(name, sumsq[:, :], 1.0, RMS_EPS)
                r = root(name)
                for tt in range(NT):
                    last = v.tensor_scalar(dst[:, tt, :], x[:, tt, :], r[:, tt:tt + 1], None, ALU.mult)
                last.then_inc(xn_ready, 1)

            def input_affine(i):
                b = bank("mod_cols", i)
                v.scalar_tensor_tensor(in_scale[:, :], b[:, KB:2 * KB], 1.0, vec[:, :, V_NORM + i], ALU.add, ALU.mult)
                v.tensor_copy(in_shift[:, :], b[:, 0:KB]).then_inc(emptied["D"], 1)
                wait_emptied("mod_cols", i)

            def low_affine(name):
                for g in range(4):
                    b = pairs(bank(name, g))
                    dve.wait_ge(bank_high, high_count(BANK_AT[name, g]))
                    a = affine_t[:, 2 * (g % 2):2 * (g % 2) + 2, :]
                    for j in range(2):
                        k = 2 * g + j
                        last = v.tensor_scalar(a[:, j, :], b[:, j, :], in_scale[:, k:k + 1], in_shift[:, k:k + 1],
                                               ALU.mult, ALU.add)
                    step(last)
                    low(xr[:, 1, 2 * g:2 * g + 2, :], a, xr[:, 0, 2 * g:2 * g + 2, :]).then_inc(emptied["D"], 1)

            def gate_row(i):
                for half in range(2):
                    v.tensor_copy(gate[:, half * 512:(half + 1) * 512], bank("mod_gate", 2 * i + half)
                                  ).then_inc(emptied["D"], 1)
                wait_emptied("mod_gate", 2 * i + 1)

            def gated_residual(name):
                for i in range(4):
                    xi = x[:, i // 2, (i % 2) * 512:(i % 2 + 1) * 512]
                    step(v.tensor_tensor(y_tmp[:, i % 2, :], bank(name, i), gate[:, (i % 2) * 512:(i % 2 + 1) * 512],
                                         ALU.mult))
                    v.tensor_tensor(xi, xi, y_tmp[:, i % 2, :], ALU.add).then_inc(emptied["D"], 1)

            clear_acc()
            wait_emptied("vecs", 0)
            normalise("rms0", 1, xn)
            angles()
            for k in range(KB):
                modulation_first(k)
            dve.wait_ge(wf_ready, 1)
            v.tensor_tensor(wf_r[:, :, FH:2 * FH], wf[:, :, :], wf_r[:, :, 0:FH].bitcast(F32), ALU.subtract
                            ).then_inc(wf_ready, 1)
            input_affine(0)
            low_affine("x0T")
            lows_until(1)
            gate_row(0)
            clear_acc()

            dve.wait_ge(trig_ready, 1)
            for name, dst in (("ret_q", rq), ("ret_k", rk)):
                for h in range(RH):
                    b = pairs(bank(name, h))
                    c2 = cos.unsqueeze(1).to_broadcast([P, 2, T])
                    s2 = sin.unsqueeze(1).to_broadcast([P, 2, T])
                    v.tensor_tensor(rot[:, 0], b, c2, ALU.mult)
                    step(v.tensor_tensor(rot[:, 1], b, s2, ALU.mult))
                    v.tensor_tensor(dst[:, 2 * h, :], rot[:, 0, 0, :], rot[:, 1, 1, :], ALU.subtract)
                    v.tensor_tensor(dst[:, 2 * h + 1, :], rot[:, 1, 0, :], rot[:, 0, 1, :], ALU.add
                                    ).then_inc(emptied["D"], 1)
                    wait_emptied(name, h)
                    if h % 2 == 1:
                        n = CHUNK_AT[name, h // 2]
                        lows_until(n + 2)
                        for m in mod_steps(n):
                            modulation(m)
            for c in range(4):
                n = CHUNK_AT["ret_v", c]
                lows_until(n + 2)
                for m in mod_steps(n):
                    modulation(m)
            for c in range(4):
                if c == 3:
                    input_affine(1)
                lows_until(CHUNK_AT["ret_g", c] + 2)

            def ret_decay(h):
                if h == 0:
                    dve.wait_ge(decay_loaded, 16)
                b = bank("ret_s", h)
                if h >= 2:
                    dve.wait_ge(bank_filled, BANK_AT["ret_o", 2 * (h - 2) + 1] + 1)
                v.tensor_tensor(dec_p[:, h % 2, 0:T], b[:, 0:T], decay[:, h, :], ALU.mult)
                v.tensor_tensor(dec_p[:, h % 2, T:3 * P], b[:, T:3 * P], decay[:, h, 0:P], ALU.mult
                                ).then_inc(emptied["D"], 1)

            ret_decay(0)
            wait_emptied("ret_g", 7)
            for h in range(RH):
                if h + 1 < RH:
                    ret_decay(h + 1)
                b = [bank("ret_o", 2 * h + tt) for tt in range(NT)]
                for tt in range(NT):
                    last = v.bn_stats(stats[:, tt, 0, :], b[tt])
                step(last)
                for tt in range(NT):
                    last = v.bn_aggr(meanvar[:, tt, :], stats[:, tt, 0, :])
                step(last)
                ask_root(f"ret{h}", meanvar[:, :, 1], 1.0, RMS_EPS)
                r = root(f"ret{h}")
                for tt in range(NT):
                    v.tensor_scalar(half_rows[:, tt, :], b[tt], meanvar[:, tt, 0:1], r[:, tt:tt + 1],
                                    ALU.subtract, ALU.mult).then_inc(emptied["D"], 1)
                wait_emptied("ret_o", 2 * h + 1)
                for tt in range(NT):
                    g = rg[:, tt, h * RHV:(h + 1) * RHV]
                    v.tensor_tensor(g, g, half_rows[:, tt, :], ALU.mult).then_inc(ret_u_ready, 1)
                dve.wait_ge(ret_u_ready, 2 * (h + 1))
            low_in("ret_uT", ruT, 8)
            lows_until(CHUNK_AT["ret_out", 3] + 1)
            gated_residual("ret_y")

            gate_row(1)
            normalise("rms1", 2, xn1)
            low_affine("x1T")
            lows_until(CHUNK_AT["ret_out", 3] + 2)
            dve.wait_ge(small_loaded, 6 * 16)
            dve.wait_ge(bf_loaded, 16)
            f = logf_t[:, 0, :]
            f3 = f.rearrange("p (t h) -> p t h", t=NT)
            b = bank("fox_f", 0)[:, 0:2 * NT * FH].rearrange("p (t j h) -> p t j h", t=NT, j=2)
            step(v.tensor_tensor(f3, b[:, :, 0, :], bf_row[:, :].unsqueeze(1).to_broadcast([P, NT, FH]), ALU.add))
            v.tensor_tensor(f3, f3, b[:, :, 1, :], ALU.add).then_inc(emptied["D"], 1)
            wait_emptied("fox_f", 0)
            v.scalar_tensor_tensor(logf_t[:, 1, :], f, -1.0, f, ALU.mult, ALU.min).then_inc(logf_in, 1)
            step(v.tensor_tensor(qk_gain[:, :], gains[:, 0:1], gains[:, 1:2], ALU.mult))
            step(v.tensor_scalar(qk_gain[:, :], qk_gain[:, :], float(FD) ** -0.5, None, ALU.mult))

            def unit_heads(name, key, dst, s):
                for i in range(4):
                    n = 4 * s + i
                    b = bank(name, i)
                    tt, c = i % 2, i // 2
                    dve.wait_ge(fox_sq, n + 1)
                    v.tensor_reduce(head_sq[:, n % 2, :], fsq[:, n % 2, :].rearrange("p (h d) -> p h d", d=FD),
                                    AX.X, ALU.add).then_inc(fox_sq_used, 1)
                    dve.wait_ge(fox_sq_used, n + 1)
                    ask_root(f"{key}{i}", head_sq[:, n % 2, :], 1.0 / FD, RMS_EPS)
                    r = root(f"{key}{i}")[:, 0:8].unsqueeze(2).to_broadcast([P, 8, FD])
                    v.tensor_tensor(dst[:, tt, c * 512:(c + 1) * 512].rearrange("p (h d) -> p h d", d=FD),
                                    b.rearrange("p (h d) -> p h d", d=FD), r, ALU.mult).then_inc(emptied["D"], 1)
                    wait_emptied(name, i)
                    if i % 2 == 1:
                        lows_until(CHUNK_AT[name, c] + 2)

            unit_heads("fox_q", "fq", fq_tok, 0)
            dve.wait_ge(logf_mid, 1)
            v.scalar_tensor_tensor(logf[:, :, :].rearrange("p t h -> p (t h)"), f, 0.0, logf_t[:, 1, :],
                                   ALU.min, ALU.subtract).then_inc(logf_ready, 1)
            unit_heads("fox_k", "fk", fk_tok, 1)
            for name in ("fox_v", "fox_g"):
                for c in range(2):
                    lows_until(CHUNK_AT[name, c] + 2)
            b = bank("fox_cum", 0)
            v.tensor_copy(cum[:, :, :].rearrange("p t h -> p (t h)"), b[:, 0:NT * FH])
            v.tensor_scalar(ncumT[:, :], b[0:FH, P:3 * P], -1.0, None, ALU.mult).then_inc(emptied["D"], 1)
            for g in range(4):
                v.tensor_scalar(fqT[:, 2 * g:2 * g + 2, :], pairs(bank("fox_qT", g)), qk_gain[:, 0:1], None, ALU.mult
                                ).then_inc(emptied["D"], 1)
            for g in range(4):
                v.tensor_copy(fkT[:, 2 * g:2 * g + 2, :], pairs(bank("fox_kT", g))).then_inc(emptied["D"], 1)

            wait_emptied("fox_kT", 3)
            for i in range(FH + 3):
                if i < FH:
                    b = bank("fox_s", i)
                    if i >= 2:
                        dve.wait_ge(probs_exp, i - 1)
                    j = i % 2
                    v.scalar_tensor_tensor(logits[:, j, 0:P], b[:, 0:P], cum[:, 0, i:i + 1],
                                           const[:, C_MASK + P:C_MASK + 2 * P], ALU.add, ALU.add)
                    v.scalar_tensor_tensor(logits[:, j, P:3 * P], b[:, P:3 * P], cum[:, 1, i:i + 1],
                                           const[:, C_MASK:C_MASK + 2 * P], ALU.add, ALU.add
                                           ).then_inc(emptied["D"], 1)
                    wait_emptied("fox_s", i)
                    v.tensor_reduce(mx[:, j, 0:1], logits[:, j, 0:P], AX.X, ALU.max, negate=True)
                    v.tensor_reduce(mx[:, j, 1:2], logits[:, j, P:3 * P], AX.X, ALU.max, negate=True
                                    ).then_inc(logits_ready, 1)
                if 1 <= i <= FH:
                    h, j = i - 1, (i - 1) % 2
                    dve.wait_ge(probs_exp, h + 1)
                    step(v.reciprocal(rinv[:, j, :], rsum[:, j, :]))
                    v.tensor_scalar(prob[:, j, 0:P], prob[:, j, 0:P], rinv[:, j, 0:1], None, ALU.mult)
                    v.tensor_scalar(prob[:, j, P:3 * P], prob[:, j, P:3 * P], rinv[:, j, 1:2], None, ALU.mult
                                    ).then_inc(probs_ready, 1)
                if i >= 4 and i % 2 == 0:
                    g = (i - 4) // 2
                    u = fgT[:, g, :]
                    step(v.tensor_tensor(u, bank("fox_o", g)[:, 0:T], u, ALU.mult))
                    step(v.tensor_copy(fuT[0][:, g, :], u))
                    low(fuT[1][:, g, :], u, fuT[0][:, g, :]).then_inc(emptied["D"], 1)
            lows_until(CHUNK_AT["fox_out", 1] + 1)
            gated_residual("fox_y")

            dve.wait_ge(sumsq_ready, 3)
            ask_root("final", sumsq[:, :], 1.0, RMS_EPS)
            r = root("final")
            dve.wait_ge(final_loaded, 16)
            for tt in range(NT):
                last = v.scalar_tensor_tensor(x[:, tt, :], x[:, tt, :], r[:, tt:tt + 1], final_row, ALU.mult, ALU.mult)
            last.then_inc(x_ready, 1)
            dve.wait_ge(x_ready, 1)
            low_in("x2T", xr_parts)
            lows_until(CHUNK_AT["fox_out", 1] + 2)

            step(v.memset(u_pad[:, :, 0:TAPS - 1], 0.0))
            v.tensor_scalar(vec[:, :, V_DW:V_DW + TAPS], vec[:, :, V_DW:V_DW + TAPS], 0.5, None, ALU.mult
                            ).then_inc(taps_halved, 1)
            dve.wait_ge(taps_halved, 1)
            chain = {}

            def tap(i, k):
                if k == 0:
                    ins = v.tensor_scalar(conv[:, i, :], u_pad[:, i, 0:T], vec[:, i, V_DW:V_DW + 1],
                                          vec[:, i, V_CB:V_CB + 1], ALU.mult, ALU.add)
                else:
                    dve.wait_ge(vector_step, chain[i])
                    ins = v.scalar_tensor_tensor(conv[:, i, :], u_pad[:, i, k:k + T], vec[:, i, V_DW + k:V_DW + k + 1],
                                                 conv[:, i, :], ALU.mult, ALU.add)
                if k == TAPS - 1:
                    ins.then_inc(conv_ready, 1)
                else:
                    ins.then_inc(vector_step, 1)
                    steps[0] += 1
                    chain[i] = steps[0]

            early = 2 * TAPS // 3
            for c in range(2):
                lows_until(CHUNK_AT["conf_g", c] + 2)
                for g in range(2 * c, 2 * c + 2):
                    wait_emptied("conf_g", g)
                    v.scalar_tensor_tensor(u_pad[:, 2 * g:2 * g + 2, TAPS - 1:], half_gate[:, c, 2 * (g % 2):2 * (g % 2) + 2, :],
                                           1.0, pairs(bank("conf_a", g)), ALU.add, ALU.mult).then_inc(emptied["D"], 1)
                wait_emptied("conf_a", 2 * c + 1)
                lows_until(CHUNK_AT["conf_a", c] + 2)
                if c == 0:
                    for k in range(early):
                        tap(0, k)
                        tap(1, k)
            for k in range(early, TAPS):
                tap(0, k)
                tap(1, k)
            for k in range(TAPS):
                for i in range(2, CONV_BY_VECTOR):
                    tap(i, k)
            for tt in range(NT):
                for half in range(2):
                    last = v.bn_stats(stats[:, tt, half, :], bank("conf_cT", 2 * tt + half))
            step(last)
            for tt in range(NT):
                last = v.bn_aggr(meanvar[:, tt, :], stats[:, tt, :, :].rearrange("p a b -> p (a b)"))
            step(last)
            ask_root("conf", meanvar[:, :, 1], 1.0, LN_EPS)
            r = root("conf")
            for tt in range(NT):
                for half in range(2):
                    v.tensor_scalar(conf_n[:, tt, half * 512:(half + 1) * 512], bank("conf_cT", 2 * tt + half),
                                    meanvar[:, tt, 0:1], r[:, tt:tt + 1], ALU.subtract, ALU.mult
                                    ).then_inc(emptied["D"], 1)
            for g in range(4):
                dve.wait_ge(conf_high, g + 1)
                low(conf_uT[1][:, 2 * g:2 * g + 2, :], pairs(conf_t[:, g % 2, :]), conf_uT[0][:, 2 * g:2 * g + 2, :]
                    ).then_inc(conf_low, 1)
            lows_until(CHUNK_AT["conf_out", 1] + 1)

            def layer_norm(name, n, y, z, g_row=rows_gb[:, 0, :], b_row=rows_gb[:, 1, :]):
                for tt in range(NT):
                    for half in range(2):
                        hs = slice(half * 512, (half + 1) * 512)
                        src, tell = y(tt, half)
                        ins = v.scalar_tensor_tensor(z[:, tt, hs], x[:, tt, hs], ALPHA, src, ALU.mult, ALU.add)
                        if tell is None:
                            step(ins)
                        else:
                            ins.then_inc(tell[0], 1)
                            dve.wait_ge(tell[0], tell[1])
                        last = v.bn_stats(stats[:, tt, half, :], z[:, tt, hs])
                step(last)
                for tt in range(NT):
                    last = v.bn_aggr(meanvar[:, tt, :], stats[:, tt, :, :].rearrange("p a b -> p (a b)"))
                step(last)
                ask_root(name, meanvar[:, :, 1], 1.0, LN_EPS)
                r = root(name)
                for tt in range(NT):
                    step(v.tensor_scalar(z[:, tt, :], z[:, tt, :], meanvar[:, tt, 0:1], r[:, tt:tt + 1],
                                         ALU.subtract, ALU.mult))
                dve.wait_ge(rows_loaded, 32 * n)
                for tt in range(NT):
                    step(v.tensor_tensor(z[:, tt, :], z[:, tt, :], g_row, ALU.mult))
                for tt in range(NT):
                    last = v.tensor_tensor(x[:, tt, :], z[:, tt, :], b_row, ALU.add)
                last.then_inc(x_ready, 1)
                dve.wait_ge(x_ready, n + 1)

            def from_banks(name):
                def y(tt, half):
                    i = 2 * tt + half
                    return bank(name, i), (emptied["D"], emptied_by(BANK_AT[name, i])[1])
                return y

            layer_norm("mix0", 1, from_banks("conf_y"), region(8448, NT, D))
            low_in("x3T", xr_parts)
            lows_until(CHUNK_AT["conf_out", 1] + 2)

            for c in range(6):
                lows_until(CHUNK_AT["ffn_gate", c] + 2)
                for i in range(2 * c, min(2 * c + 2, FB // 2)):
                    h = ffn_t[:, i % 2, :]
                    wait_emptied("ffn_gate", i)
                    v.tensor_tensor(pairs(h), ffn_s[:, c % 2, 2 * (i % 2):2 * (i % 2) + 2, :], pairs(bank("ffn_up", i)),
                                    ALU.mult).then_inc(emptied["D"], 1)
                    wait_emptied("ffn_up", i)
                    step(v.tensor_copy(ffn_h[0][:, 2 * i:2 * i + 2, :], pairs(h)))
                    low(ffn_h[1][:, 2 * i:2 * i + 2, :], pairs(h), ffn_h[0][:, 2 * i:2 * i + 2, :]).then_inc(ffn_low, 1)
                lows_until(CHUNK_AT["ffn_up", c] + 2)
            lows_until(CHUNK_AT["ffn_down", 5] + 1)
            layer_norm("ffn0", 2, from_banks("ffn_y"), region(0, NT, D))
            low_in("x4T", xr_parts)
            lows_until(CHUNK_AT["ffn_down", 5] + 2)

            step(v.memset(ch[:, :, 0:STAPS - 1], 0.0))
            for c in range(2):
                lows_until(CHUNK_AT["sc_c", c] + 2)
                for g in range(2 * c, 2 * c + 2):
                    wait_emptied("sc_c", g)
                    v.tensor_tensor(ch[:, 2 * g:2 * g + 2, STAPS - 1:], sc_c[:, c, 2 * (g % 2):2 * (g % 2) + 2, :],
                                    pairs(bank("sc_h", g)), ALU.mult).then_inc(emptied["D"], 1)
                wait_emptied("sc_h", 2 * c + 1)
                lows_until(CHUNK_AT["sc_h", c] + 2)
                for i in range(4):
                    k8 = 4 * c + i
                    step(v.tensor_scalar(sc_t[:, i, :], ch[:, k8, 0:T], vec[:, k8, V_SC:V_SC + 1], None, ALU.mult))
                    for k in range(1, STAPS):
                        step(v.scalar_tensor_tensor(sc_t[:, i, :], ch[:, k8, k:k + T], vec[:, k8, V_SC + k:V_SC + k + 1],
                                                    sc_t[:, i, :], ALU.mult, ALU.add))
                for g in range(2 * c, 2 * c + 2):
                    u = sc_t[:, 2 * (g % 2):2 * (g % 2) + 2, :]
                    v.tensor_tensor(u, u, pairs(bank("sc_b", g)), ALU.mult).then_inc(emptied["D"], 1)
                    wait_emptied("sc_b", g)
                    step(v.tensor_copy(sc_uT[0][:, 2 * g:2 * g + 2, :], u))
                    low(sc_uT[1][:, 2 * g:2 * g + 2, :], u, sc_uT[0][:, 2 * g:2 * g + 2, :]).then_inc(sc_low, 1)
                dve.wait_ge(sc_low, 2 * c + 2)
                lows_until(CHUNK_AT["sc_b", c] + 2)
            lows_until(CHUNK_AT["sc_out", 1] + 1)
            layer_norm("mix1", 3, from_banks("sc_y"), region(8448, NT, D))

            LG, M, E, C, OH1, LG2, OH2, G1, G2, CH, DIF, EX = range(12)
            row8 = desc.unsqueeze(1).to_broadcast([P, NT, NE])

            def wide(i):
                return rt[:, i, :, 0:1].to_broadcast([P, NT, NE])

            lows_until(CHUNK_AT["sc_out", 1] + 2)
            step(v.memset(rt[:, :, :, :], 0.0))
            v.tensor_copy(rt[:, LG].rearrange("p t e -> p (t e)"), bank("route", 0)[:, 0:NT * NE]
                          ).then_inc(emptied["D"], 1)
            wait_emptied("route", 0)
            for src, top, hot in ((LG, M, OH1), (LG2, E, OH2)):
                if src == LG2:
                    step(v.scalar_tensor_tensor(rt[:, LG2], rt[:, OH1], -3e38, rt[:, LG], ALU.mult, ALU.add))
                step(v.tensor_reduce(rt[:, top, :, 0], rt[:, src], AX.X, ALU.max))
                step(v.tensor_tensor(rt[:, C], rt[:, src], wide(top), ALU.is_equal))
                step(v.tensor_tensor(rt[:, C], rt[:, C], row8, ALU.mult))
                step(v.tensor_reduce(rt[:, 12, :, 0], rt[:, C], AX.X, ALU.max))
                step(v.tensor_tensor(rt[:, hot], row8, wide(12), ALU.is_equal))
            v.tensor_tensor(rt[:, CH], rt[:, OH1], rt[:, OH2], ALU.add).then_inc(mask_ready, 1)
            v.tensor_tensor(rt[:, DIF, :, 0], rt[:, E, :, 0], rt[:, M, :, 0], ALU.subtract).then_inc(lg_ready, 1)
            dve.wait_ge(lg_exp, 1)
            step(v.tensor_scalar(rt[:, 13, :, 0], rt[:, EX, :, 0], 1.0, None, ALU.add))
            step(v.reciprocal(rt[:, G1, :, 0], rt[:, 13, :, 0]))
            step(v.tensor_tensor(rt[:, G2, :, 0], rt[:, G1, :, 0], rt[:, EX, :, 0], ALU.mult))
            step(v.tensor_tensor(rt[:, C], rt[:, OH1], wide(G1), ALU.mult))
            step(v.tensor_tensor(rt[:, LG2], rt[:, OH2], wide(G2), ALU.mult))
            step(v.tensor_tensor(gate_of[:, :, :].rearrange("p e t -> p t e"), rt[:, C], rt[:, LG2], ALU.add))
            b = bank("rank", 0)
            step(v.tensor_tensor(rt[:, C], b[:, 0:NT * NE].rearrange("p (t e) -> p t e", t=NT), rt[:, CH], ALU.mult))
            step(v.memset(slot_of[:, :, :], -1.0))
            v.tensor_scalar(slot_of[:, 0:NE, :].rearrange("p e t -> p t e"), rt[:, C], -1.0, None, ALU.add
                            ).then_inc(scatter_emptied, 1)
            for q in range(2):
                v.memset(e_acc[:, q, 0:512], 0.0).then_inc(gate_emptied, 1)
                v.memset(e_acc[:, q, 512:1024], 0.0).then_inc(up_emptied, 1)
            for q in range(2):
                step(v.tensor_reduce(big[:, q:q + 1], b[0:1, 2 * NE:3 * NE], AX.X, ALU.max))
                ins = v.tensor_scalar(over[:, :], big[:, q:q + 1], float(P), None, ALU.is_gt)
                ins.then_inc(turn_emptied, 1)
            dve.wait_ge(turn_emptied, 2)
            v.tensor_copy(big[:, 0:1], b[0:1, 0:1]).then_inc(emptied["D"], 1)
            dve.wait_ge(emptied["D"], ALL_EMPTIED["D"])
            dve.wait_ge(scatter_emptied, 1)
            dve.wait_ge(up_emptied, 2)
            dve.wait_ge(gate_emptied, 2)

            def low_unit(e, q, j):
                for half in range(2):
                    dve.wait_ge(unit_high, e * (2 * PER_EXPERT) + 2 * (PRE + j) + half + 1)
                    dst, src = expert_unit_parts(q, j, half, 1)
                    low(dst, src, expert_unit_parts(q, j, half, 0)[0]).then_inc(unit_ready, 1)

            def select(of, q):
                for tt in range(NT):
                    last = v.tensor_scalar(e_sel[q][:, tt, :], const[:, C_IOTA:C_IOTA + P],
                                           slot_of[:, bass.ds(of, 1), tt], None, ALU.is_equal)
                last.then_inc(sel_ready, 1)

            def gathered(e, q):
                dve.wait_ge(gather_high, e + 1)
                low(e_x[q][1].rearrange("p k t -> p (k t)"), psum[:, 0:2, :].rearrange("p b n -> p (b n)"),
                    e_x[q][0].rearrange("p k t -> p (k t)")).then_inc(gather_emptied, 1)

            def expert(e, q, more, number):
                of = e - number * NE

                def turned(c):
                    i = c if c < PAIRS - 1 else PAIRS
                    dve.wait_ge(turn_high, e * PAIRS + c + 1)
                    low(e_h[1][:, 4 * c:4 * c + 4, :], psum[:, 2 + i % 2, :].rearrange("p (j n) -> p j n", j=4),
                        e_h[0][:, 4 * c:4 * c + 4, :]).then_inc(turn_emptied, 1)

                for c in range(PAIRS):
                    if more and 2 * c - 1 == GATHER_AFTER:
                        gathered(e + 1, 1 - q)
                    low_unit(e, q, 2 * c + 2)
                    dve.wait_ge(gate_emptied, e * PAIRS + c + 3)
                    dve.wait_ge(gu_filled, e * (2 * PAIRS) + 2 * c + 2)
                    v.tensor_tensor(e_ht[:, (q * PAIRS + c) % 2, :], e_s[:, (q * PAIRS + c) % 2, :],
                                    psum[:, 4 + (q * 2 * PAIRS + 2 * c + 1) % 4, :], ALU.mult).then_inc(up_emptied, 1)
                    low_unit(e, q, 2 * c + 3)
                    if c >= 1:
                        turned(c - 1)
                    if c == 1 and more:
                        select(of + 1, 1 - q)
                for j in range(2 * PAIRS + 2, PER_EXPERT):
                    low_unit(e, q, j)
                    if j == 2 * PAIRS + 3:
                        dve.wait_ge(turn_filled, e * 8 + PAIRS)
                        v.tensor_copy(e_selT, psum[:, 2 + (PAIRS - 1) % 2, 0:NT * P]).then_inc(turn_emptied, 1)
                        turned(PAIRS - 1)
                if more:
                    low_unit(e + 1, 1 - q, 0)
                dve.wait_ge(down_filled, e + 1)
                v.tensor_copy(e_y, psum[:, 0:2, :].rearrange("p b n -> p (b n)")).then_inc(down_emptied, 1)
                if more:
                    low_unit(e + 1, 1 - q, 1)
                dve.wait_ge(scatter_filled, e + 1)
                dve.wait_ge(scatter_emptied, e + 1)
                for tt in range(NT):
                    last = v.scalar_tensor_tensor(e_acc[:, tt, :],
                                                  psum[:, 2 * tt:2 * tt + 2, :].rearrange("p b n -> p (b n)"),
                                                  gate_of[:, bass.ds(of, 1), tt], e_acc[:, tt, :], ALU.mult, ALU.add)
                last.then_inc(scatter_emptied, 1)
                if not more:
                    dve.wait_ge(scatter_emptied, e + 2)

            def start_second():
                v.tensor_scalar(slot_of[:, :, :], slot_of[:, :, :], float(P), None, ALU.subtract).then_inc(over_done, 1)
                dve.wait_ge(over_done, 1)
                select(0, 0)
                low_unit(NE, 0, 0)
                low_unit(NE, 0, 1)
                gathered(NE, 0)

            select(0, 0)
            gathered(0, 0)
            sweeps(dve, expert, start_second)
            layer_norm("out", 4, lambda tt, half: (e_acc[:, tt, half * 512:(half + 1) * 512], None),
                       region(0, NT, D), out_g, out_b)
    return nc


_INS = ['x', 'c', 'positions', 'mod_w', 'mod_b', 'norm_g', 'ret_w_in', 'ret_w_out', 'fox_w_in', 'fox_b_f',
        'fox_q_gain', 'fox_k_gain', 'fox_w_out', 'final_g', 'ln_mix_g_2', 'ln_mix_b_2', 'ln_ffn_g_2',
        'ln_ffn_b_2', 'conf_w_in_2', 'conf_w_dw_2', 'conf_b_dw_2', 'conf_ln_g_2', 'conf_ln_b_2', 'conf_w_out_2',
        'sc_w_in_2', 'sc_w_conv_2', 'sc_w_out_2', 'ffn_w_gate_2', 'ffn_w_up_2', 'ffn_w_down_2',
        'moe_w_router_2', 'moe_w_gate_2', 'moe_w_up_2', 'moe_w_down_2']


def kernel(**inputs):
    import concourse.bacc as bacc
    from concourse.bass_utils import run_bass_kernel_spmd

    nc = bacc.Bacc("TRN2", target_bir_lowering=False, num_devices=1)
    arrays, views = {}, {}
    const, decay = shape_constants()
    given = {name: np.ascontiguousarray(inputs[name]) for name in _INS}
    given["final_g"] = given["final_g"].reshape(1, D)
    given["const"], given["decay"] = const, decay
    for name, a in given.items():
        arrays[f"in_{name}"] = a
        views[name] = nc.dram_tensor(f"in_{name}", a.shape, mybir.dt.from_np(a.dtype), kind="ExternalInput").ap()
    out = nc.dram_tensor("out", (1, T, D), F32, kind="ExternalOutput").ap()
    build(nc, views, out)
    r = run_bass_kernel_spmd(nc, [arrays], core_ids=[0])
    return r.results[0]["out"]
```

```python
from contextlib import ExitStack

import numpy as np

import concourse.bass as bass
from concourse import mybir

F32 = mybir.dt.float32
I32 = mybir.dt.int32
ACT = mybir.ActivationFunctionType
ALU = mybir.AluOpType
AX = mybir.AxisListType

P = 128
D = 1024
KB = D // P
T = 256
NT = T // P
CHUNK = 64
RH, RHK, RHV = 4, 256, 512
RV = RH * RHV
FH, FD = 16, 64
DFF = 2816
FB = DFF // P
NE = 8
EF = 3584
EB = EF // P
TAPS = 31
GATHER_AFTER = 7
CONV_BY_VECTOR = 5
CONV_SHARED = 17
DIAGS = 22
STAPS = 3
RMS_EPS = 1e-6
LN_EPS = 1e-5
ALPHA = float((2.0 * 2) ** 0.25)
BIG = 1e30

RING = 3
UNITS = 4
MOD_BUFS = 5
COLS = 512
ROWS = 4
PAIRS = EF // COLS
DOWNS = EB // ROWS
PER_EXPERT = 2 * PAIRS + DOWNS
assert PER_EXPERT % RING == 0 and 2 * PER_EXPERT % UNITS != 1

TENSOR_TAPS = ([(CONV_BY_VECTOR - 1, k) for k in range(CONV_SHARED)]
               + [(b, k) for b in range(CONV_BY_VECTOR, KB) for k in range(TAPS)])


def block_ends(n):
    return n + 1 == len(TENSOR_TAPS) or TENSOR_TAPS[n + 1][0] != TENSOR_TAPS[n][0]


V_C, V_NORM, V_CB, V_CG, V_CBETA, V_SC = 0, 1, 3, 4, 5, 6
V_DW = V_SC + STAPS
NVEC = V_DW + TAPS
REGION = 15360

C_IDENT, C_TRI, C_ONES = 0, 128, 256
C_MASK = 384
C_IOTA = C_MASK + 256
C_DESC = C_IOTA + P
C_INV = C_DESC + 8
C_END = C_INV + 1


def shape_constants():
    i = np.arange(P)
    c = np.zeros((P, C_END), np.float32)
    c[:, C_IDENT:C_IDENT + P] = np.eye(P)
    c[:, C_TRI:C_TRI + P] = i[:, None] <= i[None, :]
    c[:, C_ONES:C_ONES + P] = 1.0
    c[:, C_MASK + P:C_MASK + 2 * P] = np.where(i[:, None] >= i[None, :], 0.0, -BIG)
    c[:, C_IOTA:C_IOTA + P] = i[None, :]
    c[:, C_DESC:C_DESC + 8] = 8 - np.arange(8)[None, :]
    half = RHK // 2
    exponent = -np.arange(half, dtype=np.float32) / np.float32(half)
    c[:, C_INV] = (10000.0 ** exponent.astype(np.float64)).astype(np.float32)
    lg = np.log1p(-np.exp2(-5.0 - np.arange(RH)))
    m, t = i[:, None], i[None, :]
    seen = (m // CHUNK == t // CHUNK) | (m < t)
    d = np.zeros((P, RH, 2, P), np.float32)
    for h in range(RH):
        d[:, h, 0] = np.where(seen, np.exp(lg[h] * abs(t - m)), 0.0) * RHK ** -0.5
        d[:, h, 1] = np.exp(lg[h] * (P + t - m)) * RHK ** -0.5
    return c, d.reshape(P, RH * 2 * P)


def weight_plan():
    plan = [("ret_q", 0), ("ret_q", 1), ("ret_k", 0), ("ret_k", 1)]
    plan += [("ret_v", i) for i in range(4)] + [("ret_g", i) for i in range(4)]
    plan += [("ret_out", i) for i in range(4)]
    plan += [(n, i) for n in ("fox_q", "fox_k", "fox_v", "fox_g") for i in range(2)]
    plan += [("fox_out", i) for i in range(2)]
    plan += [(n, i) for i in range(2) for n in ("conf_g", "conf_a")]
    plan += [("conf_out", i) for i in range(2)]
    plan += [(n, i) for i in range(6) for n in ("ffn_gate", "ffn_up")]
    plan += [("ffn_down", i) for i in range(6)]
    plan += [(n, i) for i in range(2) for n in ("sc_c", "sc_h", "sc_b")]
    plan += [("sc_out", i) for i in range(2)]
    return plan


PLAN = weight_plan()
CHUNK_AT = {key: n for n, key in enumerate(PLAN)}
PRE = len(PLAN)
SWEEP = NE * PER_EXPERT
assert PRE % 2 == 0 and SWEEP % 2 == 0 and SWEEP % RING == 0


def bank_plan():
    g = [("vecs", 0, "D")] + [("x0T", i, "A") for i in range(4)] + [("mod_cols", 0, "D")]
    g += [("mod_gate", i, "D") for i in range(2)]
    g += [("ret_q", i, "D") for i in range(RH)] + [("ret_k", i, "D") for i in range(RH)]
    g += [("ret_v", i, "A") for i in range(8)] + [("ret_g", i, "A") for i in range(4)]
    g += [("mod_cols", 1, "D")] + [("ret_s", h, "D") for h in range(2)]
    g += [("ret_g", i, "A") for i in range(4, 6)] + [("ret_s", h, "D") for h in range(2, RH)]
    g += [("ret_o", i, "D") for i in range(4)]
    g += [("ret_g", i, "A") for i in range(6, 8)]
    g += [("ret_o", i, "D") for i in range(4, 8)]
    g += [("ret_uT", i, "S") for i in range(8)]
    g += [("ret_y", i, "D") for i in range(4)]
    g += [("mod_gate", 2 + i, "D") for i in range(2)]
    g += [("x1T", i, "A") for i in range(4)]
    g += [("fox_q", 0, "D"), ("fox_q", 1, "D"), ("fox_f", 0, "D"), ("fox_q", 2, "D"), ("fox_q", 3, "D")]
    g += [("fox_k", i, "D") for i in range(4)]
    g += [("fox_v", i, "A") for i in range(4)] + [("fox_g", i, "A") for i in range(4)]
    g += [("fox_cum", 0, "D")]
    g += [("fox_qT", i, "A") for i in range(4)] + [("fox_kT", i, "D") for i in range(4)]
    for i in range(FH + 3):
        if i < FH:
            g += [("fox_s", i, "D")]
        if 2 <= i < FH + 2:
            g += [("fox_pT", i - 2, "A")]
        if i >= 4 and i % 2 == 0:
            g += [("fox_o", (i - 4) // 2, "D")]
    g += [("fox_y", i, "D") for i in range(4)]
    g += [("x2T", i, "S") for i in range(4)]
    for c in range(2):
        g += [("conf_g", 2 * c + i, "A") for i in range(2)] + [("conf_a", 2 * c + i, "D") for i in range(2)]
    g += [("conf_taps", i, "A") for i in range(CONV_BY_VECTOR - 1, KB)]
    g += [("conf_cT", i, "D") for i in range(4)] + [("conf_nT", i, "A") for i in range(4)]
    g += [("conf_y", i, "D") for i in range(4)]
    g += [("x3T", i, "S") for i in range(4)]
    for c in range(6):
        n = min(2, FB // 2 - 2 * c)
        g += [("ffn_gate", 2 * c + i, "A") for i in range(n)] + [("ffn_up", 2 * c + i, "D") for i in range(n)]
    g += [("ffn_y", i, "D") for i in range(4)]
    g += [("x4T", i, "S") for i in range(4)]
    for c in range(2):
        g += [("sc_c", 2 * c + i, "A") for i in range(2)] + [("sc_h", 2 * c + i, "D") for i in range(2)]
        g += [("sc_b", 2 * c + i, "D") for i in range(2)]
    g += [("sc_y", i, "D") for i in range(4)]
    g += [("x5T", i, "A") for i in range(4)]
    g += [("route", 0, "D"), ("rank", 0, "D")]
    return g


OUT_BANKS = {"ret_out": "ret_y", "fox_out": "fox_y", "conf_out": "conf_y", "ffn_down": "ffn_y", "sc_out": "sc_y"}
TOKEN_MAJOR = ("ret_v", "ret_g", "fox_q", "fox_k", "fox_v")

BANKS = bank_plan()
BANK_AT = {(name, i): n for n, (name, i, _) in enumerate(BANKS)}
NBANK = 8


EMPTIER = {"A": "A", "D": "D", "S": "D"}


def emptied_by(n):
    who = EMPTIER[BANKS[n][2]]
    return who, sum(EMPTIER[b[2]] == who for b in BANKS[:n + 1])


def high_count(n):
    return sum(b[2] == "S" for b in BANKS[:n + 1])


ALL_EMPTIED = {who: sum(EMPTIER[b[2]] == who for b in BANKS) for who in "AD"}


def mod_steps(n):
    return range(2 * n, 2 * n + 2) if n < KB else range(0)


def unit_counted(u):
    name, i = PLAN[u // 2]
    if name in OUT_BANKS:
        return (name, i + 1) in CHUNK_AT or (u % 2 == 0 and (name, i) != ("ffn_down", FB // ROWS))
    return name in TOKEN_MAJOR and u % 2 == 0


EXPERT_UNITS_COUNTED = 2 * PAIRS + 2 * DOWNS - 1
PRE_UNITS_COUNTED = sum(unit_counted(u) for u in range(2 * PRE))


def unit_bank(u):
    name, i = PLAN[u // 2]
    if name in OUT_BANKS:
        return BANK_AT[OUT_BANKS[name], 3]
    return BANK_AT[name, min(2 * i + 1, FB // 2 - 1) if name.startswith("ffn") else 2 * i + 1]


ROOTS = (["rms0_0", "rms0_1"] + [f"ret{h}" for h in range(RH)] + ["rms1_0", "rms1_1"] + [f"fq{i}" for i in range(4)]
         + [f"fk{i}" for i in range(4)] + ["final_0", "final_1", "conf"]
         + [f"{name}{tt}" for name in ("mix0_", "ffn0_", "mix1_", "out_") for tt in range(NT)])
ROOT_WIDTH = {**{f"fq{i}": 8 for i in range(4)}, **{f"fk{i}": 8 for i in range(4)},
              **{name: 1 for name in ROOTS if "_" in name}}


def build(nc, t, out):
    ctx = ExitStack()
    with ctx:
        def sb(name, shape, dt=F32):
            return ctx.enter_context(nc.sbuf_tensor(name, shape, dt))

        def sem(name):
            return ctx.enter_context(nc.semaphore(name))

        ring = sb("ring", [P, RING, ROWS * D])
        F32R = mybir.dt.float32r
        units_at = nc.sbuf_base
        units = sb("units", [P, UNITS, 2, ROWS * D // 2], F32R)
        mod_first = nc.alloc_sbuf_tensor_at("mod_first", [P, MOD_BUFS, 3 * D], F32, offset=units_at)
        x = sb("x", [P, NT, D])
        xr_at = nc.sbuf_base
        xr = sb("xr", [P, 2, KB, T], F32R)
        X = nc.alloc_sbuf_tensor_at("X", [P, (KB + 1) * T], F32, offset=xr_at)
        region_at = nc.sbuf_base
        R = nc.alloc_sbuf_tensor_at("R", [P, REGION], F32, offset=region_at)
        H = nc.alloc_sbuf_tensor_at("H", [P, 2 * FB * T], F32R, offset=region_at)
        fence = sb("fence", [P, REGION])
        const = sb("const", [P, C_END])
        vec = sb("vec", [P, KB, NVEC])
        c_act = sb("c_act", [P, KB])
        in_scale = sb("in_scale", [P, KB])
        in_shift = sb("in_shift", [P, KB])
        wf_r = sb("wf_r", [P, KB, 2 * FH], F32R)
        w_router = sb("w_router", [P, KB, NE])
        gains = sb("gains", [P, 2])
        qk_gain = sb("qk_gain", [P, 2])
        bf_row = sb("bf_row", [P, FH])
        logf = sb("logf", [P, NT, FH])
        logf_t = sb("logf_t", [P, 2, NT * FH])
        cum = sb("cum", [P, NT, FH])
        mx = sb("mx", [P, 2, 2])
        rsum = sb("rsum", [P, 2, 2])
        rinv = sb("rinv", [P, 2, 2])
        sumsq = sb("sumsq", [P, NT])
        head_sq = sb("head_sq", [P, 2, 8])
        root_in = sb("root_in", [P, 2, 8])
        root_out = sb("root_out", [P, 2, 8])
        neg_half = sb("neg_half", [P, 8])
        stats = sb("stats", [P, NT, 2, 6])
        meanvar = sb("meanvar", [P, NT, 2])
        slot_of = sb("slot_of", [P, NE + 1, NT])
        gate_of = sb("gate_of", [P, NE, NT])
        gate = sb("gate", [P, D])
        over = sb("over", [1, 1], I32)
        big = sb("big", [1, 2])

        psum = ctx.enter_context(nc.psum_tensor("psum", [P, NBANK, 512], F32))

        def region(at, *shape):
            n = int(np.prod(shape))
            v = R[:, at:at + n]
            if len(shape) == 2:
                return v.rearrange("p (a b) -> p a b", a=shape[0])
            if len(shape) == 3:
                return v.rearrange("p (a b c) -> p a b c", a=shape[0], b=shape[1])
            return v

        ident = const[:, C_IDENT:C_IDENT + P]
        tri = const[:, C_TRI:C_TRI + P]
        ones = const[:, C_ONES:C_ONES + P]
        desc = const[:, C_DESC:C_DESC + NE]

        def split_region(at, *shape):
            n = int(np.prod(shape))
            return [H[:, at + i * n:at + (i + 1) * n].rearrange("p (a b) -> p a b", a=shape[0]) for i in range(2)]

        xn = region(0, NT, D)
        rq, rk = region(0, KB, T), region(2048, KB, T)
        rv, rg = region(4096, NT, RV), region(8192, NT, RV)
        ang = region(4096, 6, T)
        cos, sin = region(5632, T), region(5888, T)
        pos_i = region(6144, T).bitcast(I32)
        vec_rows = R[0:NVEC, 6400:6400 + D]
        affine_t = region(6400, 4, T)
        mod_w = region(8192, 2, 1536)
        rot = R[:, 11264:12288].rearrange("p (a b c) -> p a b c", a=2, b=2)
        acc = region(12288, 3 * D)
        decay = region(12288, RH, T)
        dec_p = region(13312, 2, 3 * P)
        half_rows = region(3072, 2, 512)
        ruT = split_region(0, RV // P, T)
        y_tmp = region(10240, 2, 512)
        wf = region(7424, KB, FH)
        ncumT = X[:, 0:T]
        xn1 = region(8192, NT, D)
        fq_tok, fk_tok = region(0, NT, D), region(2048, NT, D)
        fv, fgT = region(4096, NT, D), region(6144, KB, T)
        fkT = region(10240, KB, T)
        fqT = [region(8192, KB, T), X[:, T:T + KB * T].rearrange("p (k t) -> p k t", k=KB)]
        fuT = split_region(0, KB, T)
        fsq = region(12288, 2, 512)
        logits = region(12288, 2, 384)
        prob = region(13056, 2, 384)
        probT = region(13824, 4, 384)
        u_pad = region(0, KB, TAPS - 1 + T)
        conv = region(2288, KB, T)
        conf_n = region(4336, NT, D)
        conf_uT = split_region(0, KB, T)
        half_gate = region(6400, 2, 4, T)
        conf_t = region(6400, 2, 2 * T)
        diags = region(8448, DIAGS, P)
        rows_gb = region(11264, 2, D)
        final_row = region(14336, D)
        ffn_h = split_region(0, FB, T)
        ffn_s = region(11264, 2, 4, T)
        ffn_t = region(13312, 2, 2 * T)
        sc_c = region(4096, 2, 4, T)
        ch = region(6144, KB, STAPS - 1 + T)
        sc_t = region(10240, 4, T)
        sc_uT = split_region(0, KB, T)
        x5T = region(4096, KB, T)
        rt = R[:, 10496:10496 + 14 * NT * NE].rearrange("p (i t e) -> p i t e", i=14, t=NT)
        e_x = [[xr[:, i].rearrange("p k t -> p (k t)")[:, q * D:(q + 1) * D].rearrange("p (k t) -> p k t", k=KB)
                for i in range(2)] for q in range(2)]
        e_h = split_region(0, EB, P)
        e_acc = region(7168, NT, D)
        e_y = region(9216, D)
        e_sel = [region(10240 + q * NT * P, NT, P) for q in range(2)]
        e_selT = region(10752, NT * P)
        e_ht = region(11264, 2, 512)
        e_s = region(12288, 2, 512)
        out_g = gate[:, :]
        out_b = region(13312, D)

        slot_filled = [sem(f"slot_filled{s}") for s in range(RING)]
        weights_used = sem("weights_used")
        first_filled = [sem(f"mod_first_filled{b}") for b in range(MOD_BUFS)]
        first_used = sem("mod_first_used")
        mod_filled = [sem("mod_filled0"), sem("mod_filled1")]
        mod_used = sem("mod_used")
        acc_seeded = sem("acc_seeded")
        x_loaded = sem("x_loaded")
        vec_loaded = sem("vec_loaded")
        const_loaded = sem("const_loaded")
        small_loaded = sem("small_loaded")
        bf_loaded = sem("bf_loaded")
        pos_loaded = sem("pos_loaded")
        rows_loaded = sem("rows_loaded")
        final_loaded = sem("final_loaded")
        decay_loaded = sem("decay_loaded")
        bank_filled = sem("bank_filled")
        unit_high = sem("unit_high")
        unit_ready = sem("unit_ready")
        affine_low = sem("affine_low")
        bank_high = sem("bank_high")
        wf_ready = sem("wf_ready")
        conf_low = sem("conf_low")
        ffn_low = sem("ffn_low")
        sc_low = sem("sc_low")
        over_done = sem("over_done")
        emptied = {"A": sem("bank_emptied_by_scalar"), "D": sem("bank_emptied_by_vector")}
        c_ready = sem("c_ready")
        acc_clear = sem("acc_clear")
        sumsq_ready = sem("sumsq_ready")
        root_asked = sem("root_asked")
        root_ready = sem("root_ready")
        xn_ready = sem("xn_ready")
        ang_ready = sem("ang_ready")
        trig_ready = sem("trig_ready")
        ret_u_ready = sem("ret_u_ready")
        x_ready = sem("x_ready")
        fox_sq = sem("fox_sq")
        fox_sq_used = sem("fox_sq_used")
        logf_in = sem("logf_in")
        logf_mid = sem("logf_mid")
        logf_ready = sem("logf_ready")
        logits_ready = sem("logits_ready")
        probs_exp = sem("probs_exp")
        probs_ready = sem("probs_ready")
        half_ready = sem("half_ready")
        conv_ready = sem("conv_ready")
        taps_halved = sem("taps_halved")
        diag_ready = sem("diag_ready")
        diag_used = sem("diag_used")
        lg_ready = sem("lg_ready")
        lg_exp = sem("lg_exp")
        mask_ready = sem("mask_ready")
        sel_ready = sem("sel_ready")
        gather_filled = sem("gather_filled")
        gather_high = sem("gather_high")
        gather_emptied = sem("gather_emptied")
        down_filled = sem("down_filled")
        down_emptied = sem("down_emptied")
        scatter_filled = sem("scatter_filled")
        scatter_emptied = sem("scatter_emptied")
        gu_filled = sem("gu_filled")
        gate_emptied = sem("gate_emptied")
        up_emptied = sem("up_emptied")
        turn_filled = sem("turn_filled")
        turn_high = sem("turn_high")
        turn_emptied = sem("turn_emptied")
        out_written = sem("out_written")
        vector_step = sem("vector_step")
        scalar_step = sem("scalar_step")
        gpsimd_step = sem("gpsimd_step")

        def cols(w, at, n=COLS):
            return w.rearrange("(k p) n -> p k n", p=P)[:, :, at:at + n]

        def rows(w, at, n=ROWS):
            return w.rearrange("(r p) n -> p r n", p=P)[:, at:at + n, :]

        w_ret, w_fox = t["ret_w_in"][0], t["fox_w_in"][0]
        w_conf, w_sc = t["conf_w_in_2"][0], t["sc_w_in_2"][0]
        COL_SOURCES = {
            "ret_q": (w_ret, 0), "ret_k": (w_ret, D), "ret_v": (w_ret, 2 * D), "ret_g": (w_ret, 2 * D + RV),
            "fox_q": (w_fox, 0), "fox_k": (w_fox, D), "fox_v": (w_fox, 2 * D), "fox_g": (w_fox, 3 * D),
            "conf_a": (w_conf, 0), "conf_g": (w_conf, D),
            "ffn_gate": (t["ffn_w_gate_2"][0], 0), "ffn_up": (t["ffn_w_up_2"][0], 0),
            "sc_b": (w_sc, 0), "sc_c": (w_sc, D), "sc_h": (w_sc, 2 * D)}
        ROW_SOURCES = {"ret_out": t["ret_w_out"][0], "fox_out": t["fox_w_out"][0],
                       "conf_out": t["conf_w_out_2"][0], "ffn_down": t["ffn_w_down_2"][0],
                       "sc_out": t["sc_w_out_2"][0]}

        def as_cols(flat, n):
            return flat.rearrange("p (k n) -> p k n", k=n)

        def as_rows(flat, n):
            return flat.rearrange("p (r n) -> p r n", r=n)

        def chunk_width(n):
            name, i = PLAN[n]
            return min(COLS, DFF - COLS * i) if name.startswith("ffn_") and name in COL_SOURCES else COLS

        def chunk_blocks(n):
            name, i = PLAN[n]
            return min(ROWS, ROW_SOURCES[name].shape[0] // P - ROWS * i)

        def pre_load(n):
            name, i = PLAN[n]
            s = n % RING
            if name in COL_SOURCES:
                w, at = COL_SOURCES[name]
                width = chunk_width(n)
                return as_cols(ring[:, s], KB)[:, :, 0:width], cols(w, at + COLS * i, width)
            blocks = chunk_blocks(n)
            return as_rows(ring[:, s], ROWS)[:, 0:blocks, :], rows(ROW_SOURCES[name], ROWS * i, blocks)

        def unit_parts(n, half):
            size = ROWS * D // 2
            src = ring[:, n % RING, half * size:(half + 1) * size]
            dst = [units[:, (2 * n + half) % UNITS, i, :] for i in range(2)]
            return src, dst

        def released(u):
            if unit_counted(u):
                return weights_used, sum(unit_counted(v) for v in range(u + 1))
            return bank_filled, unit_bank(u) + 1

        def used_units(n):
            if n >= PRE:
                return [(0, None), (1, None)]
            name, i = PLAN[n]
            if name in COL_SOURCES:
                w = chunk_width(n)
                narrow = None if w == COLS else (lambda a: as_cols(a, 4)[:, :, 0:w])
                return [(0, narrow), (1, narrow)]
            blocks = chunk_blocks(n)
            return [(h, None) for h in range(2)] if blocks > 2 else [(0, None)]

        def expert_unit_parts(q, j, half, part):
            size = ROWS * D // 2
            return (units[:, (2 * (PRE + q * PER_EXPERT + j) + half) % UNITS, part, :],
                    ring[:, (PRE + j) % RING, half * size:(half + 1) * size])

        def expert_unit_released(e, j, half):
            if j < 2 * PAIRS:
                if half == 0:
                    return weights_used, e * EXPERT_UNITS_COUNTED + PRE_UNITS_COUNTED + j + 1
                return gu_filled, e * (2 * PAIRS) + j + 1
            r = 2 * (j - 2 * PAIRS) + half
            if r < 2 * DOWNS - 1:
                return weights_used, e * EXPERT_UNITS_COUNTED + PRE_UNITS_COUNTED + 2 * PAIRS + r + 1
            return down_filled, e + 1

        def sweeps(eng, body, before=None):
            def sweep(number):
                with eng.Fori(number * NE, (number + 1) * NE - 2, 2) as pair:
                    for q in range(2):
                        body(pair + q, q, True, number)
                for q in range(2):
                    body((number + 1) * NE - 2 + q, q, q == 0, number)

            sweep(0)
            again = eng.value_load(over[0:1, 0:1], min_val=0, max_val=1)
            with eng.If(again > 0):
                if before is not None:
                    before()
                sweep(1)

        block = ctx.enter_context(nc.Block())

        @block.sync
        def _(sp):
            def load_mod(n):
                k, half = n // 2, n % 2
                if n >= 2:
                    sp.wait_ge(mod_used, n - 1)
                sp.dma_start(mod_w[:, n % 2, :], t["mod_w"][1, k * P:(k + 1) * P, half * 1536:(half + 1) * 1536]
                             ).then_inc(mod_filled[n % 2], 16)

            for lo, src in ((V_C, t["c"]), (V_NORM, t["norm_g"]), (V_CB, t["conf_b_dw_2"]),
                            (V_CG, t["conf_ln_g_2"]), (V_CBETA, t["conf_ln_b_2"]),
                            (V_SC, t["sc_w_conv_2"][0]), (V_DW, t["conf_w_dw_2"][0])):
                sp.dma_start(vec_rows[lo:lo + src.shape[0], :], src).then_inc(vec_loaded, 16)
            sp.dma_start(const[:, :], t["const"]).then_inc(const_loaded, 16)
            for k in range(KB):
                if k >= MOD_BUFS:
                    sp.wait_ge(first_used, k - MOD_BUFS + 1)
                sp.dma_start(mod_first[:, k % MOD_BUFS, :], t["mod_w"][0, k * P:(k + 1) * P, :]
                             ).then_inc(first_filled[k % MOD_BUFS], 16)
            for n in range(PRE):
                if n >= RING:
                    sp.wait_ge(unit_ready, 2 * (n - RING) + 2)
                dst, src = pre_load(n)
                sp.dma_start(dst, src).then_inc(slot_filled[n % RING], 16)
                if n >= 2:
                    for m in mod_steps(n - 2):
                        load_mod(m)

            def expert(e, q, more, number):
                for j in range(PER_EXPERT):
                    sp.wait_ge(unit_ready, e * (2 * PER_EXPERT) + 2 * (PRE + j - RING) + 2)
                    if j < 2 * PAIRS:
                        w = t["moe_w_gate_2"] if j % 2 == 0 else t["moe_w_up_2"]
                        src = w[0].rearrange("e (k p) n -> e p k n", p=P)[
                            bass.ds(e - number * NE, 1), :, :, (j // 2) * COLS:(j // 2 + 1) * COLS]
                        dst = as_cols(ring[:, (PRE + j) % RING], KB)
                    else:
                        r = (j - 2 * PAIRS) * ROWS
                        src = t["moe_w_down_2"][0].rearrange("e (r p) n -> e p r n", p=P)[
                            bass.ds(e - number * NE, 1), :, r:r + ROWS, :]
                        dst = as_rows(ring[:, (PRE + j) % RING], ROWS)
                    sp.dma_start(dst, src.rearrange("o p k n -> (o p) k n")).then_inc(slot_filled[(PRE + j) % RING], 16)

            sweeps(sp, expert)

            for tt in range(NT):
                sp.wait_ge(x_ready, 4 * NT + tt + 1)
                sp.dma_start(out[0, tt * P:(tt + 1) * P, :], x[:, tt, :]).then_inc(out_written, 16)
            sp.wait_ge(out_written, NT * 16)

        @block.tensor
        def _(pe):
            mm = nc.tensor.matmul

            def take_bank(name, i):
                n = BANK_AT[name, i]
                if n >= NBANK:
                    who, count = emptied_by(n - NBANK)
                    pe.wait_ge(emptied[who], count)
                return psum[:, n % NBANK, :]

            def wait_emptied(name, i):
                who, count = emptied_by(BANK_AT[name, i])
                pe.wait_ge(emptied[who], count)

            def unit(n, half, view):
                pe.wait_ge(unit_ready, 2 * n + half + 1)
                return [view(units[:, (2 * n + half) % UNITS, i, :]) for i in range(2)]

            def product(dst, left, right, first, last):
                mm(dst, left[0], right[0], start=first, stop=False)
                mm(dst, left[0], right[1], start=False, stop=False)
                return mm(dst, left[1], right[0], start=False, stop=last)

            def transpose_in(name, src, ready=None):
                banks = [take_bank(name, g) for g in range(4)]
                for tt in range(NT):
                    if ready is not None:
                        ready(tt)
                    for g in range(4):
                        for j in range(2):
                            last = nc.tensor.transpose(banks[g][:, j * T + tt * P:j * T + (tt + 1) * P],
                                                       src[:, tt, (2 * g + j) * P:(2 * g + j + 1) * P], ident)
                        if tt == NT - 1:
                            last.then_inc(bank_filled, 1)

            def token_chunk(name, i, ready=None):
                n = CHUNK_AT[name, i]
                banks = [take_bank(name, NT * i + tt) for tt in range(NT)]
                for half in range(2):
                    w = unit(n, half, lambda a: as_cols(a, 4))
                    for tt in range(NT):
                        for k in range(4):
                            kk = 4 * half + k
                            if ready is not None and tt == 0 and k % 2 == 0:
                                ready(kk // 2)
                            left = [xr[:, h, kk, tt * P:(tt + 1) * P] for h in range(2)]
                            last = product(banks[tt], left, [a[:, k, :] for a in w], kk == 0, kk == KB - 1)
                        if half == 1:
                            last.then_inc(bank_filled, 1)
                    if half == 0:
                        last.then_inc(weights_used, 1)

            def feature_chunk(name, i, ready=None):
                n = CHUNK_AT[name, i]
                w = [unit(n, half, lambda a: as_cols(a, 4)) for half in range(2)]
                for g in range(chunk_width(n) // (2 * P)):
                    b = take_bank(name, 2 * i + g)
                    for j in range(2):
                        c = slice((2 * g + j) * P, (2 * g + j + 1) * P)
                        for k in range(KB):
                            if ready is not None and (g, j, k % 2) == (0, 0, 0):
                                ready(k // 2)
                            last = product(b[:, j * T:(j + 1) * T], [a[:, k % 4, c] for a in w[k // 4]],
                                           [xr[:, h, k, :] for h in range(2)], k == 0, k == KB - 1)
                    last.then_inc(bank_filled, 1)

            def out_product(name, src, blocks, ready):
                banks = [take_bank(OUT_BANKS[name], i) for i in range(4)]

                def block(k, tt, w):
                    for c in range(2):
                        last = product(banks[2 * tt + c], [a[:, k, tt * P:(tt + 1) * P] for a in src],
                                       [a[:, k % 2, c * 512:(c + 1) * 512] for a in w], k == 0, k == blocks - 1)
                        if k == blocks - 1:
                            last.then_inc(bank_filled, 1)
                    return last

                def weights(k):
                    return unit(CHUNK_AT[name, k // ROWS], k % ROWS // 2, lambda a: as_rows(a, 2))

                tail = blocks % ROWS or ROWS
                for k in range(blocks - tail):
                    if k % 2 == 0:
                        ready(k // 2)
                        w = weights(k)
                    for tt in range(NT):
                        last = block(k, tt, w)
                    if k % 2 == 1:
                        last.then_inc(weights_used, 1)
                w = {}
                for tt in range(NT):
                    for k in range(blocks - tail, blocks):
                        if tt == 0 and k % 2 == 0:
                            ready(k // 2)
                            w[k // 2] = weights(k)
                        last = block(k, tt, w[k // 2])
                        if tt == NT - 1 and k % 2 == 1 and k < blocks - 1:
                            last.then_inc(weights_used, 1)

            pe.wait_ge(const_loaded, 16)
            pe.wait_ge(vec_loaded, 7 * 16)
            b = take_bank("vecs", 0)
            for k in range(KB):
                last = nc.tensor.transpose(b[:, k * NVEC:(k + 1) * NVEC], vec_rows[:, k * P:(k + 1) * P],
                                           ident[0:NVEC, 0:NVEC])
            last.then_inc(bank_filled, 1)

            def modulation_columns(i):
                if i == 0:
                    pe.wait_ge(first_used, KB)
                else:
                    pe.wait_ge(mod_used, 2 * KB)
                b = take_bank("mod_cols", i)
                for m in range(2 * KB):
                    last = mm(b[:, m:m + 1], acc[:, m * P:(m + 1) * P], ones[:, 0:1], start=True, stop=True)
                last.then_inc(bank_filled, 1)

            def modulation_gate(i):
                for half in range(2):
                    b = take_bank("mod_gate", 2 * i + half)
                    mm(b, ones, acc[:, 2 * D + half * 512:2 * D + (half + 1) * 512], start=True, stop=True
                       ).then_inc(bank_filled, 1)

            transpose_in("x0T", xn, lambda tt: pe.wait_ge(xn_ready, tt + 1))
            modulation_columns(0)
            modulation_gate(0)
            for name in ("ret_q", "ret_k"):
                for c in range(2):
                    feature_chunk(name, c, (lambda g: pe.wait_ge(affine_low, g + 1)) if (name, c) == ("ret_q", 0) else None)
            for c in range(4):
                token_chunk("ret_v", c)

            def ret_scores(h):
                b = take_bank("ret_s", h)
                for d in range(2):
                    mm(b[:, 0:T], rk[:, 2 * h + d, 0:P], rq[:, 2 * h + d, :], start=(d == 0), stop=(d == 1))
                for d in range(2):
                    last = mm(b[:, T:T + P], rk[:, 2 * h + d, P:T], rq[:, 2 * h + d, P:T], start=(d == 0), stop=(d == 1))
                last.then_inc(bank_filled, 1)

            def ret_read(h):
                wait_emptied("ret_s", h)
                p, cols_h = dec_p[:, h % 2, :], slice(h * RHV, (h + 1) * RHV)
                b = take_bank("ret_o", 2 * h)
                mm(b, p[:, 0:P], rv[:, 0, cols_h], start=True, stop=True).then_inc(bank_filled, 1)
                b = take_bank("ret_o", 2 * h + 1)
                mm(b, p[:, P:2 * P], rv[:, 0, cols_h], start=True, stop=False)
                mm(b, p[:, 2 * P:3 * P], rv[:, 1, cols_h], start=False, stop=True).then_inc(bank_filled, 1)

            token_chunk("ret_g", 0)
            token_chunk("ret_g", 1)
            modulation_columns(1)
            wait_emptied("ret_k", RH - 1)
            ret_scores(0)
            ret_scores(1)
            token_chunk("ret_g", 2)
            ret_scores(2)
            ret_scores(3)
            wait_emptied("ret_v", 7)
            ret_read(0)
            ret_read(1)
            token_chunk("ret_g", 3)
            ret_read(2)
            ret_read(3)
            for h in range(RH):
                pe.wait_ge(ret_u_ready, 2 * (h + 1))
                for g in range(2 * h, 2 * h + 2):
                    b = take_bank("ret_uT", g)
                    for j in range(2):
                        for tt in range(NT):
                            last = nc.tensor.transpose(b[:, j * T + tt * P:j * T + (tt + 1) * P],
                                                       rg[:, tt, (2 * g + j) * P:(2 * g + j + 1) * P], ident)
                    last.then_inc(bank_filled, 1)
            out_product("ret_out", ruT, RV // P, lambda g: wait_emptied("ret_uT", g))

            modulation_gate(1)
            transpose_in("x1T", xn1, lambda tt: pe.wait_ge(xn_ready, NT + tt + 1))
            token_chunk("fox_q", 0, lambda g: pe.wait_ge(affine_low, 4 + g + 1))
            b = take_bank("fox_f", 0)
            pe.wait_ge(wf_ready, 2)
            for tt in range(NT):
                for k in range(KB):
                    f = b[:, 2 * tt * FH:2 * (tt + 1) * FH]
                    mm(f, xr[:, 0, k, tt * P:(tt + 1) * P], wf_r[:, k, :], start=(k == 0), stop=False)
                    last = mm(f[:, 0:FH], xr[:, 1, k, tt * P:(tt + 1) * P], wf_r[:, k, 0:FH], start=False, stop=(k == KB - 1))
            last.then_inc(bank_filled, 1)
            token_chunk("fox_q", 1)
            token_chunk("fox_k", 0)
            token_chunk("fox_k", 1)
            for c in range(2):
                token_chunk("fox_v", c)
            for c in range(2):
                feature_chunk("fox_g", c)
            pe.wait_ge(logf_ready, 1)
            b = take_bank("fox_cum", 0)
            mm(b[:, 0:FH], tri, logf[:, 0, :], start=True, stop=True)
            mm(b[:, FH:2 * FH], ones, logf[:, 0, :], start=True, stop=False)
            mm(b[:, FH:2 * FH], tri, logf[:, 1, :], start=False, stop=True)
            mm(b[0:FH, P:2 * P], logf[:, 0, :], tri, start=True, stop=True)
            mm(b[0:FH, 2 * P:3 * P], logf[:, 0, :], ones, start=True, stop=False)
            mm(b[0:FH, 2 * P:3 * P], logf[:, 1, :], tri, start=False, stop=True).then_inc(bank_filled, 1)
            wait_emptied("fox_q", 3)
            transpose_in("fox_qT", fq_tok)
            wait_emptied("fox_k", 3)
            transpose_in("fox_kT", fk_tok)

            def fox_scores(h):
                b = take_bank("fox_s", h)
                blk = h // 2
                pick = ident[:, h:h + 1].to_broadcast([P, P])
                for tt, lo, n in ((0, 0, P), (1, P, T)):
                    mm(b[:, lo:lo + n], fqT[h % 2][:, blk, tt * P:(tt + 1) * P], fkT[:, blk, 0:n],
                       start=True, stop=False)
                    last = mm(b[:, lo:lo + n], pick, ncumT[:, 0:n], start=False, stop=True)
                last.then_inc(bank_filled, 1)

            def fox_turn(h):
                b = take_bank("fox_pT", h)
                pe.wait_ge(probs_ready, h + 1)
                for j in range(3):
                    last = nc.tensor.transpose(b[:, j * P:(j + 1) * P], prob[:, h % 2, j * P:(j + 1) * P], ident)
                last.then_inc(bank_filled, 1)

            def fox_read(pair):
                b = take_bank("fox_o", pair)
                wait_emptied("fox_pT", 2 * pair + 1)
                for j in range(2):
                    h = 2 * pair + j
                    p, o, f = probT[:, h % 4, :], b[FD * j:FD * (j + 1), :], slice(h * FD, (h + 1) * FD)
                    mm(o[:, 0:T], fv[:, 0, f], p[:, 0:T], start=True, stop=False)
                    last = mm(o[:, P:T], fv[:, 1, f], p[:, T:3 * P], start=False, stop=True)
                last.then_inc(bank_filled, 1)

            for i in range(FH + 3):
                if i < FH:
                    if i % 4 == 0:
                        wait_emptied("fox_qT", i // 4)
                        wait_emptied("fox_kT", i // 4)
                    fox_scores(i)
                if 2 <= i < FH + 2:
                    fox_turn(i - 2)
                if i >= 4 and i % 2 == 0:
                    fox_read((i - 4) // 2)
            out_product("fox_out", fuT, KB, lambda g: wait_emptied("fox_o", 2 * g + 1))

            transpose_in("x2T", x, lambda tt: pe.wait_ge(x_ready, tt + 1))
            for c in range(2):
                feature_chunk("conf_g", c, (lambda g: wait_emptied("x2T", g)) if c == 0 else None)
                feature_chunk("conf_a", c)
            wait_emptied("conf_a", 3)
            for n, (k8, k) in enumerate(TENSOR_TAPS):
                if k == 0:
                    b = take_bank("conf_taps", k8)
                pe.wait_ge(diag_ready, n + 1)
                mm(b[:, 0:T], diags[:, n % DIAGS, :], u_pad[:, k8, k:k + T], start=(k == 0), stop=block_ends(n)
                   ).then_inc(bank_filled if block_ends(n) else diag_used, 1)
            for g in range(4):
                tt, half = g // 2, g % 2
                b = take_bank("conf_cT", g)
                pe.wait_ge(conv_ready, 4 if half == 0 else CONV_BY_VECTOR)
                if half == 1:
                    wait_emptied("conf_taps", KB - 1)
                for j in range(4):
                    last = nc.tensor.transpose(b[:, j * P:(j + 1) * P], conv[:, 4 * half + j, tt * P:(tt + 1) * P], ident)
                last.then_inc(bank_filled, 1)
            transpose_in("conf_nT", conf_n, lambda tt: wait_emptied("conf_cT", 2 * tt + 1))
            out_product("conf_out", conf_uT, KB, lambda g: pe.wait_ge(conf_low, g + 1))

            transpose_in("x3T", x, lambda tt: pe.wait_ge(x_ready, NT + tt + 1))
            for c in range(6):
                feature_chunk("ffn_gate", c, (lambda g: wait_emptied("x3T", g)) if c == 0 else None)
                feature_chunk("ffn_up", c)
            out_product("ffn_down", ffn_h, FB, lambda g: pe.wait_ge(ffn_low, g + 1))

            transpose_in("x4T", x, lambda tt: pe.wait_ge(x_ready, NT * 2 + tt + 1))
            for c in range(2):
                for name in ("sc_c", "sc_h", "sc_b"):
                    feature_chunk(name, c, (lambda g: wait_emptied("x4T", g)) if (name, c) == ("sc_c", 0) else None)
            out_product("sc_out", sc_uT, KB, lambda g: pe.wait_ge(sc_low, g + 1))

            transpose_in("x5T", x, lambda tt: pe.wait_ge(x_ready, NT * 3 + tt + 1))
            wait_emptied("x5T", 3)
            b = take_bank("route", 0)
            for tt in range(NT):
                for k in range(KB):
                    last = mm(b[:, tt * NE:(tt + 1) * NE], x5T[:, k, tt * P:(tt + 1) * P], w_router[:, k, :],
                              start=(k == 0), stop=(k == KB - 1))
            last.then_inc(bank_filled, 1)
            chosen = rt[:, 9]
            pe.wait_ge(mask_ready, 1)
            b = take_bank("rank", 0)
            mm(b[:, 0:NE], tri, chosen[:, 0, :], start=True, stop=True)
            mm(b[:, NE:2 * NE], ones, chosen[:, 0, :], start=True, stop=False)
            mm(b[:, NE:2 * NE], tri, chosen[:, 1, :], start=False, stop=True)
            mm(b[:, 2 * NE:3 * NE], ones, chosen[:, 0, :], start=True, stop=False)
            mm(b[:, 2 * NE:3 * NE], ones, chosen[:, 1, :], start=False, stop=True).then_inc(bank_filled, 1)

            pe.wait_ge(emptied["A"], ALL_EMPTIED["A"])
            pe.wait_ge(emptied["D"], ALL_EMPTIED["D"])

            def expert_unit(e, q, j, half, view):
                pe.wait_ge(unit_ready, e * (2 * PER_EXPERT) + 2 * (PRE + j) + half + 1)
                s = (2 * (PRE + q * PER_EXPERT + j) + half) % UNITS
                return [view(units[:, s, i, :]) for i in range(2)]

            def gather(e, q):
                pe.wait_ge(sel_ready, e + 1)
                for k in range(KB):
                    for tt in range(NT):
                        last = mm(psum[:, k // 4, (k % 4) * P:(k % 4 + 1) * P], x[:, tt, k * P:(k + 1) * P],
                                  e_sel[q][:, tt, :], start=(tt == 0), stop=(tt == NT - 1))
                last.then_inc(gather_filled, 1)

            def wide_product(e, q, j):
                b = psum[:, 4 + (q * 2 * PAIRS + j) % 4, :]
                if j == 0:
                    pe.wait_ge(gather_emptied, e + 1)
                pe.wait_ge(gate_emptied if j % 2 == 0 else up_emptied, e * PAIRS + j // 2 + 1)
                for half in range(2):
                    w = expert_unit(e, q, j, half, lambda a: as_cols(a, 4))
                    for k in range(4):
                        kk = 4 * half + k
                        last = product(b, [a[:, kk, :] for a in e_x[q]], [a[:, k, :] for a in w], kk == 0, kk == KB - 1)
                    last.then_inc(weights_used if half == 0 else gu_filled, 1)

            def expert(e, q, more, number):
                def turn_bank(i):
                    pe.wait_ge(turn_emptied, e * 8 + i + 1)
                    return psum[:, 2 + i % 2, :]

                def turn_hidden(c):
                    pe.wait_ge(up_emptied, e * PAIRS + c + 3)
                    b = turn_bank(c if c < PAIRS - 1 else PAIRS)
                    for j in range(4):
                        last = nc.tensor.transpose(b[:, j * P:(j + 1) * P],
                                                   e_ht[:, (q * PAIRS + c) % 2, j * P:(j + 1) * P], ident)
                    last.then_inc(turn_filled, 1)

                for j in range(1, 2 * PAIRS):
                    wide_product(e, q, j)
                    if j == 3:
                        pe.wait_ge(scatter_emptied, e + 1)
                    if j % 2 == 1 and j > 1:
                        turn_hidden(j // 2 - 1)
                    if j == GATHER_AFTER and more:
                        gather(e + 1, 1 - q)
                if more:
                    pe.wait_ge(gather_emptied, e + 2)
                for k in range(EB):
                    if k == 2 * ROWS:
                        b = turn_bank(PAIRS - 1)
                        for tt in range(NT):
                            last = nc.tensor.transpose(b[:, tt * P:(tt + 1) * P], e_sel[q][:, tt, :], ident)
                        last.then_inc(turn_filled, 1)
                        turn_hidden(PAIRS - 1)
                    if k % 2 == 0:
                        w = expert_unit(e, q, 2 * PAIRS + k // ROWS, k % ROWS // 2, lambda a: as_rows(a, 2))
                    if k % 4 == 0:
                        c = k // 4
                        pe.wait_ge(turn_emptied, e * 8 + 2 + (c if c < PAIRS - 1 else PAIRS) + 1)
                    for c in range(2):
                        last = product(psum[:, c, :], [a[:, k, :] for a in e_h],
                                       [a[:, k % 2, c * 512:(c + 1) * 512] for a in w], k == 0, k == EB - 1)
                    if k % 2 == 1 and k < EB - 1:
                        last.then_inc(weights_used, 1)
                last.then_inc(down_filled, 1)
                if more:
                    wide_product(e + 1, 1 - q, 0)
                pe.wait_ge(down_emptied, e + 1)
                for tt in range(NT):
                    for c in range(2):
                        last = mm(psum[:, 2 * tt + c, :], e_selT[:, tt * P:(tt + 1) * P], e_y[:, c * 512:(c + 1) * 512],
                                  start=True, stop=True)
                last.then_inc(scatter_filled, 1)

            def start_second():
                gather(NE, 0)
                wide_product(NE, 0, 0)

            gather(0, 0)
            wide_product(0, 0, 0)
            sweeps(pe, expert, start_second)

        @block.scalar
        def _(act):
            act.dma_start(x[:, :, :], t["x"][0].rearrange("(t p) d -> p t d", p=P)).then_inc(x_loaded, 16)
            act.dma_start(pos_i, t["positions"][0:1, :].to_broadcast([P, T])).then_inc(pos_loaded, 16)
            act.dma_start(wf[:, :, :], cols(w_fox, 4 * D, FH)).then_inc(small_loaded, 16)
            act.dma_start(w_router[:, :, :], cols(t["moe_w_router_2"][0], 0, NE)).then_inc(small_loaded, 16)
            for j in range(2):
                act.dma_start(gains[j * FD:(j + 1) * FD, 0:1], t["fox_q_gain"].rearrange("a d -> d a")
                              ).then_inc(small_loaded, 16)
                act.dma_start(gains[j * FD:(j + 1) * FD, 1:2], t["fox_k_gain"].rearrange("a d -> d a")
                              ).then_inc(small_loaded, 16)

            def bank(name, i):
                n = BANK_AT[name, i]
                act.wait_ge(bank_filled, n + 1)
                return psum[:, n % NBANK, :]

            def pairs(b):
                return b.rearrange("p (j n) -> p j n", j=2)

            def wait_emptied(name, i):
                who, count = emptied_by(BANK_AT[name, i])
                act.wait_ge(emptied[who], count)

            split = [0]

            def highs_until(n):
                for m in range(split[0], n + 1):
                    act.wait_ge(slot_filled[m % RING], 16 * (m // RING + 1))
                    parts = used_units(m)
                    for half, narrow in parts:
                        if 2 * m + half >= UNITS:
                            act.wait_ge(*released(2 * m + half - UNITS))
                        src, dst = unit_parts(m, half)
                        if narrow:
                            src, dst = narrow(src), [narrow(d) for d in dst]
                        nc.scalar.copy(dst[0], src).then_inc(unit_high, 3 - len(parts))
                split[0] = max(split[0], n + 1)

            def square_rows(junk, ready=None):
                for tt in range(NT):
                    if ready is not None:
                        ready(tt)
                    nc.scalar.activation(junk[:, tt, :], x[:, tt, :], ACT.Square, scale=float(D) ** -0.5,
                                         accum_out=sumsq[:, tt:tt + 1]).then_inc(sumsq_ready, 1)

            def affine(i):
                for g in range(4):
                    b = pairs(bank(f"x{i}T", g))
                    n = 4 * i + g
                    if n >= 2:
                        act.wait_ge(affine_low, n - 1)
                    for j in range(2):
                        k = 2 * g + j
                        last = nc.scalar.activation(affine_t[:, 2 * (g % 2) + j, :], b[:, j, :], ACT.Identity,
                                                    scale=in_scale[:, k:k + 1], bias=in_shift[:, k:k + 1])
                    last.then_inc(emptied["A"], 1)

            def high_in(name, dst, n=4):
                for g in range(n):
                    nc.scalar.copy(dst[:, 2 * g:2 * g + 2, :], pairs(bank(name, g))).then_inc(bank_high, 1)

            act.wait_ge(x_loaded, 16)
            square_rows(xn)
            wait_emptied("vecs", 0)
            nc.scalar.activation(c_act[:, :], vec[:, :, V_C], ACT.Silu).then_inc(c_ready, 1)
            act.wait_ge(small_loaded, 6 * 16)
            nc.scalar.copy(wf_r[:, :, 0:FH], wf[:, :, :]).then_inc(wf_ready, 1)
            act.wait_ge(ang_ready, 1)
            nc.scalar.activation(cos, ang[:, 4, :], ACT.Sin)
            nc.scalar.activation(sin, ang[:, 3, :], ACT.Sin).then_inc(trig_ready, 1)
            act.wait_ge(first_used, KB)
            highs_until(0)

            wait_emptied("mod_cols", 0)
            affine(0)
            highs_until(1)
            for name in ("ret_q", "ret_k"):
                for c in range(2):
                    highs_until(CHUNK_AT[name, c] + 2)
            wait_emptied("ret_k", RH - 1)
            for c in range(4):
                for tt in range(NT):
                    nc.scalar.copy(rv[:, tt, c * 512:(c + 1) * 512], bank("ret_v", 2 * c + tt)
                                   ).then_inc(emptied["A"], 1)
                highs_until(CHUNK_AT["ret_v", c] + 2)
            act.wait_ge(mod_used, 2 * KB)
            for c in range(4):
                for tt in range(NT):
                    nc.scalar.activation(rg[:, tt, c * 512:(c + 1) * 512], bank("ret_g", 2 * c + tt), ACT.Silu
                                         ).then_inc(emptied["A"], 1)
                if c == 1:
                    act.wait_ge(bank_filled, BANK_AT["mod_cols", 1] + 1)
                    act.dma_start(decay, t["decay"].rearrange("p (h n) -> p h n", h=RH)).then_inc(decay_loaded, 16)
                highs_until(CHUNK_AT["ret_g", c] + 2)
            high_in("ret_uT", ruT[0], 8)
            highs_until(CHUNK_AT["ret_out", 3] + 1)

            square_rows(xn1, lambda tt: wait_emptied("ret_y", 2 * tt + 1))
            affine(1)
            highs_until(CHUNK_AT["ret_out", 3] + 2)
            for s, name in enumerate(("fox_q", "fox_k")):
                for c in range(2):
                    for tt in range(NT):
                        i = 2 * c + tt
                        n = 4 * s + i
                        b = bank(name, i)
                        if n >= 2:
                            act.wait_ge(fox_sq_used, n - 1)
                        nc.scalar.activation(fsq[:, n % 2, :], b, ACT.Square).then_inc(fox_sq, 1)
                    highs_until(CHUNK_AT[name, c] + 2)
                if s == 0:
                    act.wait_ge(logf_in, 1)
                    nc.scalar.activation(logf_t[:, 1, :], logf_t[:, 1, :], ACT.Exp).then_inc(scalar_step, 1)
                    act.wait_ge(scalar_step, 1)
                    nc.scalar.activation(logf_t[:, 1, :], logf_t[:, 1, :], ACT.Ln, bias=1.0).then_inc(logf_mid, 1)
            for c in range(2):
                for tt in range(NT):
                    nc.scalar.copy(fv[:, tt, c * 512:(c + 1) * 512], bank("fox_v", 2 * c + tt)
                                   ).then_inc(emptied["A"], 1)
                highs_until(CHUNK_AT["fox_v", c] + 2)
            for c in range(2):
                for g in range(2 * c, 2 * c + 2):
                    nc.scalar.activation(fgT[:, 2 * g:2 * g + 2, :], pairs(bank("fox_g", g)), ACT.Silu
                                         ).then_inc(emptied["A"], 1)
                if c == 0:
                    highs_until(CHUNK_AT["fox_g", c] + 2)
            for g in range(4):
                for odd in range(2):
                    last = nc.scalar.activation(fqT[odd][:, 2 * g:2 * g + 2, :], pairs(bank("fox_qT", g)), ACT.Identity,
                                                scale=qk_gain[:, odd:odd + 1])
                last.then_inc(emptied["A"], 1)
            for i in range(FH + 2):
                if i < FH:
                    act.wait_ge(logits_ready, i + 1)
                    if i >= 2:
                        act.wait_ge(bank_filled, BANK_AT["fox_pT", i - 2] + 1)
                    nc.scalar.activation(prob[:, i % 2, 0:P], logits[:, i % 2, 0:P], ACT.Exp,
                                         bias=mx[:, i % 2, 0:1], accum_out=rsum[:, i % 2, 0:1])
                    nc.scalar.activation(prob[:, i % 2, P:3 * P], logits[:, i % 2, P:3 * P], ACT.Exp,
                                         bias=mx[:, i % 2, 1:2], accum_out=rsum[:, i % 2, 1:2]).then_inc(probs_exp, 1)
                if i >= 2:
                    h = i - 2
                    if h >= 4:
                        act.wait_ge(bank_filled, BANK_AT["fox_o", (h - 4) // 2] + 1)
                    nc.scalar.copy(probT[:, h % 4, :], bank("fox_pT", h)[:, 0:3 * P]).then_inc(emptied["A"], 1)
            highs_until(CHUNK_AT["fox_out", 1] + 1)
            wait_emptied("fox_o", KB - 1)
            act.dma_start(final_row, t["final_g"].to_broadcast([P, D])).then_inc(final_loaded, 16)
            square_rows(xn1, lambda tt: wait_emptied("fox_y", 2 * tt + 1))

            def load_rows(g, b):
                act.dma_start(rows_gb[:, 0, :], g.to_broadcast([P, D])).then_inc(rows_loaded, 16)
                act.dma_start(rows_gb[:, 1, :], b.to_broadcast([P, D])).then_inc(rows_loaded, 16)

            act.wait_ge(x_ready, NT)
            load_rows(t["ln_mix_g_2"][0:1, :], t["ln_mix_b_2"][0:1, :])

            def diagonal(n):
                k8, k = TENSOR_TAPS[n]
                nc.scalar.activation(diags[:, n % DIAGS, :], ident, ACT.Identity,
                                     scale=vec[:, k8, V_DW + k:V_DW + k + 1]).then_inc(diag_ready, 1)

            def take_taps(k8):
                nc.scalar.activation(conv[:, k8, :], bank("conf_taps", k8)[:, 0:T], ACT.Identity,
                                     bias=vec[:, k8, V_CB:V_CB + 1]).then_inc(emptied["A"], 1)

            high_in("x2T", xr[:, 0])
            highs_until(CHUNK_AT["fox_out", 1] + 2)
            for c in range(2):
                for i in range(2):
                    nc.scalar.activation(half_gate[:, c, 2 * i:2 * i + 2, :], pairs(bank("conf_g", 2 * c + i)), ACT.Tanh,
                                         scale=0.5).then_inc(emptied["A"], 1)
                highs_until(CHUNK_AT["conf_g", c] + 2)
                highs_until(CHUNK_AT["conf_a", c] + 2)
                if c == 0:
                    act.wait_ge(taps_halved, 1)
                    for n in range(DIAGS):
                        diagonal(n)
            for n in range(DIAGS, len(TENSOR_TAPS) + DIAGS):
                before = n - DIAGS
                if block_ends(before):
                    take_taps(TENSOR_TAPS[before][0])
                elif n < len(TENSOR_TAPS):
                    act.wait_ge(diag_used, sum(not block_ends(m) for m in range(before + 1)))
                if n < len(TENSOR_TAPS):
                    diagonal(n)
            for g in range(4):
                b = pairs(bank("conf_nT", g))
                if g >= 2:
                    act.wait_ge(conf_low, g - 1)
                tmp = pairs(conf_t[:, g % 2, :])
                for j in range(2):
                    k = 2 * g + j
                    last = nc.scalar.activation(tmp[:, j, :], b[:, j, :], ACT.Silu,
                                                scale=vec[:, k, V_CG:V_CG + 1], bias=vec[:, k, V_CBETA:V_CBETA + 1])
                last.then_inc(emptied["A"], 1)
            highs_until(CHUNK_AT["conf_out", 1] + 1)

            act.wait_ge(x_ready, NT * 2)
            high_in("x3T", xr[:, 0])
            highs_until(CHUNK_AT["conf_out", 1] + 2)
            for c in range(6):
                for i in range(2 * c, min(2 * c + 2, FB // 2)):
                    if c >= 2:
                        wait_emptied("ffn_up", i - 4)
                    nc.scalar.activation(ffn_s[:, c % 2, 2 * (i % 2):2 * (i % 2) + 2, :], pairs(bank("ffn_gate", i)),
                                         ACT.Silu).then_inc(emptied["A"], 1)
                highs_until(CHUNK_AT["ffn_gate", c] + 2)
                highs_until(CHUNK_AT["ffn_up", c] + 2)
            wait_emptied("ffn_up", FB // 2 - 1)
            load_rows(t["ln_ffn_g_2"][0:1, :], t["ln_ffn_b_2"][0:1, :])
            highs_until(CHUNK_AT["ffn_down", 5] + 1)

            act.wait_ge(x_ready, NT * 3)
            load_rows(t["ln_mix_g_2"][1:2, :], t["ln_mix_b_2"][1:2, :])
            high_in("x4T", xr[:, 0])
            highs_until(CHUNK_AT["ffn_down", 5] + 2)
            for c in range(2):
                for i in range(2):
                    nc.scalar.copy(sc_c[:, c, 2 * i:2 * i + 2, :], pairs(bank("sc_c", 2 * c + i))
                                   ).then_inc(emptied["A"], 1)
                for name in ("sc_c", "sc_h", "sc_b"):
                    highs_until(CHUNK_AT[name, c] + 2)
            highs_until(CHUNK_AT["sc_out", 1] + 1)

            act.wait_ge(x_ready, NT * 4)
            for g in range(4):
                nc.scalar.copy(x5T[:, 2 * g:2 * g + 2, :], pairs(bank("x5T", g))).then_inc(emptied["A"], 1)
            highs_until(CHUNK_AT["sc_out", 1] + 2)
            act.wait_ge(lg_ready, 1)
            nc.scalar.activation(rt[:, 11, :, 0], rt[:, 10, :, 0], ACT.Exp).then_inc(lg_exp, 1)
            act.wait_ge(emptied["D"], ALL_EMPTIED["D"])
            act.dma_start(out_g, t["ln_ffn_g_2"][1:2, :].to_broadcast([P, D])).then_inc(rows_loaded, 16)
            act.dma_start(out_b, t["ln_ffn_b_2"][1:2, :].to_broadcast([P, D])).then_inc(rows_loaded, 16)

            def high(e, q, j):
                s = (PRE + j) % RING
                act.wait_ge(slot_filled[s], e * (16 * PER_EXPERT // RING) + 16 * ((PRE + j) // RING + 1))
                for half in range(2):
                    before = (e, j - 2) if j >= 2 else (e - 1, j - 2 + PER_EXPERT)
                    act.wait_ge(*expert_unit_released(*before, half))
                    nc.scalar.copy(*expert_unit_parts(q, j, half, 0)).then_inc(unit_high, 1)

            def gathered(e, q):
                act.wait_ge(gather_filled, e + 1)
                nc.scalar.copy(e_x[q][0].rearrange("p k t -> p (k t)"), psum[:, 0:2, :].rearrange("p b n -> p (b n)")
                               ).then_inc(gather_high, 1)

            def expert(e, q, more, number):
                def turned(c):
                    i = c if c < PAIRS - 1 else PAIRS
                    act.wait_ge(turn_filled, e * 8 + i + 1)
                    nc.scalar.copy(e_h[0][:, 4 * c:4 * c + 4, :], psum[:, 2 + i % 2, :].rearrange("p (j n) -> p j n", j=4)
                                   ).then_inc(turn_high, 1)

                for c in range(PAIRS):
                    if more and 2 * c - 1 == GATHER_AFTER:
                        gathered(e + 1, 1 - q)
                    high(e, q, 2 * c + 2)
                    act.wait_ge(gu_filled, e * (2 * PAIRS) + 2 * c + 1)
                    act.wait_ge(up_emptied, e * PAIRS + c + 1)
                    nc.scalar.activation(e_s[:, (q * PAIRS + c) % 2, :], psum[:, 4 + (q * 2 * PAIRS + 2 * c) % 4, :],
                                         ACT.Silu).then_inc(gate_emptied, 1)
                    high(e, q, 2 * c + 3)
                    if c >= 1:
                        turned(c - 1)
                for j in range(2 * PAIRS + 2, PER_EXPERT):
                    high(e, q, j)
                    if j == 2 * PAIRS + 3:
                        turned(PAIRS - 1)
                if more:
                    high(e + 1, 1 - q, 0)
                    high(e + 1, 1 - q, 1)

            def start_second():
                act.wait_ge(over_done, 1)
                high(NE, 0, 0)
                high(NE, 0, 1)
                gathered(NE, 0)

            gathered(0, 0)
            sweeps(act, expert, start_second)

        @block.gpsimd
        def _(pool):
            pool.dma_start(bf_row[:, :], t["fox_b_f"].to_broadcast([P, FH])).then_inc(bf_loaded, 16)
            nc.gpsimd.memset(neg_half[:, :], -0.5).then_inc(gpsimd_step, 1)
            pool.wait_ge(gpsimd_step, 1)
            pool.wait_ge(acc_clear, 1)
            pool.dma_start(acc[0:1, :], t["mod_b"][0:1, :]).then_inc(acc_seeded, 16)
            for n, name in enumerate(ROOTS):
                w = ROOT_WIDTH.get(name, NT)
                pool.wait_ge(root_asked, n + 1)
                nc.gpsimd.tensor_tensor(root_out[:, n % 2, 0:w], root_in[:, n % 2, 0:w], neg_half[:, 0:w], ALU.pow
                                        ).then_inc(root_ready, 1)
                if name == "rms0_1":
                    pool.wait_ge(acc_clear, 2)
                    pool.dma_start(acc[0:1, :], t["mod_b"][1:2, :]).then_inc(acc_seeded, 16)

        @block.vector
        def _(dve):
            v = nc.vector
            steps = [0]

            def step(ins):
                steps[0] += 1
                ins.then_inc(vector_step, 1)
                dve.wait_ge(vector_step, steps[0])

            def bank(name, i):
                n = BANK_AT[name, i]
                dve.wait_ge(bank_filled, n + 1)
                return psum[:, n % NBANK, :]

            def pairs(b):
                return b.rearrange("p (j n) -> p j n", j=2)

            def wait_emptied(name, i):
                who, count = emptied_by(BANK_AT[name, i])
                dve.wait_ge(emptied[who], count)

            def low(dst, src, high):
                return v.tensor_tensor(dst, src, high.bitcast(F32), ALU.subtract)

            split = [0]

            def lows_until(n):
                for m in range(split[0], n + 1):
                    parts = used_units(m)
                    for half, narrow in parts:
                        dve.wait_ge(unit_high, 2 * m + half + 3 - len(parts))
                        src, dst = unit_parts(m, half)
                        if narrow:
                            src, dst = narrow(src), [narrow(d) for d in dst]
                        low(dst[1], src, dst[0]).then_inc(unit_ready, 3 - len(parts))
                split[0] = max(split[0], n + 1)

            def low_in(name, dst, n=4):
                for g in range(n):
                    dve.wait_ge(bank_high, high_count(BANK_AT[name, g]))
                    low(dst[1][:, 2 * g:2 * g + 2, :], pairs(bank(name, g)), dst[0][:, 2 * g:2 * g + 2, :]
                        ).then_inc(emptied["D"], 1)

            xr_parts = [xr[:, 0], xr[:, 1]]

            def ask_root(name, src, scale, eps):
                n = ROOTS.index(name)
                w = ROOT_WIDTH.get(name, NT)
                v.tensor_scalar(root_in[:, n % 2, 0:w], src, scale, eps, ALU.mult, ALU.add).then_inc(root_asked, 1)

            def root(name):
                n = ROOTS.index(name)
                dve.wait_ge(root_ready, n + 1)
                return root_out[:, n % 2, :]

            def angles():
                dve.wait_ge(pos_loaded, 16)
                dve.wait_ge(const_loaded, 16)
                step(v.tensor_copy(ang[:, 0, :], pos_i))
                step(v.tensor_scalar(ang[:, 1, :], ang[:, 0, :], const[:, C_INV:C_INV + 1], None, ALU.mult))
                magic = 12582912.0
                step(v.tensor_scalar(ang[:, 2, :], ang[:, 1, :], float(1 / (2 * np.pi)), magic, ALU.mult, ALU.add))
                step(v.tensor_scalar(ang[:, 2, :], ang[:, 2, :], magic, None, ALU.subtract))
                c1 = 6.28125
                c2 = float(np.round((2 * np.pi - c1) * 2 ** 19) / 2 ** 19)
                c3 = float(2 * np.pi - c1 - c2)
                for c in (c1, c2, c3):
                    step(v.scalar_tensor_tensor(ang[:, 1, :], ang[:, 2, :], -c, ang[:, 1, :], ALU.mult, ALU.add))
                top = 3.1415925
                step(v.tensor_scalar(ang[:, 4, :], ang[:, 1, :], float(np.pi / 2), None, ALU.add))
                step(v.tensor_scalar(ang[:, 5, :], ang[:, 4, :], float(np.pi), float(-2 * np.pi), ALU.is_gt, ALU.mult))
                step(v.tensor_tensor(ang[:, 5, :], ang[:, 5, :], ang[:, 4, :], ALU.add))
                step(v.tensor_scalar(ang[:, 4, :], ang[:, 5, :], top, -top, ALU.min, ALU.max))
                v.tensor_scalar(ang[:, 3, :], ang[:, 1, :], top, -top, ALU.min, ALU.max).then_inc(ang_ready, 1)

            v.memset(acc, 0.0).then_inc(acc_clear, 1)
            v.tensor_copy(vec[:, :, :].rearrange("p k n -> p (k n)"), bank("vecs", 0)[:, 0:KB * NVEC]
                          ).then_inc(emptied["D"], 1)

            def modulation_first(k):
                if k == 0:
                    dve.wait_ge(acc_seeded, 16)
                    dve.wait_ge(c_ready, 1)
                else:
                    dve.wait_ge(first_used, k)
                dve.wait_ge(first_filled[k % MOD_BUFS], 16 * (k // MOD_BUFS + 1))
                v.scalar_tensor_tensor(acc, mod_first[:, k % MOD_BUFS, :], c_act[:, k:k + 1], acc, ALU.mult, ALU.add
                                       ).then_inc(first_used, 1)

            def modulation(n):
                k, half = n // 2, n % 2
                if n == 0:
                    dve.wait_ge(acc_seeded, 32)
                dve.wait_ge(mod_filled[half], 16 * (n // 2 + 1))
                a = acc[:, half * 1536:(half + 1) * 1536]
                if n >= 2:
                    dve.wait_ge(mod_used, n - 1)
                v.scalar_tensor_tensor(a, mod_w[:, half, :], c_act[:, k:k + 1], a, ALU.mult, ALU.add
                                       ).then_inc(mod_used, 1)

            def rms(name, n, tt):
                dve.wait_ge(sumsq_ready, NT * n + tt + 1)
                ask_root(f"{name}_{tt}", sumsq[:, tt:tt + 1], 1.0, RMS_EPS)
                return root(f"{name}_{tt}")[:, 0:1]

            def normalise(name, n, dst):
                for tt in range(NT):
                    v.tensor_scalar(dst[:, tt, :], x[:, tt, :], rms(name, n, tt), None, ALU.mult).then_inc(xn_ready, 1)

            def input_affine(i):
                b = bank("mod_cols", i)
                v.scalar_tensor_tensor(in_scale[:, :], b[:, KB:2 * KB], 1.0, vec[:, :, V_NORM + i], ALU.add, ALU.mult)
                v.tensor_copy(in_shift[:, :], b[:, 0:KB]).then_inc(emptied["D"], 1)
                wait_emptied("mod_cols", i)

            def split_affine(i):
                for g in range(4):
                    wait_emptied(f"x{i}T", g)
                    a, high = affine_t[:, 2 * (g % 2):2 * (g % 2) + 2, :], xr[:, 0, 2 * g:2 * g + 2, :]
                    step(v.tensor_copy(high, a))
                    low(xr[:, 1, 2 * g:2 * g + 2, :], a, high).then_inc(affine_low, 1)

            def gate_row(i):
                for half in range(2):
                    v.tensor_copy(gate[:, half * 512:(half + 1) * 512], bank("mod_gate", 2 * i + half)
                                  ).then_inc(emptied["D"], 1)
                wait_emptied("mod_gate", 2 * i + 1)

            def gated_residual(name):
                for i in range(4):
                    xi = x[:, i // 2, (i % 2) * 512:(i % 2 + 1) * 512]
                    step(v.tensor_tensor(y_tmp[:, i % 2, :], bank(name, i), gate[:, (i % 2) * 512:(i % 2 + 1) * 512],
                                         ALU.mult))
                    v.tensor_tensor(xi, xi, y_tmp[:, i % 2, :], ALU.add).then_inc(emptied["D"], 1)

            wait_emptied("vecs", 0)
            normalise("rms0", 0, xn)
            angles()
            for k in range(KB):
                modulation_first(k)
            dve.wait_ge(wf_ready, 1)
            v.tensor_tensor(wf_r[:, :, FH:2 * FH], wf[:, :, :], wf_r[:, :, 0:FH].bitcast(F32), ALU.subtract
                            ).then_inc(wf_ready, 1)
            lows_until(0)
            input_affine(0)
            split_affine(0)
            lows_until(1)
            gate_row(0)
            v.memset(acc, 0.0).then_inc(acc_clear, 1)

            dve.wait_ge(trig_ready, 1)
            for name, dst in (("ret_q", rq), ("ret_k", rk)):
                for h in range(RH):
                    b = pairs(bank(name, h))
                    c2 = cos.unsqueeze(1).to_broadcast([P, 2, T])
                    s2 = sin.unsqueeze(1).to_broadcast([P, 2, T])
                    v.tensor_tensor(rot[:, 0], b, c2, ALU.mult)
                    step(v.tensor_tensor(rot[:, 1], b, s2, ALU.mult))
                    v.tensor_tensor(dst[:, 2 * h, :], rot[:, 0, 0, :], rot[:, 1, 1, :], ALU.subtract)
                    v.tensor_tensor(dst[:, 2 * h + 1, :], rot[:, 1, 0, :], rot[:, 0, 1, :], ALU.add
                                    ).then_inc(emptied["D"], 1)
                    wait_emptied(name, h)
                    if h % 2 == 1:
                        n = CHUNK_AT[name, h // 2]
                        lows_until(n + 2)
                        for m in mod_steps(n):
                            modulation(m)
            for c in range(4):
                n = CHUNK_AT["ret_v", c]
                lows_until(n + 2)
                for m in mod_steps(n):
                    modulation(m)
            def ret_decay(h):
                if h == 0:
                    dve.wait_ge(decay_loaded, 16)
                b = bank("ret_s", h)
                if h >= 2:
                    dve.wait_ge(bank_filled, BANK_AT["ret_o", 2 * (h - 2) + 1] + 1)
                v.tensor_tensor(dec_p[:, h % 2, 0:T], b[:, 0:T], decay[:, h, :], ALU.mult)
                v.tensor_tensor(dec_p[:, h % 2, T:3 * P], b[:, T:3 * P], decay[:, h, 0:P], ALU.mult
                                ).then_inc(emptied["D"], 1)

            lows_until(CHUNK_AT["ret_g", 1] + 2)
            input_affine(1)
            ret_decay(0)
            ret_decay(1)
            lows_until(CHUNK_AT["ret_g", 2] + 2)
            ret_decay(2)
            ret_decay(3)
            for h in range(RH):
                b = [bank("ret_o", 2 * h + tt) for tt in range(NT)]
                for tt in range(NT):
                    last = v.bn_stats(stats[:, tt, 0, :], b[tt])
                step(last)
                for tt in range(NT):
                    last = v.bn_aggr(meanvar[:, tt, :], stats[:, tt, 0, :])
                step(last)
                ask_root(f"ret{h}", meanvar[:, :, 1], 1.0, RMS_EPS)
                r = root(f"ret{h}")
                for tt in range(NT):
                    v.tensor_scalar(half_rows[:, tt, :], b[tt], meanvar[:, tt, 0:1], r[:, tt:tt + 1],
                                    ALU.subtract, ALU.mult).then_inc(emptied["D"], 1)
                wait_emptied("ret_o", 2 * h + 1)
                wait_emptied("ret_g", 2 * h + 1)
                for tt in range(NT):
                    g = rg[:, tt, h * RHV:(h + 1) * RHV]
                    v.tensor_tensor(g, g, half_rows[:, tt, :], ALU.mult).then_inc(ret_u_ready, 1)
                dve.wait_ge(ret_u_ready, 2 * (h + 1))
            low_in("ret_uT", ruT, 8)
            lows_until(CHUNK_AT["ret_g", 3] + 2)
            lows_until(CHUNK_AT["ret_out", 3] + 1)
            gated_residual("ret_y")

            gate_row(1)
            normalise("rms1", 1, xn1)
            split_affine(1)
            lows_until(CHUNK_AT["ret_out", 3] + 2)
            f = logf_t[:, 0, :]

            def forget_gates():
                dve.wait_ge(small_loaded, 6 * 16)
                dve.wait_ge(bf_loaded, 16)
                f3 = f.rearrange("p (t h) -> p t h", t=NT)
                b = bank("fox_f", 0)[:, 0:2 * NT * FH].rearrange("p (t j h) -> p t j h", t=NT, j=2)
                step(v.tensor_tensor(f3, b[:, :, 0, :], bf_row[:, :].unsqueeze(1).to_broadcast([P, NT, FH]), ALU.add))
                v.tensor_tensor(f3, f3, b[:, :, 1, :], ALU.add).then_inc(emptied["D"], 1)
                wait_emptied("fox_f", 0)
                v.scalar_tensor_tensor(logf_t[:, 1, :], f, -1.0, f, ALU.mult, ALU.min).then_inc(logf_in, 1)
                step(v.tensor_tensor(qk_gain[:, 0:1], gains[:, 0:1], gains[:, 1:2], ALU.mult))
                step(v.tensor_scalar(qk_gain[:, 0:1], qk_gain[:, 0:1], float(FD) ** -0.5, None, ALU.mult))
                step(v.tensor_copy(qk_gain[FD:P, 1:2], qk_gain[FD:P, 0:1]))
                v.memset(qk_gain[0:FD, 1:2], 0.0)
                step(v.memset(qk_gain[FD:P, 0:1], 0.0))

            def unit_heads(name, key, dst, s):
                for i in range(4):
                    n = 4 * s + i
                    if n == 2:
                        forget_gates()
                    b = bank(name, i)
                    tt, c = i % 2, i // 2
                    dve.wait_ge(fox_sq, n + 1)
                    v.tensor_reduce(head_sq[:, n % 2, :], fsq[:, n % 2, :].rearrange("p (h d) -> p h d", d=FD),
                                    AX.X, ALU.add).then_inc(fox_sq_used, 1)
                    dve.wait_ge(fox_sq_used, n + 1)
                    ask_root(f"{key}{i}", head_sq[:, n % 2, :], 1.0 / FD, RMS_EPS)
                    r = root(f"{key}{i}")[:, 0:8].unsqueeze(2).to_broadcast([P, 8, FD])
                    v.tensor_tensor(dst[:, tt, c * 512:(c + 1) * 512].rearrange("p (h d) -> p h d", d=FD),
                                    b.rearrange("p (h d) -> p h d", d=FD), r, ALU.mult).then_inc(emptied["D"], 1)
                    wait_emptied(name, i)
                    if i % 2 == 1:
                        lows_until(CHUNK_AT[name, c] + 2)

            unit_heads("fox_q", "fq", fq_tok, 0)
            dve.wait_ge(logf_mid, 1)
            v.scalar_tensor_tensor(logf[:, :, :].rearrange("p t h -> p (t h)"), f, 0.0, logf_t[:, 1, :],
                                   ALU.min, ALU.subtract).then_inc(logf_ready, 1)
            unit_heads("fox_k", "fk", fk_tok, 1)
            for key in (("fox_v", 0), ("fox_v", 1), ("fox_g", 0)):
                lows_until(CHUNK_AT[key] + 2)
            b = bank("fox_cum", 0)
            v.tensor_copy(cum[:, :, :].rearrange("p t h -> p (t h)"), b[:, 0:NT * FH])
            step(v.memset(ncumT, 0.0))
            v.tensor_scalar(ncumT[0:FH, :], b[0:FH, P:3 * P], -1.0, None, ALU.mult).then_inc(emptied["D"], 1)
            for g in range(4):
                v.tensor_copy(fkT[:, 2 * g:2 * g + 2, :], pairs(bank("fox_kT", g))).then_inc(emptied["D"], 1)

            wait_emptied("fox_kT", 3)
            for i in range(FH + 3):
                if i < FH:
                    b = bank("fox_s", i)
                    if i >= 2:
                        dve.wait_ge(probs_exp, i - 1)
                    j = i % 2
                    v.scalar_tensor_tensor(logits[:, j, 0:P], b[:, 0:P], cum[:, 0, i:i + 1],
                                           const[:, C_MASK + P:C_MASK + 2 * P], ALU.add, ALU.add)
                    v.scalar_tensor_tensor(logits[:, j, P:3 * P], b[:, P:3 * P], cum[:, 1, i:i + 1],
                                           const[:, C_MASK:C_MASK + 2 * P], ALU.add, ALU.add
                                           ).then_inc(emptied["D"], 1)
                    wait_emptied("fox_s", i)
                    v.tensor_reduce(mx[:, j, 0:1], logits[:, j, 0:P], AX.X, ALU.max, negate=True)
                    v.tensor_reduce(mx[:, j, 1:2], logits[:, j, P:3 * P], AX.X, ALU.max, negate=True
                                    ).then_inc(logits_ready, 1)
                if 1 <= i <= FH:
                    h, j = i - 1, (i - 1) % 2
                    dve.wait_ge(probs_exp, h + 1)
                    step(v.reciprocal(rinv[:, j, :], rsum[:, j, :]))
                    v.tensor_scalar(prob[:, j, 0:P], prob[:, j, 0:P], rinv[:, j, 0:1], None, ALU.mult)
                    v.tensor_scalar(prob[:, j, P:3 * P], prob[:, j, P:3 * P], rinv[:, j, 1:2], None, ALU.mult
                                    ).then_inc(probs_ready, 1)
                if i >= 4 and i % 2 == 0:
                    g = (i - 4) // 2
                    u = fgT[:, g, :]
                    step(v.tensor_tensor(u, bank("fox_o", g)[:, 0:T], u, ALU.mult))
                    step(v.tensor_copy(fuT[0][:, g, :], u))
                    low(fuT[1][:, g, :], u, fuT[0][:, g, :]).then_inc(emptied["D"], 1)
            lows_until(CHUNK_AT["fox_out", 1] + 1)
            gated_residual("fox_y")

            dve.wait_ge(final_loaded, 16)
            for tt in range(NT):
                v.scalar_tensor_tensor(x[:, tt, :], x[:, tt, :], rms("final", 2, tt), final_row, ALU.mult, ALU.mult
                                       ).then_inc(x_ready, 1)
            dve.wait_ge(x_ready, NT)
            low_in("x2T", xr_parts)
            lows_until(CHUNK_AT["fox_out", 1] + 2)

            step(v.memset(u_pad[:, :, 0:TAPS - 1], 0.0))
            v.tensor_scalar(vec[:, :, V_DW:V_DW + TAPS], vec[:, :, V_DW:V_DW + TAPS], 0.5, None, ALU.mult
                            ).then_inc(taps_halved, 1)
            dve.wait_ge(taps_halved, 1)
            chain = {}

            def tap(i, k):
                if i == CONV_BY_VECTOR - 1 and k < CONV_SHARED:
                    return
                if k == 0:
                    ins = v.tensor_scalar(conv[:, i, :], u_pad[:, i, 0:T], vec[:, i, V_DW:V_DW + 1],
                                          vec[:, i, V_CB:V_CB + 1], ALU.mult, ALU.add)
                else:
                    if i in chain:
                        dve.wait_ge(vector_step, chain[i])
                    else:
                        wait_emptied("conf_taps", i)
                    ins = v.scalar_tensor_tensor(conv[:, i, :], u_pad[:, i, k:k + T], vec[:, i, V_DW + k:V_DW + k + 1],
                                                 conv[:, i, :], ALU.mult, ALU.add)
                if k == TAPS - 1:
                    ins.then_inc(conv_ready, 1)
                else:
                    ins.then_inc(vector_step, 1)
                    steps[0] += 1
                    chain[i] = steps[0]

            early = TAPS // 2
            for c in range(2):
                lows_until(CHUNK_AT["conf_g", c] + 2)
                for g in range(2 * c, 2 * c + 2):
                    wait_emptied("conf_g", g)
                    v.scalar_tensor_tensor(u_pad[:, 2 * g:2 * g + 2, TAPS - 1:], half_gate[:, c, 2 * (g % 2):2 * (g % 2) + 2, :],
                                           1.0, pairs(bank("conf_a", g)), ALU.add, ALU.mult).then_inc(emptied["D"], 1)
                wait_emptied("conf_a", 2 * c + 1)
                lows_until(CHUNK_AT["conf_a", c] + 2)
                if c == 0:
                    for k in range(early):
                        tap(0, k)
                        tap(1, k)
            for k in range(early, TAPS):
                tap(0, k)
                tap(1, k)
            for k in range(TAPS):
                for i in range(2, CONV_BY_VECTOR):
                    tap(i, k)
            for tt in range(NT):
                for half in range(2):
                    last = v.bn_stats(stats[:, tt, half, :], bank("conf_cT", 2 * tt + half))
            step(last)
            for tt in range(NT):
                last = v.bn_aggr(meanvar[:, tt, :], stats[:, tt, :, :].rearrange("p a b -> p (a b)"))
            step(last)
            ask_root("conf", meanvar[:, :, 1], 1.0, LN_EPS)
            r = root("conf")
            for tt in range(NT):
                for half in range(2):
                    v.tensor_scalar(conf_n[:, tt, half * 512:(half + 1) * 512], bank("conf_cT", 2 * tt + half),
                                    meanvar[:, tt, 0:1], r[:, tt:tt + 1], ALU.subtract, ALU.mult
                                    ).then_inc(emptied["D"], 1)
            for g in range(4):
                wait_emptied("conf_nT", g)
                step(v.tensor_copy(conf_uT[0][:, 2 * g:2 * g + 2, :], pairs(conf_t[:, g % 2, :])))
                low(conf_uT[1][:, 2 * g:2 * g + 2, :], pairs(conf_t[:, g % 2, :]), conf_uT[0][:, 2 * g:2 * g + 2, :]
                    ).then_inc(conf_low, 1)
            lows_until(CHUNK_AT["conf_out", 1] + 1)

            def layer_norm(name, n, y, z, g_row=rows_gb[:, 0, :], b_row=rows_gb[:, 1, :]):
                for tt in range(NT):
                    for half in range(2):
                        hs = slice(half * 512, (half + 1) * 512)
                        if y is not None:
                            src, count = y(tt, half)
                            v.scalar_tensor_tensor(z[:, tt, hs], x[:, tt, hs], ALPHA, src, ALU.mult, ALU.add
                                                   ).then_inc(emptied["D"], 1)
                            dve.wait_ge(emptied["D"], count)
                        last = v.bn_stats(stats[:, tt, half, :], z[:, tt, hs])
                    step(last)
                    step(v.bn_aggr(meanvar[:, tt, :], stats[:, tt, :, :].rearrange("p a b -> p (a b)")))
                    ask_root(f"{name}_{tt}", meanvar[:, tt, 1:2], 1.0, LN_EPS)
                    if tt == 0:
                        dve.wait_ge(rows_loaded, 32 * n)
                    step(v.scalar_tensor_tensor(z[:, tt, :], z[:, tt, :], meanvar[:, tt, 0:1], g_row, ALU.subtract, ALU.mult))
                    r = root(f"{name}_{tt}")
                    v.scalar_tensor_tensor(x[:, tt, :], z[:, tt, :], r[:, 0:1], b_row, ALU.mult, ALU.add).then_inc(x_ready, 1)
                dve.wait_ge(x_ready, NT * (n + 1))

            def from_banks(name):
                def y(tt, half):
                    i = 2 * tt + half
                    return bank(name, i), emptied_by(BANK_AT[name, i])[1]
                return y

            layer_norm("mix0", 1, from_banks("conf_y"), region(8448, NT, D))
            low_in("x3T", xr_parts)
            lows_until(CHUNK_AT["conf_out", 1] + 2)

            for c in range(6):
                lows_until(CHUNK_AT["ffn_gate", c] + 2)
                for i in range(2 * c, min(2 * c + 2, FB // 2)):
                    h = ffn_t[:, i % 2, :]
                    wait_emptied("ffn_gate", i)
                    v.tensor_tensor(pairs(h), ffn_s[:, c % 2, 2 * (i % 2):2 * (i % 2) + 2, :], pairs(bank("ffn_up", i)),
                                    ALU.mult).then_inc(emptied["D"], 1)
                    wait_emptied("ffn_up", i)
                    step(v.tensor_copy(ffn_h[0][:, 2 * i:2 * i + 2, :], pairs(h)))
                    low(ffn_h[1][:, 2 * i:2 * i + 2, :], pairs(h), ffn_h[0][:, 2 * i:2 * i + 2, :]).then_inc(ffn_low, 1)
                lows_until(CHUNK_AT["ffn_up", c] + 2)
            lows_until(CHUNK_AT["ffn_down", 5] + 1)
            layer_norm("ffn0", 2, from_banks("ffn_y"), region(0, NT, D))
            low_in("x4T", xr_parts)
            lows_until(CHUNK_AT["ffn_down", 5] + 2)

            step(v.memset(ch[:, :, 0:STAPS - 1], 0.0))
            for c in range(2):
                lows_until(CHUNK_AT["sc_c", c] + 2)
                for g in range(2 * c, 2 * c + 2):
                    wait_emptied("sc_c", g)
                    v.tensor_tensor(ch[:, 2 * g:2 * g + 2, STAPS - 1:], sc_c[:, c, 2 * (g % 2):2 * (g % 2) + 2, :],
                                    pairs(bank("sc_h", g)), ALU.mult).then_inc(emptied["D"], 1)
                wait_emptied("sc_h", 2 * c + 1)
                lows_until(CHUNK_AT["sc_h", c] + 2)
                for i in range(4):
                    k8 = 4 * c + i
                    step(v.tensor_scalar(sc_t[:, i, :], ch[:, k8, 0:T], vec[:, k8, V_SC:V_SC + 1], None, ALU.mult))
                    for k in range(1, STAPS):
                        step(v.scalar_tensor_tensor(sc_t[:, i, :], ch[:, k8, k:k + T], vec[:, k8, V_SC + k:V_SC + k + 1],
                                                    sc_t[:, i, :], ALU.mult, ALU.add))
                for g in range(2 * c, 2 * c + 2):
                    u = sc_t[:, 2 * (g % 2):2 * (g % 2) + 2, :]
                    v.tensor_tensor(u, u, pairs(bank("sc_b", g)), ALU.mult).then_inc(emptied["D"], 1)
                    wait_emptied("sc_b", g)
                    step(v.tensor_copy(sc_uT[0][:, 2 * g:2 * g + 2, :], u))
                    low(sc_uT[1][:, 2 * g:2 * g + 2, :], u, sc_uT[0][:, 2 * g:2 * g + 2, :]).then_inc(sc_low, 1)
                dve.wait_ge(sc_low, 2 * c + 2)
                lows_until(CHUNK_AT["sc_b", c] + 2)
            lows_until(CHUNK_AT["sc_out", 1] + 1)
            layer_norm("mix1", 3, from_banks("sc_y"), region(8448, NT, D))

            LG, M, E, C, OH1, LG2, OH2, G1, G2, CH, DIF, EX = range(12)
            row8 = desc.unsqueeze(1).to_broadcast([P, NT, NE])

            def wide(i):
                return rt[:, i, :, 0:1].to_broadcast([P, NT, NE])

            lows_until(CHUNK_AT["sc_out", 1] + 2)
            step(v.memset(rt[:, :, :, :], 0.0))
            v.tensor_copy(rt[:, LG].rearrange("p t e -> p (t e)"), bank("route", 0)[:, 0:NT * NE]
                          ).then_inc(emptied["D"], 1)
            wait_emptied("route", 0)
            for src, top, hot in ((LG, M, OH1), (LG2, E, OH2)):
                if src == LG2:
                    step(v.scalar_tensor_tensor(rt[:, LG2], rt[:, OH1], -3e38, rt[:, LG], ALU.mult, ALU.add))
                step(v.tensor_reduce(rt[:, top, :, 0], rt[:, src], AX.X, ALU.max))
                step(v.tensor_tensor(rt[:, C], rt[:, src], wide(top), ALU.is_equal))
                step(v.tensor_tensor(rt[:, C], rt[:, C], row8, ALU.mult))
                step(v.tensor_reduce(rt[:, 12, :, 0], rt[:, C], AX.X, ALU.max))
                step(v.tensor_tensor(rt[:, hot], row8, wide(12), ALU.is_equal))
            v.tensor_tensor(rt[:, CH], rt[:, OH1], rt[:, OH2], ALU.add).then_inc(mask_ready, 1)
            v.tensor_tensor(rt[:, DIF, :, 0], rt[:, E, :, 0], rt[:, M, :, 0], ALU.subtract).then_inc(lg_ready, 1)
            dve.wait_ge(lg_exp, 1)
            step(v.tensor_scalar(rt[:, 13, :, 0], rt[:, EX, :, 0], 1.0, None, ALU.add))
            step(v.reciprocal(rt[:, G1, :, 0], rt[:, 13, :, 0]))
            step(v.tensor_tensor(rt[:, G2, :, 0], rt[:, G1, :, 0], rt[:, EX, :, 0], ALU.mult))
            step(v.tensor_tensor(rt[:, C], rt[:, OH1], wide(G1), ALU.mult))
            step(v.tensor_tensor(rt[:, LG2], rt[:, OH2], wide(G2), ALU.mult))
            step(v.tensor_tensor(gate_of[:, :, :].rearrange("p e t -> p t e"), rt[:, C], rt[:, LG2], ALU.add))
            b = bank("rank", 0)
            step(v.tensor_tensor(rt[:, C], b[:, 0:NT * NE].rearrange("p (t e) -> p t e", t=NT), rt[:, CH], ALU.mult))
            step(v.memset(slot_of[:, :, :], -1.0))
            v.tensor_scalar(slot_of[:, 0:NE, :].rearrange("p e t -> p t e"), rt[:, C], -1.0, None, ALU.add
                            ).then_inc(scatter_emptied, 1)
            for q in range(2):
                v.tensor_scalar(e_acc[:, q, 0:512], x[:, q, 0:512], ALPHA, None, ALU.mult).then_inc(gate_emptied, 1)
                v.tensor_scalar(e_acc[:, q, 512:1024], x[:, q, 512:1024], ALPHA, None, ALU.mult).then_inc(up_emptied, 1)
            for q in range(2):
                step(v.tensor_reduce(big[:, q:q + 1], b[0:1, 2 * NE:3 * NE], AX.X, ALU.max))
                ins = v.tensor_scalar(over[:, :], big[:, q:q + 1], float(P), None, ALU.is_gt)
                ins.then_inc(turn_emptied, 1)
            dve.wait_ge(turn_emptied, 2)
            v.tensor_copy(big[:, 0:1], b[0:1, 0:1]).then_inc(emptied["D"], 1)
            dve.wait_ge(emptied["D"], ALL_EMPTIED["D"])
            dve.wait_ge(scatter_emptied, 1)
            dve.wait_ge(up_emptied, 2)
            dve.wait_ge(gate_emptied, 2)

            def low_unit(e, q, j):
                for half in range(2):
                    dve.wait_ge(unit_high, e * (2 * PER_EXPERT) + 2 * (PRE + j) + half + 1)
                    dst, src = expert_unit_parts(q, j, half, 1)
                    low(dst, src, expert_unit_parts(q, j, half, 0)[0]).then_inc(unit_ready, 1)

            def select(of, q):
                for tt in range(NT):
                    last = v.tensor_scalar(e_sel[q][:, tt, :], const[:, C_IOTA:C_IOTA + P],
                                           slot_of[:, bass.ds(of, 1), tt], None, ALU.is_equal)
                last.then_inc(sel_ready, 1)

            def gathered(e, q):
                dve.wait_ge(gather_high, e + 1)
                low(e_x[q][1].rearrange("p k t -> p (k t)"), psum[:, 0:2, :].rearrange("p b n -> p (b n)"),
                    e_x[q][0].rearrange("p k t -> p (k t)")).then_inc(gather_emptied, 1)

            def expert(e, q, more, number):
                of = e - number * NE

                def turned(c):
                    i = c if c < PAIRS - 1 else PAIRS
                    dve.wait_ge(turn_high, e * PAIRS + c + 1)
                    low(e_h[1][:, 4 * c:4 * c + 4, :], psum[:, 2 + i % 2, :].rearrange("p (j n) -> p j n", j=4),
                        e_h[0][:, 4 * c:4 * c + 4, :]).then_inc(turn_emptied, 1)

                for c in range(PAIRS):
                    if more and 2 * c - 1 == GATHER_AFTER:
                        gathered(e + 1, 1 - q)
                    low_unit(e, q, 2 * c + 2)
                    dve.wait_ge(gate_emptied, e * PAIRS + c + 3)
                    dve.wait_ge(gu_filled, e * (2 * PAIRS) + 2 * c + 2)
                    v.tensor_tensor(e_ht[:, (q * PAIRS + c) % 2, :], e_s[:, (q * PAIRS + c) % 2, :],
                                    psum[:, 4 + (q * 2 * PAIRS + 2 * c + 1) % 4, :], ALU.mult).then_inc(up_emptied, 1)
                    low_unit(e, q, 2 * c + 3)
                    if c >= 1:
                        turned(c - 1)
                    if c == 1 and more:
                        select(of + 1, 1 - q)
                for j in range(2 * PAIRS + 2, PER_EXPERT):
                    low_unit(e, q, j)
                    if j == 2 * PAIRS + 3:
                        dve.wait_ge(turn_filled, e * 8 + PAIRS)
                        v.tensor_copy(e_selT, psum[:, 2 + (PAIRS - 1) % 2, 0:NT * P]).then_inc(turn_emptied, 1)
                        turned(PAIRS - 1)
                if more:
                    low_unit(e + 1, 1 - q, 0)
                dve.wait_ge(down_filled, e + 1)
                v.tensor_copy(e_y, psum[:, 0:2, :].rearrange("p b n -> p (b n)")).then_inc(down_emptied, 1)
                if more:
                    low_unit(e + 1, 1 - q, 1)
                dve.wait_ge(scatter_filled, e + 1)
                dve.wait_ge(scatter_emptied, e + 1)
                for tt in range(NT):
                    last = v.scalar_tensor_tensor(e_acc[:, tt, :],
                                                  psum[:, 2 * tt:2 * tt + 2, :].rearrange("p b n -> p (b n)"),
                                                  gate_of[:, bass.ds(of, 1), tt], e_acc[:, tt, :], ALU.mult, ALU.add)
                last.then_inc(scatter_emptied, 1)
                if not more:
                    dve.wait_ge(scatter_emptied, e + 2)

            def start_second():
                v.tensor_scalar(slot_of[:, :, :], slot_of[:, :, :], float(P), None, ALU.subtract).then_inc(over_done, 1)
                dve.wait_ge(over_done, 1)
                select(0, 0)
                low_unit(NE, 0, 0)
                low_unit(NE, 0, 1)
                gathered(NE, 0)

            select(0, 0)
            gathered(0, 0)
            sweeps(dve, expert, start_second)
            layer_norm("out", 4, None, e_acc, out_g, out_b)
    return nc


_INS = ['x', 'c', 'positions', 'mod_w', 'mod_b', 'norm_g', 'ret_w_in', 'ret_w_out', 'fox_w_in', 'fox_b_f',
        'fox_q_gain', 'fox_k_gain', 'fox_w_out', 'final_g', 'ln_mix_g_2', 'ln_mix_b_2', 'ln_ffn_g_2',
        'ln_ffn_b_2', 'conf_w_in_2', 'conf_w_dw_2', 'conf_b_dw_2', 'conf_ln_g_2', 'conf_ln_b_2', 'conf_w_out_2',
        'sc_w_in_2', 'sc_w_conv_2', 'sc_w_out_2', 'ffn_w_gate_2', 'ffn_w_up_2', 'ffn_w_down_2',
        'moe_w_router_2', 'moe_w_gate_2', 'moe_w_up_2', 'moe_w_down_2']


def kernel(**inputs):
    import concourse.bacc as bacc
    from concourse.bass_utils import run_bass_kernel_spmd

    nc = bacc.Bacc("TRN2", target_bir_lowering=False, num_devices=1)
    arrays, views = {}, {}
    const, decay = shape_constants()
    given = {name: np.ascontiguousarray(inputs[name]) for name in _INS}
    given["final_g"] = given["final_g"].reshape(1, D)
    given["const"], given["decay"] = const, decay
    for name, a in given.items():
        arrays[f"in_{name}"] = a
        views[name] = nc.dram_tensor(f"in_{name}", a.shape, mybir.dt.from_np(a.dtype), kind="ExternalInput").ap()
    out = nc.dram_tensor("out", (1, T, D), F32, kind="ExternalOutput").ap()
    build(nc, views, out)
    r = run_bass_kernel_spmd(nc, [arrays], core_ids=[0])
    return r.results[0]["out"]
```
